# Optimizing a Trainium2 kernel written in Bass

```python
import jax, jax.numpy as jnp
from jax import lax
import numpy as np

D_MODEL = 1024
BATCH = 1
SEQ = 1024
DEPTH = 2

GRID_W = 64
CTX_LEN = 256
EXPAND = 2
D_INNER = EXPAND * D_MODEL
M_HEADS = 4
M_HEAD_DIM = D_INNER // M_HEADS
CHUNK = 64
N_CONV_LAYERS = (DEPTH + 1) // 2
N_MLSTM_LAYERS = DEPTH // 2
EPS = 1e-6

kernel_name = "hybrid_shortconv_mlstm_dit"

def _rmsnorm(x, g):
    xf = x.astype(jnp.float32)
    y = xf * lax.rsqrt(jnp.mean(xf * xf, axis=-1, keepdims=True) + EPS)
    return (y * g.astype(jnp.float32)).astype(x.dtype)

def _modulate(x, g, shift, scale):
    return _rmsnorm(x, g) * (1 + scale) + shift

def _dwconv3(u, w):
    pad = [(0, 0)] * (u.ndim - 2) + [(1, 1), (0, 0)]
    p = jnp.pad(u, pad)
    return p[..., :-2, :] * w[0] + p[..., 1:-1, :] * w[1] + p[..., 2:, :] * w[2]

def _grid_conv3(u, w):
    b, s, ch = u.shape
    rows = s // GRID_W
    return _dwconv3(u.reshape(b, rows, GRID_W, ch), w).reshape(b, s, ch)

def _shortconv_mixer(h, w_in, w_conv, w_out, conv_fn):
    b_gate, c_gate, u, z = jnp.split(h @ w_in, 4, axis=-1)
    y = b_gate * conv_fn(c_gate * u, w_conv)
    return (y * jax.nn.silu(z)) @ w_out

def _zero_state(b):
    return (jnp.zeros((b, M_HEADS, M_HEAD_DIM, M_HEAD_DIM), jnp.float32),
            jnp.zeros((b, M_HEADS, M_HEAD_DIM), jnp.float32),
            jnp.zeros((b, M_HEADS), jnp.float32))

def _mlstm_scan(q, k, v, ig, lf, state):
    b, nh, t, dh = q.shape
    nc = t // CHUNK

    def to_chunks(a):
        return jnp.moveaxis(a.reshape(b, nh, nc, CHUNK, *a.shape[3:]), 2, 0)

    mask = jnp.tril(jnp.ones((CHUNK, CHUNK), bool))

    def step(carry, xs):
        c_prev, n_prev, m_prev = carry
        qc, kc, vc, ic, fc = xs
        bcum = jnp.cumsum(fc, axis=-1)
        dmat = bcum[..., :, None] - bcum[..., None, :] + ic[..., None, :]
        dmat = jnp.where(mask, dmat, -jnp.inf)
        m_inter = bcum + m_prev[..., None]
        m_j = jnp.maximum(m_inter, dmat.max(-1))
        s = jnp.einsum('bhjd,bhsd->bhjs', qc, kc) * jnp.exp(dmat - m_j[..., None])
        w_inter = jnp.exp(m_inter - m_j)
        num = w_inter[..., None] * jnp.einsum('bhjd,bhde->bhje', qc, c_prev) + jnp.einsum('bhjs,bhse->bhje', s, vc)
        den = w_inter * jnp.einsum('bhjd,bhd->bhj', qc, n_prev) + s.sum(-1)
        h = num / jnp.maximum(jnp.abs(den), jnp.exp(-m_j))[..., None]
        b_last = bcum[..., -1]
        g = b_last[..., None] - bcum + ic
        m_new = jnp.maximum(b_last + m_prev, g.max(-1))
        w_decay = jnp.exp(b_last + m_prev - m_new)
        w_s = jnp.exp(g - m_new[..., None])
        c_new = w_decay[..., None, None] * c_prev + jnp.einsum('bhs,bhsd,bhse->bhde', w_s, kc, vc)
        n_new = w_decay[..., None] * n_prev + jnp.einsum('bhs,bhsd->bhd', w_s, kc)
        return (c_new, n_new, m_new), h

    state, hs = lax.scan(step, state, (to_chunks(q), to_chunks(k), to_chunks(v), to_chunks(ig), to_chunks(lf)))
    h = jnp.moveaxis(hs, 0, 2).reshape(b, nh, t, dh)
    return h, state

def _mlstm_final_state(k, v, ig, lf):
    bcum = jnp.cumsum(lf, axis=-1)
    b_last = bcum[..., -1]
    g = b_last[..., None] - bcum + ig
    m = jnp.maximum(b_last, g.max(-1))
    w = jnp.exp(g - m[..., None])
    return (jnp.einsum('bht,bhtd,bhte->bhde', w, k, v), jnp.einsum('bht,bhtd->bhd', w, k), m)

def _flip_t(a):
    return jnp.flip(a, axis=2)

def _mlstm_inputs(u, w_conv, wq, wk, wv, w_gate, b_gate, conv_fn):
    b, t, _ = u.shape
    u_c = jax.nn.silu(conv_fn(u, w_conv))
    uc_h = u_c.reshape(b, t, M_HEADS, M_HEAD_DIM)
    u_h = u.reshape(b, t, M_HEADS, M_HEAD_DIM)
    q = jnp.einsum('bthd,hde->bthe', uc_h, wq)
    k = jnp.einsum('bthd,hde->bthe', uc_h, wk) * (M_HEAD_DIM ** -0.5)
    v = jnp.einsum('bthd,hde->bthe', u_h, wv)
    gin = jnp.concatenate([q.reshape(b, t, D_INNER), k.reshape(b, t, D_INNER), v.reshape(b, t, D_INNER)], axis=-1)
    gates = (gin @ w_gate + b_gate).astype(jnp.float32).reshape(b, t, 4, M_HEADS)
    gates = jnp.transpose(gates, (2, 0, 3, 1))
    to_bhtd = lambda a: jnp.transpose(a, (0, 2, 1, 3)).astype(jnp.float32)
    return to_bhtd(q), to_bhtd(k), to_bhtd(v), gates, u_c

def _mlstm_mixer(h, w_in, w_conv, wq, wk, wv, w_gate, b_gate, norm_g, skip, w_out, conv_fn, st_f, st_b):
    b, t, _ = h.shape
    u, z, o_pre = jnp.split(h @ w_in, 3, axis=-1)
    q, k, v, g, u_c = _mlstm_inputs(u, w_conv, wq, wk, wv, w_gate, b_gate, conv_fn)
    h_f, st_f = _mlstm_scan(q, k, v, g[0], jax.nn.log_sigmoid(g[1]), st_f)
    h_b, st_b = _mlstm_scan(_flip_t(q), _flip_t(k), _flip_t(v), _flip_t(g[2]),
                            jax.nn.log_sigmoid(_flip_t(g[3])), st_b)
    h_sum = h_f + _flip_t(h_b)
    mu = jnp.mean(h_sum, axis=-1, keepdims=True)
    var = jnp.mean(jnp.square(h_sum - mu), axis=-1, keepdims=True)
    hn = (h_sum - mu) * lax.rsqrt(var + EPS)
    hn = jnp.transpose(hn, (0, 2, 1, 3)).reshape(b, t, D_INNER).astype(h.dtype) * norm_g
    y = jax.nn.sigmoid(o_pre) * hn
    y = (y + skip * u_c) * jax.nn.silu(z)
    return y @ w_out, st_f, st_b

def _mlstm_context_states(h, w_in, w_conv, wq, wk, wv, w_gate, b_gate):
    u = h @ w_in[:, :D_INNER]
    q, k, v, g, _ = _mlstm_inputs(u, w_conv, wq, wk, wv, w_gate, b_gate, _dwconv3)
    st_f = _mlstm_final_state(k, v, g[0], jax.nn.log_sigmoid(g[1]))
    st_b = _mlstm_final_state(_flip_t(k), _flip_t(v), _flip_t(g[2]), jax.nn.log_sigmoid(_flip_t(g[3])))
    return st_f, st_b

def setup_inputs(seed: int = 0) -> dict:
    key = jax.random.key(seed)
    ks = jax.random.split(key, 32)
    f32 = jnp.float32
    nrm = lambda k, shape, scale: jax.random.normal(k, shape, f32) * scale
    nc, nm, h = N_CONV_LAYERS, N_MLSTM_LAYERS, M_HEADS
    f_bias = jnp.linspace(3.0, 6.0, h, dtype=f32)
    b_gate = jnp.concatenate([nrm(ks[20], (nm, h), 0.1), f_bias + nrm(ks[21], (nm, h), 0.1),
                              nrm(ks[22], (nm, h), 0.1), f_bias + nrm(ks[23], (nm, h), 0.1)], axis=-1)
    return {
        "x": nrm(ks[0], (BATCH, SEQ, D_MODEL), 1.0),
        "c": nrm(ks[1], (BATCH, D_MODEL), 1.0),
        "ctx": nrm(ks[2], (BATCH, CTX_LEN, D_MODEL), 1.0),
        "c_ctx": nrm(ks[3], (D_MODEL,), 1.0),
        "norm_g": 1.0 + nrm(ks[4], (DEPTH, D_MODEL), 0.05),
        "mod_w": nrm(ks[5], (DEPTH, D_MODEL, 3 * D_MODEL), 0.5 * D_MODEL ** -0.5),
        "mod_b": nrm(ks[6], (DEPTH, 3 * D_MODEL), 0.02),
        "conv_w_in": nrm(ks[7], (nc, D_MODEL, 4 * D_INNER), D_MODEL ** -0.5),
        "conv_w": nrm(ks[8], (nc, 3, D_INNER), 3 ** -0.5),
        "conv_w_out": nrm(ks[9], (nc, D_INNER, D_MODEL), D_INNER ** -0.5),
        "m_w_in": nrm(ks[10], (nm, D_MODEL, 3 * D_INNER), D_MODEL ** -0.5),
        "m_conv_w": nrm(ks[11], (nm, 3, D_INNER), 3 ** -0.5),
        "m_wq": nrm(ks[12], (nm, h, M_HEAD_DIM, M_HEAD_DIM), M_HEAD_DIM ** -0.5),
        "m_wk": nrm(ks[13], (nm, h, M_HEAD_DIM, M_HEAD_DIM), M_HEAD_DIM ** -0.5),
        "m_wv": nrm(ks[14], (nm, h, M_HEAD_DIM, M_HEAD_DIM), M_HEAD_DIM ** -0.5),
        "m_w_gate": nrm(ks[15], (nm, 3 * D_INNER, 4 * h), 0.3 * (3 * D_INNER) ** -0.5),
        "m_b_gate": b_gate,
        "m_norm_g": 1.0 + nrm(ks[16], (nm, D_INNER), 0.05),
        "m_skip": 1.0 + nrm(ks[17], (nm, D_INNER), 0.1),
        "m_w_out": nrm(ks[18], (nm, D_INNER, D_MODEL), D_INNER ** -0.5),
        "final_g": 1.0 + nrm(ks[19], (D_MODEL,), 0.05),
    }

def reference(x, c, ctx, c_ctx, norm_g, mod_w, mod_b, conv_w_in, conv_w, conv_w_out,
              m_w_in, m_conv_w, m_wq, m_wk, m_wv, m_w_gate, m_b_gate, m_norm_g, m_skip, m_w_out, final_g):
    b = x.shape[0]
    sc = jax.nn.silu(c)
    scc = jax.nn.silu(c_ctx)
    for i in range(DEPTH):
        last = i == DEPTH - 1
        j = i // 2
        shift, scale, gate = jnp.split(sc @ mod_w[i] + mod_b[i], 3, axis=-1)
        hx = _modulate(x, norm_g[i], shift[:, None], scale[:, None])
        if i % 2 == 0:
            x = x + gate[:, None] * _shortconv_mixer(hx, conv_w_in[j], conv_w[j], conv_w_out[j], _grid_conv3)
            if not last:
                shift_c, scale_c, gate_c = jnp.split(scc @ mod_w[i] + mod_b[i], 3, axis=-1)
                hc = _modulate(ctx, norm_g[i], shift_c, scale_c)
                ctx = ctx + gate_c * _shortconv_mixer(hc, conv_w_in[j], conv_w[j], conv_w_out[j], _dwconv3)
        else:
            shift_c, scale_c, gate_c = jnp.split(scc @ mod_w[i] + mod_b[i], 3, axis=-1)
            hc = _modulate(ctx, norm_g[i], shift_c, scale_c)
            if last:
                st_f, st_b = _mlstm_context_states(hc, m_w_in[j], m_conv_w[j], m_wq[j], m_wk[j], m_wv[j],
                                                   m_w_gate[j], m_b_gate[j])
            else:
                yc, st_f, st_b = _mlstm_mixer(hc, m_w_in[j], m_conv_w[j], m_wq[j], m_wk[j], m_wv[j],
                                              m_w_gate[j], m_b_gate[j], m_norm_g[j], m_skip[j], m_w_out[j],
                                              _dwconv3, _zero_state(b), _zero_state(b))
                ctx = ctx + gate_c * yc
            yx, _, _ = _mlstm_mixer(hx, m_w_in[j], m_conv_w[j], m_wq[j], m_wk[j], m_wv[j],
                                    m_w_gate[j], m_b_gate[j], m_norm_g[j], m_skip[j], m_w_out[j],
                                    _grid_conv3, st_f, st_b)
            x = x + gate[:, None] * yx
    return _rmsnorm(x, final_g)


_drawn_inputs = setup_inputs


def setup_inputs(seed=0):
    import zlib

    import numpy as np

    out = dict(_drawn_inputs(seed))
    spreads = {}
    factors = {'ctx': 3.106, 'm_w_gate': 3.678, 'm_norm_g': 8.0, 'm_skip': 4.19}
    for name, (base, spread) in spreads.items():
        noise = np.random.default_rng([zlib.crc32(name.encode()), seed]).standard_normal(out[name].shape)
        drawn = base * np.exp(spread * noise) if base else spread * noise
        out[name] = __import__('jax').numpy.asarray(drawn.astype(out[name].dtype))
    for name, factor in factors.items():
        out[name] = (out[name] * factor).astype(out[name].dtype)
    return out
```

```python
import concourse.bass as bass
from concourse import mybir
from contextlib import ExitStack

D = 1024
DI = 2048
TX = 1024
TC = 256
TT = TX + TC
HEADS = 4
DH = DI // HEADS
ROW = 64
EPS = 1e-6
P = 128
KD = D // P
KI = DI // P
KH = DH // P
NT = TT // P
NTX = TX // P
BANK = 512
GROUPS = [(0, 512), (512, 512), (1024, 256)]

F32 = mybir.dt.float32
F32R = mybir.dt.float32r
ALU = mybir.AluOpType
ACT = mybir.ActivationFunctionType

COL_CONV, COL_MCONV, COL_NORM, COL_SKIP, COL_G, COL_C = 0, 48, 96, 112, 128, 144


def over(eng, n, step, last_differs=True):
    step(0, True, False)
    end = n - 1 if last_differs else n
    with eng.Fori(1, end) as i:
        step(i, False, False)
    if last_differs:
        step(n - 1, False, True)


def mm3(nc, out, w_hi, w_lo, x_hi, x_lo, first, last):
    nc.tensor.matmul(out, w_lo, x_hi, start=first, stop=False)
    nc.tensor.matmul(out, w_hi, x_lo, start=False, stop=False)
    return nc.tensor.matmul(out, w_hi, x_hi, start=False, stop=last)


def build(nc, io):
    es = ExitStack()
    with es:
        held = []

        def sem(name):
            held.append(nc.alloc_semaphore(name=name))
            return held[-1]

        def end_phase():
            nc.clear_and_free_semaphores(held)
            held.clear()
            nc.all_engine_barrier()

        def dram(name, shape):
            return nc.dram_tensor(name, shape, F32, kind="Internal").ap()

        keep = {
            "ps": es.enter_context(nc.psum_tensor("ps", [P, 8, BANK], F32)),
            "ident": es.enter_context(nc.sbuf_tensor("ident", [P, P], F32)),
            "par": es.enter_context(nc.sbuf_tensor("par", [P, 160], F32)),
            "mod": es.enter_context(nc.sbuf_tensor("mod", [P, 2, 2, 2, KD], F32)),
        }
        scr = {
            "gates": dram("gate_rows", (2, 2, D)),
            "yT": dram("yT", (DI, TT)),
            "x1": dram("x1", (TT, D)),
            "uT": dram("uT", (DI, TT)),
            "ucT": dram("ucT", (DI, TT)),
            "qkvT": dram("qkvT", (3, DI, TT)),
            "ymul": dram("ymul", (DI, TX)),
            "yadd": dram("yadd", (DI, TX)),
            "nmrow": dram("nmrow", (2, HEADS, TX)),
        }
        modulation(nc, sem, keep, scr, io)
        end_phase()
        for layer in range(2):
            with ExitStack() as hold:
                h_hi = hold.enter_context(nc.sbuf_tensor(f"h{layer}_hi", [P, KD, TT], F32R))
                h_lo = hold.enter_context(nc.sbuf_tensor(f"h{layer}_lo", [P, KD, TT], F32R))
                norm_phase(nc, sem, keep, scr, io, layer, h_hi, h_lo)
                end_phase()
                if layer == 0:
                    conv_in_phase(nc, sem, keep, scr, io, h_hi, h_lo)
                else:
                    lstm_in_phase(nc, sem, keep, scr, io, h_hi, h_lo)
                end_phase()
            if layer == 1:
                with ExitStack() as hold:
                    cols = hold.enter_context(nc.sbuf_tensor("a_cols", [P, NT, 2, HEADS], F32))
                    em = hold.enter_context(nc.sbuf_tensor("em_cols", [P, NTX, 2, HEADS], F32))
                    with ExitStack() as inner:
                        gates = inner.enter_context(nc.sbuf_tensor("gates", [P, TT], F32))
                        qkv_phase(nc, sem, keep, scr, io, gates)
                        end_phase()
                        gate_phase(nc, sem, keep, scr, io, gates, cols, em)
                        end_phase()
                    attention_phase(nc, sem, keep, scr, io, cols, em)
                    end_phase()
            out_phase(nc, sem, keep, scr, io, layer)
            end_phase()


def modulation(nc, sem, keep, scr, io):
    ps, ident, par, mod = keep["ps"], keep["ident"], keep["par"], keep["mod"]
    NCH = 3 * D // BANK
    RING = 3
    with ExitStack() as st:
        sb = lambda n, s, d=F32: st.enter_context(nc.sbuf_tensor(n, s, d))
        rows1, rows2 = sb("par_rows1", [P, P]), sb("par_rows2", [32, P])
        sg, sc = sb("sc_sig", [P, 16]), sb("sc", [P, 16])
        w = sb("modw", [P, RING, KD, BANK])
        brow, mrow = sb("mod_brow", [2, 2, 3 * D]), sb("mod_row", [2, 2, 3 * D])
        s_id, s_par, s_tp, s_cp, s_sg, s_sc = (sem(n) for n in ("id_made", "par_loaded", "par_turned", "par_copied", "sc_sigmoid", "sc_made"))
        s_w = [sem(f"modw_loaded{i}") for i in range(RING)]
        s_mm, s_row, s_tr, s_col, s_b, s_out = (sem(n) for n in ("mod_product", "mod_row_made", "mod_turned", "mod_col_made", "modb_loaded", "gate_stored"))

        def wsrc(l, n):
            return io["mod_w"][l].rearrange("(k p) n -> p k n", p=P)[:, :, n * BANK:(n + 1) * BANK]

        with nc.Block() as block:
            @block.sync
            def _(sp):
                for src, r0, n in ((io["conv_w"], 0, 48), (io["m_conv_w"], 48, 48)):
                    sp.dma_start(rows1[r0:r0 + n, :], src[0].rearrange("j (f p) -> (j f) p", p=P)).then_inc(s_par, 16)
                for src, r0 in ((io["m_norm_g"], 96), (io["m_skip"], 112)):
                    sp.dma_start(rows1[r0:r0 + 16, :], src[0].rearrange("(f p) -> f p", p=P)).then_inc(s_par, 16)
                sp.dma_start(rows2[0:16, :], io["norm_g"].rearrange("l (k p) -> (l k) p", p=P)).then_inc(s_par, 16)
                sp.dma_start(rows2[16:24, :], io["c"][0].rearrange("(k p) -> k p", p=P)).then_inc(s_par, 16)
                sp.dma_start(rows2[24:32, :], io["c_ctx"].rearrange("(k p) -> k p", p=P)).then_inc(s_par, 16)
                for r in range(2):
                    sp.dma_start(brow[r:r + 1, :, :], io["mod_b"].rearrange("(o l) n -> o l n", o=1)).then_inc(s_b, 16)
                for i in range(2 * NCH):
                    if i >= RING:
                        sp.wait_ge(s_mm, i - RING + 1)
                    sp.dma_start(w[:, i % RING], wsrc(i // NCH, i % NCH)).then_inc(s_w[i % RING], 16)
                for l in range(2):
                    sp.wait_ge(s_row, NCH * (l + 1))
                    sp.dma_start(scr["gates"][l], mrow[:, l, 2 * D:3 * D]).then_inc(s_out, 16)
                sp.wait_ge(s_out, 32)

            @block.gpsimd
            def _(pool):
                nc.gpsimd.memset(ident[:, :], 0.0).then_inc(s_id, 1)
                pool.wait_ge(s_id, 1)
                nc.gpsimd.affine_select(out=ident[:, :], in_=ident[:, :], compare_op=ALU.not_equal, fill=1.0, base=0,
                                        pattern=[[-1, P]], channel_multiplier=1).then_inc(s_id, 1)

            @block.tensor
            def _(pe):
                pe.wait_ge(s_id, 2)
                pe.wait_ge(s_par, 16 * 7)
                nc.tensor.transpose(ps[:, 0, 0:P], rows1[:, :], ident[:, :]).then_inc(s_tp, 1)
                nc.tensor.transpose(ps[:, 1, 0:32], rows2[:, :], ident[0:32, 0:32]).then_inc(s_tp, 1)
                pe.wait_ge(s_sc, 1)
                for i in range(2 * NCH):
                    pe.wait_ge(s_w[i % RING], 16 * (i // RING + 1))
                    if i >= 4:
                        pe.wait_ge(s_row, i - 3)
                    for k in range(KD):
                        mm = nc.tensor.matmul(ps[0:2, 2 + i % 4, :], sc[:, k:16:KD], w[:, i % RING, k, :], start=(k == 0), stop=(k == KD - 1))
                    mm.then_inc(s_mm, 1)
                for l in range(2):
                    pe.wait_ge(s_row, NCH * (l + 1))
                    for j in range(2 * KD):
                        tr = nc.tensor.transpose(ps[:, l, 2 * j:2 * j + 2], mrow[:, l, j * P:(j + 1) * P], ident[0:2, 0:2])
                    tr.then_inc(s_tr, 1)

            @block.scalar
            def _(act):
                act.wait_ge(s_tp, 2)
                nc.scalar.activation(par[:, 0:P], ps[:, 0, 0:P], ACT.Copy).then_inc(s_cp, 1)
                nc.scalar.activation(par[:, P:160], ps[:, 1, 0:32], ACT.Copy).then_inc(s_cp, 1)
                act.wait_ge(s_cp, 2)
                nc.scalar.activation(sg[:, :], par[:, COL_C:COL_C + 16], ACT.Sigmoid).then_inc(s_sg, 1)

            @block.vector
            def _(dve):
                dve.wait_ge(s_sg, 1)
                nc.vector.tensor_tensor(sc[:, :], sg[:, :], par[:, COL_C:COL_C + 16], ALU.mult).then_inc(s_sc, 1)
                dve.wait_ge(s_b, 32)
                for i in range(2 * NCH):
                    l, n = i // NCH, i % NCH
                    dve.wait_ge(s_mm, i + 1)
                    nc.vector.tensor_tensor(mrow[:, l, n * BANK:(n + 1) * BANK], ps[0:2, 2 + i % 4, :],
                                            brow[:, l, n * BANK:(n + 1) * BANK], ALU.add).then_inc(s_row, 1)
                for l in range(2):
                    dve.wait_ge(s_tr, l + 1)
                    for s in range(2):
                        g = par[:, COL_G + KD * l:COL_G + KD * (l + 1)]
                        nc.vector.tensor_copy(mod[:, l, 1, s, :], ps[:, l, s:2 * KD:2]).then_inc(s_col, 1)
                        nc.vector.scalar_tensor_tensor(mod[:, l, 0, s, :], ps[:, l, 2 * KD + s:4 * KD:2], 1.0, g, ALU.add, ALU.mult).then_inc(s_col, 1)


def norm_phase(nc, sem, keep, scr, io, layer, h_hi, h_lo):
    ps, ident, mod = keep["ps"], keep["ident"], keep["mod"]
    GT = [(0, 4), (4, 4), (8, 2)]
    if layer == 0:
        tiles = io["x"][0].rearrange("(t p) d -> t p d", p=P), io["ctx"][0].rearrange("(t p) d -> t p d", p=P)
        src = lambda t: tiles[0][t] if t < NTX else tiles[1][t - NTX]
    else:
        tiles = scr["x1"].rearrange("(t p) d -> t p d", p=P)
        src = lambda t: tiles[t]
    with ExitStack() as st:
        sb = lambda n, s, d=F32: st.enter_context(nc.sbuf_tensor(f"n{layer}_{n}", s, d))
        x, xn = sb("x", [P, 4, D]), sb("xn", [P, 2, 4, D])
        junk, ss, rt, rs = sb("junk", [P, D]), sb("ss", [P, NT]), sb("rt", [P, NT]), sb("rs", [P, NT])
        hf = sb("hf", [P, 2, BANK])
        s_x = [sem(f"n{layer}_x_loaded{i}") for i in range(4)]
        s_ss, s_ms, s_rt, s_rs, s_xn, s_tr, s_hf, s_hi, s_lo = (sem(f"n{layer}_{n}") for n in (
            "squared", "mean", "root", "rsqrt", "scaled", "turned", "modulated", "hi_made", "lo_made"))
        with nc.Block() as block:
            @block.sync
            def _(sp):
                for t in range(NT):
                    if t >= 4:
                        sp.wait_ge(s_xn, t - 3)
                    sp.dma_start(x[:, t % 4, :], src(t)).then_inc(s_x[t % 4], 16)

            def chunks():
                n = 0
                for g, (t0, nt) in enumerate(GT):
                    for k in range(KD):
                        yield n, g, t0, nt, k
                        n += 1

            @block.scalar
            def _(act):
                def roots(t):
                    act.wait_ge(s_x[t % 4], 16 * (t // 4 + 1))
                    if t:
                        act.wait_ge(s_ss, t)
                    nc.scalar.activation(junk[:, :], x[:, t % 4, :], ACT.Square, accum_out=ss[:, t:t + 1]).then_inc(s_ss, 1)
                    act.wait_ge(s_ms, t + 1)
                    nc.scalar.activation(rt[:, t:t + 1], rs[:, t:t + 1], ACT.Sqrt).then_inc(s_rt, 1)

                for t in range(4):
                    roots(t)
                for n, g, t0, nt, k in chunks():
                    if k < 4 and t0 + nt + k < min(NT, t0 + nt + 4):
                        roots(t0 + nt + k)
                    s = 0 if g < 2 else 1
                    act.wait_ge(s_tr, n + 1)
                    if n >= 2:
                        act.wait_ge(s_lo, n - 1)
                    nc.scalar.activation(hf[:, n % 2, 0:nt * P], ps[:, n % 4, 0:nt * P], ACT.Identity,
                                         bias=mod[:, layer, 1, s, k:k + 1], scale=mod[:, layer, 0, s, k:k + 1]).then_inc(s_hf, 1)
                    act.wait_ge(s_hf, n + 1)
                    nc.scalar.activation(h_hi[:, k, t0 * P:(t0 + nt) * P], hf[:, n % 2, 0:nt * P], ACT.Copy).then_inc(s_hi, 1)

            @block.vector
            def _(dve):
                def scale(t):
                    dve.wait_ge(s_ss, t + 1)
                    nc.vector.tensor_scalar(rs[:, t:t + 1], ss[:, t:t + 1], 1.0 / D, EPS, ALU.mult, ALU.add).then_inc(s_ms, 1)
                    dve.wait_ge(s_rt, t + 1)
                    nc.vector.reciprocal(ss[:, t:t + 1], rt[:, t:t + 1]).then_inc(s_rs, 1)
                    dve.wait_ge(s_rs, t + 1)
                    if t >= 8:
                        dve.wait_ge(s_tr, KD)
                    nc.vector.tensor_scalar(xn[:, (t // 4) % 2, t % 4, :], x[:, t % 4, :], ss[:, t:t + 1], None, ALU.mult).then_inc(s_xn, 1)

                for t in range(4):
                    scale(t)
                for n, g, t0, nt, k in chunks():
                    if k < 4 and t0 + nt + k < min(NT, t0 + nt + 4):
                        scale(t0 + nt + k)
                    dve.wait_ge(s_hi, n + 1)
                    cols = slice(t0 * P, (t0 + nt) * P)
                    nc.vector.tensor_tensor(h_lo[:, k, cols], hf[:, n % 2, 0:nt * P], h_hi[:, k, cols].bitcast(F32), ALU.subtract).then_inc(s_lo, 1)

            @block.tensor
            def _(pe):
                for n, g, t0, nt, k in chunks():
                    if k == 0:
                        pe.wait_ge(s_xn, t0 + nt)
                    if n >= 4:
                        pe.wait_ge(s_hf, n - 3)
                    for i in range(nt):
                        tr = nc.tensor.transpose(ps[:, n % 4, i * P:(i + 1) * P], xn[:, g % 2, i, k * P:(k + 1) * P], ident[:, :])
                    tr.then_inc(s_tr, 1)


def conv_taps(nc, dve, out, x, par, col0, f, s_done, base):
    tap = lambda j: par[:, bass.ds(col0 + j * KI + f, 1)]
    nc.vector.tensor_scalar(out[:, :], x[:, :], tap(1), None, ALU.mult).then_inc(s_done, 1)
    xr, orow = (a[:, 0:TX].rearrange("p (r c) -> p r c", c=ROW) for a in (x, out))
    dve.wait_ge(s_done, base + 1)
    nc.vector.scalar_tensor_tensor(orow[:, :, 1:], xr[:, :, :-1], tap(0), orow[:, :, 1:], ALU.mult, ALU.add).then_inc(s_done, 1)
    nc.vector.scalar_tensor_tensor(out[:, TX + 1:], x[:, TX:TT - 1], tap(0), out[:, TX + 1:], ALU.mult, ALU.add).then_inc(s_done, 1)
    dve.wait_ge(s_done, base + 3)
    nc.vector.scalar_tensor_tensor(orow[:, :, :-1], xr[:, :, 1:], tap(2), orow[:, :, :-1], ALU.mult, ALU.add).then_inc(s_done, 1)
    nc.vector.scalar_tensor_tensor(out[:, TX:TT - 1], x[:, TX + 1:], tap(2), out[:, TX:TT - 1], ALU.mult, ALU.add).then_inc(s_done, 1)


def conv_in_phase(nc, sem, keep, scr, io, h_hi, h_lo):
    ps, par = keep["ps"], keep["par"]
    UNITS = (1, 2, 3, 0)
    U, G = len(UNITS), len(GROUPS)
    CH = U * G
    R = 6
    w_src = io["conv_w_in"][0].rearrange("(k p) n -> p k n", p=P)
    y_dst = scr["yT"].rearrange("(f p) t -> f p t", p=P)
    with ExitStack() as st:
        sb = lambda n, s, d=F32: st.enter_context(nc.sbuf_tensor(f"a0_{n}", s, d))
        raw, w_hi, w_lo = sb("raw", [P, U, KD, P]), sb("w_hi", [P, U, KD, P], F32R), sb("w_lo", [P, U, KD, P], F32R)
        ev = sb("ev", [P, U, TT])
        sg, cu, cv, y = sb("sg", [P, TT]), sb("cu", [P, TT]), sb("cv", [P, TT]), sb("y", [P, TT])
        s_w = [sem(f"a0_w_loaded{q}") for q in range(U)]
        s_hi, s_lo, s_mm, s_ev, s_sg, s_ew, s_y, s_st = (sem(f"a0_{n}") for n in (
            "w_hi_made", "w_lo_made", "chunk_done", "chunk_read", "sigmoid", "mixed", "y_made", "y_stored"))
        EW = 8
        with nc.Block() as block:
            @block.sync
            def _(sp):
                def load(f, q):
                    sp.dma_start(raw[:, q], w_src[:, :, bass.ds(UNITS[q] * DI + f * P, P)]).then_inc(s_w[q], 16)

                def store(f):
                    sp.wait_ge(s_y, f + 1)
                    sp.dma_start(y_dst[bass.ds(f, 1)].rearrange("a p t -> p (a t)"), y[:, :]).then_inc(s_st, 16)

                for q in range(U):
                    load(0, q)

                def step(f, first, last):
                    nxt = f + 1 if first or last else sp.snap(f + 1)
                    if not last:
                        for q in range(U):
                            if q < U - 2:
                                sp.wait_ge(s_lo, U * f + q + 1)
                            elif q == U - 2:
                                sp.wait_ge(s_lo, U * f + U)
                            load(nxt, q)
                    if not first:
                        store(f - 1)
                over(sp, KI, step)
                store(KI - 1)
                sp.wait_ge(s_st, 16 * KI)

            @block.tensor
            def _(pe):
                def step(f, first, last):
                    for q in range(U):
                        pe.wait_ge(s_lo, U * f + q + 1)
                        for g, (t0, n) in enumerate(GROUPS):
                            c = q * G + g
                            if not (first and c < R):
                                pe.wait_ge(s_ev, CH * f + c - R + 1)
                            out = ps[:, c % R, 0:n]
                            for k in range(KD):
                                mm = mm3(nc, out, w_hi[:, q, k], w_lo[:, q, k], h_hi[:, k, t0:t0 + n], h_lo[:, k, t0:t0 + n], k == 0, k == KD - 1)
                            mm.then_inc(s_mm, 1)
                over(pe, KI, step, last_differs=False)

            @block.scalar
            def _(act):
                def split(f, q):
                    act.wait_ge(s_w[q], 16 * (f + 1))
                    nc.scalar.activation(w_hi[:, q], raw[:, q], ACT.Copy).then_inc(s_hi, 1)

                for q in range(U):
                    split(0, q)

                def step(f, first, last):
                    for q in range(U):
                        if not first:
                            act.wait_ge(s_ew, EW * (f - 1) + (6, 6, 7, 8)[q])
                        for g, (t0, n) in enumerate(GROUPS):
                            c = q * G + g
                            act.wait_ge(s_mm, CH * f + c + 1)
                            if q == 2:
                                nc.scalar.activation(sg[:, t0:t0 + n], ps[:, c % R, 0:n], ACT.Sigmoid).then_inc(s_sg, 1)
                            nc.scalar.activation(ev[:, q, t0:t0 + n], ps[:, c % R, 0:n], ACT.Copy).then_inc(s_ev, 1)
                        if not last:
                            split(f + 1, q)
                over(act, KI, step)

            @block.vector
            def _(dve):
                def split(f, q, mm=None):
                    dve.wait_ge(s_hi, U * f + q + 1)
                    nc.vector.tensor_tensor(w_lo[:, q], raw[:, q], w_hi[:, q].bitcast(F32), ALU.subtract).then_inc(s_lo, 1)

                for q in range(U):
                    split(0, q)

                def step(f, first, last):
                    if not last:
                        split(f + 1, 0)
                    dve.wait_ge(s_ev, CH * f + 2 * G)
                    nc.vector.tensor_tensor(cu[:, :], ev[:, 0, :], ev[:, 1, :], ALU.mult).then_inc(s_ew, 1)
                    dve.wait_ge(s_ew, EW * f + 1)
                    conv_taps(nc, dve, cv, cu, par, COL_CONV, f, s_ew, EW * f + 1)
                    if not last:
                        split(f + 1, 1)
                    dve.wait_ge(s_ev, CH * f + 3 * G)
                    dve.wait_ge(s_sg, G * (f + 1))
                    dve.wait_ge(s_ew, EW * f + 6)
                    nc.vector.tensor_tensor(ev[:, 2, :], ev[:, 2, :], sg[:, :], ALU.mult).then_inc(s_ew, 1)
                    dve.wait_ge(s_ew, EW * f + 7)
                    nc.vector.tensor_tensor(cv[:, :], cv[:, :], ev[:, 2, :], ALU.mult).then_inc(s_ew, 1)
                    if not last:
                        split(f + 1, 2)
                    dve.wait_ge(s_ev, CH * (f + 1))
                    dve.wait_ge(s_ew, EW * f + 8)
                    if not first:
                        dve.wait_ge(s_st, 16 * f)
                    nc.vector.tensor_tensor(y[:, :], cv[:, :], ev[:, 3, :], ALU.mult).then_inc(s_y, 1)
                    if not last:
                        split(f + 1, 3)
                over(dve, KI, step)


def lstm_in_phase(nc, sem, keep, scr, io, h_hi, h_lo):
    ps, par = keep["ps"], keep["par"]
    U = 3
    GR = (GROUPS, GROUPS[:2], GROUPS[:2])
    CH = sum(len(g) for g in GR)
    FIRST = (0, 3, 5)
    R = CH
    w_src = io["m_w_in"][0].rearrange("(k p) n -> p k n", p=P)
    by_tile = lambda a: a.rearrange("(f p) t -> f p t", p=P)
    dst = [by_tile(scr[n]) for n in ("uT", "ucT", "ymul", "yadd")]
    with ExitStack() as st:
        sb = lambda n, s, d=F32: st.enter_context(nc.sbuf_tensor(f"a1_{n}", s, d))
        raw, w_hi, w_lo = sb("raw", [P, U, KD, P]), sb("w_hi", [P, U, KD, P], F32R), sb("w_lo", [P, U, KD, P], F32R)
        u, cv, sc, uc = sb("u", [P, TT]), sb("cv", [P, TT]), sb("sc", [P, TT]), sb("uc", [P, TT])
        z, sz, so, mul, add = (sb(n, [P, TX]) for n in ("z", "sz", "so", "mul", "add"))
        out_tiles = (u, uc, mul, add)
        s_w = [sem(f"a1_w_loaded{q}") for q in range(U)]
        s_hi, s_lo, s_mm, s_ev, s_cv, s_scv, s_ew, s_st = (sem(f"a1_{n}") for n in (
            "w_hi_made", "w_lo_made", "chunk_done", "chunk_read", "conv_round", "conv_sigmoid", "mixed", "stored"))
        s_uo = sem("a1_u_stored")
        EW = 5
        with nc.Block() as block:
            @block.sync
            def _(sp):
                def load(f, q):
                    sp.dma_start(raw[:, q], w_src[:, :, bass.ds(q * DI + f * P, P)]).then_inc(s_w[q], 16)

                def store(f):
                    sp.wait_ge(s_ev, CH * f + 3)
                    sp.dma_start(dst[0][bass.ds(f, 1)].rearrange("a p t -> p (a t)"), u[:, :]).then_inc(s_uo, 16)
                    sp.wait_ge(s_ew, EW * (f + 1))
                    for i in range(1, 4):
                        sp.dma_start(dst[i][bass.ds(f, 1)].rearrange("a p t -> p (a t)"), out_tiles[i][:, :]).then_inc(s_st, 16)

                for q in range(U):
                    load(0, q)

                def step(f, first, last):
                    nxt = f + 1 if first or last else sp.snap(f + 1)
                    if not last:
                        for q in range(U):
                            sp.wait_ge(s_lo, U * f + q + 1)
                            load(nxt, q)
                    if not first:
                        store(f - 1)
                over(sp, KI, step)
                store(KI - 1)
                sp.wait_ge(s_uo, 16 * KI)
                sp.wait_ge(s_st, 48 * KI)

            @block.tensor
            def _(pe):
                def step(f, first, last):
                    for q in range(U):
                        pe.wait_ge(s_lo, U * f + q + 1)
                        for g, (t0, n) in enumerate(GR[q]):
                            c = FIRST[q] + g
                            if not first:
                                pe.wait_ge(s_ev, CH * f + c - R + 1)
                            out = ps[:, c, 0:n]
                            for k in range(KD):
                                mm = mm3(nc, out, w_hi[:, q, k], w_lo[:, q, k], h_hi[:, k, t0:t0 + n], h_lo[:, k, t0:t0 + n], k == 0, k == KD - 1)
                            mm.then_inc(s_mm, 1)
                over(pe, KI, step, last_differs=False)

            @block.scalar
            def _(act):
                def split(f, q):
                    act.wait_ge(s_w[q], 16 * (f + 1))
                    nc.scalar.activation(w_hi[:, q], raw[:, q], ACT.Copy).then_inc(s_hi, 1)

                for q in range(U):
                    split(0, q)

                def step(f, first, last):
                    if not first:
                        act.wait_ge(s_uo, 16 * f)
                        act.wait_ge(s_cv, 5 * f)
                    for g, (t0, n) in enumerate(GR[0]):
                        act.wait_ge(s_mm, CH * f + g + 1)
                        nc.scalar.activation(u[:, t0:t0 + n], ps[:, g, 0:n], ACT.Copy).then_inc(s_ev, 1)
                    if not last:
                        split(f + 1, 0)
                    act.wait_ge(s_cv, 5 * (f + 1))
                    if not first:
                        act.wait_ge(s_ew, EW * f)
                    nc.scalar.activation(sc[:, :], cv[:, :], ACT.Sigmoid).then_inc(s_scv, 1)
                    for g, (t0, n) in enumerate(GR[1]):
                        c = FIRST[1] + g
                        act.wait_ge(s_mm, CH * f + c + 1)
                        nc.scalar.activation(sz[:, t0:t0 + n], ps[:, c, 0:n], ACT.Sigmoid).then_inc(s_scv, 1)
                        nc.scalar.activation(z[:, t0:t0 + n], ps[:, c, 0:n], ACT.Copy).then_inc(s_ev, 1)
                    if not last:
                        split(f + 1, 1)
                    for g, (t0, n) in enumerate(GR[2]):
                        c = FIRST[2] + g
                        act.wait_ge(s_mm, CH * f + c + 1)
                        nc.scalar.activation(so[:, t0:t0 + n], ps[:, c, 0:n], ACT.Sigmoid).then_inc(s_ev, 1)
                    if not last:
                        split(f + 1, 2)
                over(act, KI, step)

            @block.vector
            def _(dve):
                def split(f, q):
                    dve.wait_ge(s_hi, U * f + q + 1)
                    nc.vector.tensor_tensor(w_lo[:, q], raw[:, q], w_hi[:, q].bitcast(F32), ALU.subtract).then_inc(s_lo, 1)

                for q in range(U):
                    split(0, q)

                def step(f, first, last):
                    dve.wait_ge(s_ev, CH * f + 3)
                    if not first:
                        dve.wait_ge(s_ew, EW * f)
                    conv_taps(nc, dve, cv, u, par, COL_MCONV, f, s_cv, 5 * f)
                    if not last:
                        split(f + 1, 0)
                    dve.wait_ge(s_cv, 5 * (f + 1))
                    dve.wait_ge(s_scv, 3 * f + 1)
                    if not first:
                        dve.wait_ge(s_st, 48 * f)
                    nc.vector.tensor_tensor(uc[:, :], cv[:, :], sc[:, :], ALU.mult).then_inc(s_ew, 1)
                    dve.wait_ge(s_ev, CH * f + 5)
                    dve.wait_ge(s_scv, 3 * f + 3)
                    nc.vector.tensor_tensor(z[:, :], z[:, :], sz[:, :], ALU.mult).then_inc(s_ew, 1)
                    if not last:
                        split(f + 1, 1)
                    dve.wait_ge(s_ew, EW * f + 2)
                    nc.vector.scalar_tensor_tensor(add[:, :], uc[:, 0:TX], par[:, bass.ds(COL_SKIP + f, 1)], z[:, :], ALU.mult, ALU.mult).then_inc(s_ew, 1)
                    dve.wait_ge(s_ev, CH * (f + 1))
                    nc.vector.scalar_tensor_tensor(mul[:, :], so[:, :], par[:, bass.ds(COL_NORM + f, 1)], z[:, :], ALU.mult, ALU.mult).then_inc(s_ew, 2)
                    if not last:
                        split(f + 1, 2)
                over(dve, KI, step)


def qkv_phase(nc, sem, keep, scr, io, gates):
    ps = keep["ps"]
    UN = 6
    RS = 3
    EB = 2
    G = len(GROUPS)
    CH = UN * EB * G
    R = 4
    TILES = UN * EB
    RT = 3
    XS = 4
    SCALE = float(DH) ** -0.5
    w_src = [io[n][0].rearrange("h (k p) e -> h p k e", p=P) for n in ("m_wq", "m_wk", "m_wv")]
    x_src = [scr[n].rearrange("(f p) t -> f p t", p=P) for n in ("ucT", "uT")]
    dst = scr["qkvT"].rearrange("m (f p) t -> m f p t", p=P)
    KINDS = (0, 2, 1, 3)
    with ExitStack() as st:
        sb = lambda n, s, d=F32: st.enter_context(nc.sbuf_tensor(f"q_{n}", s, d))
        raw, w_hi, w_lo = sb("raw", [P, RS, KH, EB * P]), sb("w_hi", [P, RS, KH, EB * P], F32R), sb("w_lo", [P, RS, KH, EB * P], F32R)
        xr = sb("xr", [P, XS, TT])
        x_hi, x_lo = sb("x_hi", [P, 2, KH, TT], F32R), sb("x_lo", [P, 2, KH, TT], F32R)
        wg = sb("wg", [P, 3, HEADS * KH, 4 * HEADS])
        wgp = sb("wgp", [P, TILES, P])
        tile = sb("tile", [P, RT, TT])
        bg = sb("bg", [P, 1])
        s_w = [sem(f"q_w_loaded{i}") for i in range(RS)]
        s_xr = [sem(f"q_x_loaded{i}") for i in range(XS)]
        s_st = [sem(f"q_tile_stored{i}") for i in range(RT)]
        s_hi, s_lo, s_xhi, s_xlo, s_mm, s_ev, s_g, s_gr, s_wg, s_wgz, s_wgp = (sem(f"q_{n}") for n in (
            "w_hi_made", "w_lo_made", "x_hi_made", "x_lo_made", "chunk_done", "chunk_read",
            "gates_done", "gates_read", "gate_w_loaded", "gate_w_cleared", "gate_w_placed"))

        def xwhich(h, j):
            return x_src[j // KH][bass.ds(h * KH + j % KH, 1)].rearrange("a p t -> p (a t)")

        with nc.Block() as block:
            @block.sync
            def _(sp):
                def load_w(h, n):
                    m, e0 = n // 2, (n % 2) * EB * P
                    sp.dma_start(raw[:, n % RS], w_src[m][bass.ds(h, 1), :, :, e0:e0 + EB * P].rearrange("a p k e -> p (a k) e")).then_inc(s_w[n % RS], 16)

                def load_x(h, j):
                    sp.dma_start(xr[:, j % XS], xwhich(h, j)).then_inc(s_xr[j % XS], 16)

                for j in range(KH):
                    load_x(0, j)
                load_w(0, 0)
                sp.dma_start(wg[:, :, :, :], io["m_w_gate"][0].rearrange("(m f p) c -> p m f c", m=3, p=P)).then_inc(s_wg, 16)
                for q, kind in enumerate(KINDS):
                    sp.dma_start(bg[32 * kind:32 * kind + HEADS, :], io["m_b_gate"][0, q * HEADS:(q + 1) * HEADS].rearrange("(h o) -> h o", o=1)).then_inc(s_wg, 16)
                load_w(0, 1)
                load_w(0, 2)
                for j in range(KH, 2 * KH):
                    sp.wait_ge(s_xlo, j - KH + 1)
                    load_x(0, j)

                def step(h, first, last):
                    for n in range(UN):
                        if n + RS < UN or not last:
                            if n != 2:
                                sp.wait_ge(s_lo, UN * h + (n + 1 if n != 1 else 3))
                            if n + RS >= UN:
                                load_w(h + 1, n + RS - UN)
                            elif n == 1:
                                load_w(h, 5)
                                load_w(h, 4)
                            elif n != 2:
                                load_w(h, n + RS)
                        if n == 1 and not last:
                            for j in range(KH):
                                sp.wait_ge(s_xlo, 8 * h + KH + j + 1)
                                load_x(h + 1, j)
                        for e in range(EB):
                            t = n * EB + e
                            sp.wait_ge(s_ev, CH * h + (t + 1) * G)
                            sp.dma_start(dst[n // 2][bass.ds(h * KH + t % KH, 1)].rearrange("a p t -> p (a t)"), tile[:, t % RT, :]).then_inc(s_st[t % RT], 16)
                    if not last:
                        for j in range(KH, 2 * KH):
                            sp.wait_ge(s_xlo, 8 * (h + 1) + j - KH + 1)
                            load_x(h + 1, j)
                over(sp, HEADS, step)
                for i in range(RT):
                    sp.wait_ge(s_st[i], 16 * HEADS * TILES // RT)

            def gate_products(pe, h, c):
                t, g = c // G, c % G
                t0, n = GROUPS[g]
                pe.wait_ge(s_ev, CH * h + c + 1)
                mm = nc.tensor.matmul(ps[:, R + g, 0:n], wgp[:, t, :], tile[:, t % RT, t0:t0 + n], start=(t == 0), stop=(t == TILES - 1))
                mm.then_inc(s_g, 1)

            @block.tensor
            def _(pe):
                LAG = 2

                def step(h, first, last):
                    for n in range(UN):
                        pe.wait_ge(s_lo, UN * h + n + 1)
                        src = 0 if n < 4 else 1
                        if n == 0:
                            pe.wait_ge(s_xlo, 8 * h + KH)
                        if n == 4:
                            pe.wait_ge(s_xlo, 8 * h + 2 * KH)
                        for e in range(EB):
                            for g, (t0, nn) in enumerate(GROUPS):
                                c = (n * EB + e) * G + g
                                if not (first and c < R):
                                    pe.wait_ge(s_ev, CH * h + c - R + 1)
                                for k in range(KH):
                                    mm = mm3(nc, ps[:, c % R, 0:nn], w_hi[:, n % RS, k, e * P:(e + 1) * P], w_lo[:, n % RS, k, e * P:(e + 1) * P],
                                             x_hi[:, src, k, t0:t0 + nn], x_lo[:, src, k, t0:t0 + nn], k == 0, k == KH - 1)
                                mm.then_inc(s_mm, 1)
                                if c >= LAG:
                                    if c == LAG:
                                        pe.wait_ge(s_wgp, 12 * (h + 1))
                                        if not first:
                                            pe.wait_ge(s_gr, G * h)
                                    gate_products(pe, h, c - LAG)
                    for c in range(CH - LAG, CH):
                        gate_products(pe, h, c)
                over(pe, HEADS, step, last_differs=False)

            @block.scalar
            def _(act):
                def split_w(h, n):
                    act.wait_ge(s_w[n % RS], 32 * h + 16 * (n // RS + 1))
                    nc.scalar.activation(w_hi[:, n % RS], raw[:, n % RS], ACT.Copy).then_inc(s_hi, 1)

                def split_x(h, j):
                    act.wait_ge(s_xr[j % XS], 32 * h + 16 * (j // XS + 1))
                    nc.scalar.activation(x_hi[:, j // KH, j % KH, :], xr[:, j % XS, :], ACT.Copy).then_inc(s_xhi, 1)

                for j in range(KH):
                    split_x(0, j)
                for n in range(RS):
                    split_w(0, n)
                for j in range(KH, 2 * KH):
                    split_x(0, j)

                def step(h, first, last):
                    for n in range(UN):
                        for c in range(n * EB * G, (n + 1) * EB * G):
                            t, g = c // G, c % G
                            t0, nn = GROUPS[g]
                            act.wait_ge(s_mm, CH * h + c + 1)
                            if g == 0 and not (first and t < RT):
                                act.wait_ge(s_st[t % RT], 16 * ((TILES // RT) * h + t // RT))
                                act.wait_ge(s_g, CH * h + (t - RT + 1) * G)
                            nc.scalar.activation(tile[:, t % RT, t0:t0 + nn], ps[:, c % R, 0:nn], ACT.Copy,
                                                 scale=SCALE if n // 2 == 1 else 1.0).then_inc(s_ev, 1)
                        if n + RS < UN:
                            split_w(h, n + RS)
                        elif not last:
                            split_w(h + 1, n + RS - UN)
                        if n == 1 and not first:
                            for j in range(KH, 2 * KH):
                                split_x(h, j)
                        if n == 4 and not last:
                            for j in range(KH):
                                split_x(h + 1, j)
                over(act, HEADS, step)

            @block.vector
            def _(dve):
                def split_w(h, n):
                    dve.wait_ge(s_hi, UN * h + n + 1)
                    nc.vector.tensor_tensor(w_lo[:, n % RS], raw[:, n % RS], w_hi[:, n % RS].bitcast(F32), ALU.subtract).then_inc(s_lo, 1)

                def split_x(h, j):
                    dve.wait_ge(s_xhi, 8 * h + j + 1)
                    a = (slice(None), j // KH, j % KH)
                    nc.vector.tensor_tensor(x_lo[a], xr[:, j % XS, :], x_hi[a].bitcast(F32), ALU.subtract).then_inc(s_xlo, 1)

                def place(h):
                    for m in range(3):
                        for q, kind in enumerate(KINDS):
                            nc.vector.tensor_copy(wgp[:, KH * m:KH * (m + 1), 32 * kind:32 * kind + HEADS],
                                                  wg[:, m, bass.ds(h * KH, KH), q * HEADS:(q + 1) * HEADS]).then_inc(s_wgp, 1)

                nc.vector.memset(wgp[:, :, :], 0.0).then_inc(s_wgz, 1)
                nc.vector.memset(gates[:, :], 0.0).then_inc(s_wgz, 1)
                for j in range(KH):
                    split_x(0, j)
                split_w(0, 0)
                dve.wait_ge(s_wgz, 2)
                dve.wait_ge(s_wg, 80)
                place(0)
                split_w(0, 1)
                split_w(0, 2)
                for j in range(KH, 2 * KH):
                    split_x(0, j)

                def step(h, first, last):
                    for n in range(UN):
                        if n + RS < UN:
                            split_w(h, n + RS)
                        elif not last:
                            split_w(h + 1, n + RS - UN)
                        if n == 1 and not first:
                            for j in range(KH, 2 * KH):
                                split_x(h, j)
                        if n == 4 and not last:
                            for j in range(KH):
                                split_x(h + 1, j)
                    dve.wait_ge(s_g, CH * (h + 1))
                    for g, (t0, nn) in enumerate(GROUPS):
                        nc.vector.tensor_tensor(gates[:, t0:t0 + nn], gates[:, t0:t0 + nn], ps[:, R + g, 0:nn], ALU.add).then_inc(s_gr, 1)
                    if not last:
                        place(h + 1)
                over(dve, HEADS, step)
                dve.wait_ge(s_gr, G * HEADS)
                for kind in range(4):
                    r = slice(32 * kind, 32 * kind + HEADS)
                    nc.vector.tensor_scalar(gates[r, :], gates[r, :], bg[r, :], None, ALU.add).then_inc(s_wgz, 1)


def gate_phase(nc, sem, keep, scr, io, gates, cols, em):
    ps, ident = keep["ps"], keep["ident"]
    with ExitStack() as st:
        sb = lambda n, s, d=F32: st.enter_context(nc.sbuf_tensor(f"g_{n}", s, d))
        ones, lf, t1, bsum, big = (sb(n, [64, TT]) for n in ("ones", "lf", "t1", "bsum", "m"))
        a = sb("a", [P, TT])
        mc = sb("mc", [64, 1])
        s_v, s_a, s_tr, s_cp, s_out = (sem(f"g_{n}") for n in ("vector_step", "scalar_step", "turned", "copied", "stored"))
        nv = [0]

        def done(ins):
            nv[0] += 1
            ins.then_inc(s_v, 1)

        X, C = slice(0, TX), slice(TX, TT)
        with nc.Block() as block:
            @block.vector
            def _(dve):
                def then():
                    dve.wait_ge(s_v, nv[0])
                done(nc.vector.memset(ones[:, :], 1.0))
                done(nc.vector.memset(a[:, :], 0.0))
                done(nc.vector.memset(lf[:, :], 0.0))
                done(nc.vector.memset(mc[:, :], 0.0))
                then()
                f = gates[64:128, :]
                done(nc.vector.scalar_tensor_tensor(t1[:, :], f, -1.0, f, ALU.mult, ALU.max))
                then()
                dve.wait_ge(s_a, 2)
                done(nc.vector.tensor_scalar(bsum[:, :], f, 0.0, None, ALU.min))
                then()
                done(nc.vector.tensor_tensor(lf[:, :], bsum[:, :], t1[:, :], ALU.subtract))
                then()
                for d in range(2):
                    r = slice(32 * d, 32 * d + HEADS)
                    way = (lambda ap: ap) if d == 0 else (lambda ap: ap[:, ::-1])
                    last = (TX - 1, TT - 1) if d == 0 else (0, TX)
                    for s in (X, C):
                        done(nc.vector.tensor_tensor_scan(way(bsum[r, s]), ones[r, s], way(lf[r, s]), 0.0, ALU.mult, ALU.add))
                    then()
                    done(nc.vector.tensor_tensor(a[r, :], gates[r, :], bsum[r, :], ALU.subtract))
                    then()
                    total = bsum[r, last[1]:last[1] + 1]
                    done(nc.vector.tensor_scalar(a[r, C], a[r, C], total, None, ALU.add))
                    then()
                    done(nc.vector.reduce_max(mc[r, :], a[r, C], mybir.AxisListType.X))
                    then()
                    done(nc.vector.tensor_tensor(mc[r, :], mc[r, :], total, ALU.max))
                    then()
                    done(nc.vector.tensor_tensor_scan(way(big[r, X]), ones[r, X], way(a[r, X]), mc[r, :], ALU.mult, ALU.max))
                    then()
                    done(nc.vector.tensor_tensor(t1[r, X], big[r, X], bsum[r, X], ALU.add))
                    done(nc.vector.tensor_scalar(lf[r, X], big[r, X], -1.0, None, ALU.mult))
                    then()

            n_all = 8 - 1 + 2 * 9

            @block.scalar
            def _(act):
                act.wait_ge(s_v, 5)
                nc.scalar.activation(t1[:, :], t1[:, :], ACT.Exp, scale=-1.0).then_inc(s_a, 1)
                act.wait_ge(s_a, 1)
                nc.scalar.activation(t1[:, :], t1[:, :], ACT.Ln, bias=1.0).then_inc(s_a, 1)
                act.wait_ge(s_v, n_all)
                for d in range(2):
                    nc.scalar.activation(a[64 + 32 * d:64 + 32 * d + HEADS, X], t1[32 * d:32 * d + HEADS, X], ACT.Exp, scale=-1.0).then_inc(s_a, 1)
                for t in range(NT):
                    act.wait_ge(s_tr, t + 1)
                    for d in range(2):
                        cp = nc.scalar.activation(cols[:, t, d, :], ps[:, t % 8, 32 * d:32 * d + HEADS], ACT.Copy)
                        if t < NTX:
                            cp = nc.scalar.activation(em[:, t, d, :], ps[:, t % 8, 64 + 32 * d:64 + 32 * d + HEADS], ACT.Copy)
                    cp.then_inc(s_cp, 1)

            @block.tensor
            def _(pe):
                pe.wait_ge(s_a, 4)
                pe.wait_ge(s_v, n_all)
                for t in range(NT):
                    if t >= 8:
                        pe.wait_ge(s_cp, t - 7)
                    nc.tensor.transpose(ps[:, t % 8, 0:P], a[:, t * P:(t + 1) * P], ident[:, :]).then_inc(s_tr, 1)

            @block.sync
            def _(sp):
                sp.wait_ge(s_v, n_all)
                for d in range(2):
                    sp.dma_start(scr["nmrow"][d], lf[32 * d:32 * d + HEADS, X]).then_inc(s_out, 16)
                sp.wait_ge(s_out, 32)
            assert nv[0] == n_all, nv


def attention_phase(nc, sem, keep, scr, io, cols, em):
    ps, ident = keep["ps"], keep["ident"]
    NG = 2
    JT = BANK // P
    FULL, DIAG = BANK, BANK + P
    PT = 4 * FULL + 4 * FULL + 4 * DIAG
    NV = KH * 3
    VCH = [(0, 4), (4, 4), (8, 2)]
    src = scr["qkvT"].rearrange("m (h k p) t -> m h k p t", p=P, k=KH)
    fac = [scr[n].rearrange("(f p) t -> f p t", p=P) for n in ("ymul", "yadd")]
    y_dst = scr["yT"].rearrange("(f p) t -> f p t", p=P)

    def subs(g):
        out = []
        for t in (NTX, NTX + 1):
            for d in range(2):
                out.append((t, d, len(out) * FULL))
        off = 4 * FULL
        for t in range(NTX):
            if not JT * g <= t < JT * (g + 1):
                out.append((t, 0 if t < JT * g else 1, off))
                off += FULL
        for t in range(JT * g, JT * (g + 1)):
            out.append((t, None, off))
            off += DIAG
        return out

    NS = len(subs(0))
    NC_ = NT
    with ExitStack() as st:
        sb = lambda n, s, d=F32: st.enter_context(nc.sbuf_tensor(f"b_{n}", s, d))
        q_hi, q_lo = sb("q_hi", [P, KH, BANK], F32R), sb("q_lo", [P, KH, BANK], F32R)
        k_hi, k_lo = sb("k_hi", [P, KH, TT], F32R), sb("k_lo", [P, KH, TT], F32R)
        v_hi, v_lo = sb("v_hi", [P, NT, DH], F32R), sb("v_lo", [P, NT, DH], F32R)
        p_hi, p_lo = sb("p_hi", [P, PT], F32R), sb("p_lo", [P, PT], F32R)
        qr, kr = sb("qr", [P, KH, BANK]), sb("kr", [P, 2, TT])
        nm = sb("nm", [P, 2, TX])
        e, pr = sb("e", [P, 2, DIAG]), sb("pr", [P, 2, DIAG])
        mask = sb("mask", [P, 2, P])
        one = sb("one", [P, 1])
        hc = sb("hc", [P, NT, 2])
        acc = sb("acc", [P, 2, BANK])
        rn, st6, mv, rstd, tmp4 = sb("rn", [P, 2, JT]), sb("st6", [P, JT, 6]), sb("mv", [P, JT, 2]), sb("rstd", [P, JT]), sb("tmp4", [P, JT])
        hs = sb("hs", [P, JT, DH])
        fc = sb("fc", [P, 2, 2, BANK])
        names = ("q_loaded", "nm_loaded", "q_hi_made", "q_lo_made", "k_hi_made", "k_lo_made", "v_hi_made", "v_lo_made",
                 "v_turned", "s_done", "arg_made", "e_made", "p_made", "p_hi_made", "p_lo_made", "p_summed", "acc_cleared",
                 "den_done", "norm_step", "pv_done", "pvf_read", "pvb_read", "stat_step", "ln_step", "hn_made", "hn_turned", "y_step", "const")
        (s_q, s_nm, s_qhi, s_qlo, s_khi, s_klo, s_vhi, s_vlo, s_vt, s_s, s_arg, s_e, s_p, s_phi, s_plo, s_acc, s_az,
         s_den, s_nrm, s_pv, s_pvf, s_pvb, s_st, s_ln, s_hn, s_ht, s_y, s_c) = (sem("b_" + n) for n in names)
        s_kr, s_fc, s_yst = ([sem(f"b_{n}{i}") for i in range(2)] for n in ("kr_loaded", "fac_loaded", "y_stored"))
        s_hc, s_hs2, s_hs3 = sem("b_head_cols"), sem("b_head_stats"), sem("b_head_mean")

        def chunk_of(i):
            return (i // 2, i % 2 == 1) if i < 4 else (i - 2, True)

        def pieces_to(c):
            return 2 * c + 2 if c < 2 else c + 3

        VAT = {1: [0, 1], 2: [2], 3: [3, 4], 4: [5], 5: [6, 7], 6: [8, 9], 7: [10, 11]}
        SB, HB, VB, PB = 3, 3, 5, 4
        VR = 3
        TAT = (2, 4, 5, 7)

        def gi(h, g):
            return NG * h + g

        def load_kv(eng, h, j):
            eng.dma_start(kr[:, j % 2], src[1 + j // KH][bass.ds(h, 1), j % KH].rearrange("a p t -> p (a t)")).then_inc(s_kr[j % 2], 16)

        with nc.Block() as block:
            @block.sync
            def _(sp):
                def load_q(h, g):
                    for k in range(KH):
                        sp.dma_start(qr[:, k], src[0][bass.ds(h, 1), k, :, g * BANK:(g + 1) * BANK].rearrange("a p t -> p (a t)")).then_inc(s_q, 16)

                def load_nm(h):
                    for d in range(2):
                        sp.dma_start(nm[:, d, :], scr["nmrow"][d][bass.ds(h, 1), :].to_broadcast([P, TX])).then_inc(s_nm, 16)

                def factors(h, g):
                    for k in range(KH + 1):
                        if k < KH:
                            if k > 1 or not isinstance(h, int) or h or g:
                                sp.wait_ge(s_yst[k % 2], 16 * (2 * gi(h, g) + k // 2))
                            for i in range(2):
                                sp.dma_start(fc[:, k % 2, i, :], fac[i][bass.ds(h * KH + k, 1), :, g * BANK:(g + 1) * BANK].rearrange("a p t -> p (a t)")).then_inc(s_fc[k % 2], 16)
                        if k:
                            sp.wait_ge(s_y, 2 * (KH * gi(h, g) + k))
                            sp.dma_start(y_dst[bass.ds(h * KH + k - 1, 1), :, g * BANK:(g + 1) * BANK].rearrange("a p t -> p (a t)"), fc[:, (k - 1) % 2, 0, :]).then_inc(s_yst[(k - 1) % 2], 16)

                load_q(0, 0)
                load_kv(sp, 0, 0)
                load_kv(sp, 0, 1)
                load_nm(0)
                for j in (2, 3):
                    sp.wait_ge(s_klo, j - 1)
                    load_kv(sp, 0, j)

                def step(h, first, last):
                    for j in (KH, KH + 1):
                        sp.wait_ge(s_klo, KH * h + j - 1)
                        load_kv(sp, h, j)
                    sp.wait_ge(s_qlo, NG * h + 1)
                    load_q(h, 1)
                    if not first:
                        factors(h - 1, 1)
                    if not last:
                        sp.wait_ge(s_qlo, NG * h + 2)
                        load_q(h + 1, 0)
                    factors(h, 0)
                    if not last:
                        sp.wait_ge(s_e, NG * (h + 1) * NS)
                        load_nm(h + 1)
                        sp.wait_ge(s_vt, NV * (h + 1))
                        for j in range(KH):
                            if j > 1:
                                sp.wait_ge(s_klo, KH * (h + 1) + j - 1)
                            load_kv(sp, h + 1, j)
                over(sp, HEADS, step)
                factors(HEADS - 1, 1)
                for i in range(2):
                    sp.wait_ge(s_yst[i], 16 * (KH // 2) * NG * HEADS)

            def each_group(run):
                def step(h, first, last):
                    for g in range(NG):
                        run(h, g, first and g == 0, last and g == NG - 1, first, last)
                return step

            @block.tensor
            def _(pe):
                def turn_hn(h, g, k):
                    pe.wait_ge(s_hn, JT * (gi(h, g) + 1))
                    n = KH * gi(h, g) + k
                    if k > 1 or not isinstance(h, int) or h or g:
                        pe.wait_ge(s_y, 2 * n - 3)
                    for j in range(JT):
                        tr = nc.tensor.transpose(ps[:, HB + k % 2, j * P:(j + 1) * P], hs[:, j, k * P:(k + 1) * P], ident[:, :])
                    tr.then_inc(s_ht, 1)

                def run(h, g, first, last, first_head, last_head):
                    n = gi(h, g)
                    pieces = subs(g)
                    order = [pieces[0][0], pieces[2][0]] + [x[0] for x in pieces[4:]]
                    pe.wait_ge(s_qlo, n + 1)
                    if g == 0:
                        pe.wait_ge(s_klo, KH * (h + 1))
                    for c, t in enumerate(order):
                        if c >= SB:
                            pe.wait_ge(s_p, NS * n + pieces_to(c - SB))
                        elif not first:
                            pe.wait_ge(s_p, NS * n)
                        for k in range(KH):
                            mm = mm3(nc, ps[:, c % SB, :], k_hi[:, k, t * P:(t + 1) * P], k_lo[:, k, t * P:(t + 1) * P], q_hi[:, k, :], q_lo[:, k, :], k == 0, k == KH - 1)
                        mm.then_inc(s_s, 1)
                        if c in TAT and not first:
                            turn_hn(h if g else h - 1, 1 - g, TAT.index(c))
                        if g == 0:
                            for v in VAT.get(c, ()):
                                k, (t0, nt) = v // 3, VCH[v % 3]
                                if v % 3 == 0:
                                    kr_uses = 4 * h + (KH + k) // 2 + 1
                                    pe.wait_ge(s_kr[k % 2], 16 * kr_uses)
                                if v >= VR:
                                    pe.wait_ge(s_vlo, NV * h + v - VR + 1)
                                elif v == 0 and not first_head:
                                    pe.wait_ge(s_pvf, JT * n)
                                    pe.wait_ge(s_pvb, JT * n)
                                for i in range(nt):
                                    tr = nc.tensor.transpose(ps[:, VB + v % VR, i * P:(i + 1) * P], kr[:, k % 2, (t0 + i) * P:(t0 + i + 1) * P], ident[:, :])
                                tr.then_inc(s_vt, 1)
                    where = {(t, d): off for t, d, off in pieces}
                    for j in range(JT):
                        J = JT * g + j
                        for d in range(2):
                            keys = [(t, where[(t, d)] + j * P) for t in (NTX, NTX + 1)]
                            for t, dd, off in pieces[4:]:
                                if dd is None:
                                    if t == J:
                                        keys.append((t, off + (j * P if d == 0 else BANK)))
                                    elif (t < J) == (d == 0):
                                        keys.append((t, off + j * P))
                                elif dd == d:
                                    keys.append((t, off + j * P))
                            b = PB + 2 * (j % 2) + d
                            if not (first and j < 2):
                                pe.wait_ge(s_pvf if d == 0 else s_pvb, JT * n + j - 1)
                            if j == 0 and d == 0 and not first:
                                pe.wait_ge(s_y, 2 * KH * n - 1)
                            for i, (t, off) in enumerate(keys):
                                if j == 0:
                                    piece = [x[0] for x in pieces].index(t) + (d if t >= NTX else 0)
                                    pe.wait_ge(s_plo, NS * n + piece + 1)
                                    if d == 0 and i == 0 and g == 0:
                                        pe.wait_ge(s_vlo, NV * (h + 1))
                                mm = mm3(nc, ps[:, b, :], p_hi[:, off:off + P], p_lo[:, off:off + P], v_hi[:, t, :], v_lo[:, t, :], i == 0, i == len(keys) - 1)
                            mm.then_inc(s_pv, 1)
                        if j == 0:
                            pe.wait_ge(s_acc, NS * (n + 1))
                            for d in range(2):
                                for jj in range(JT):
                                    mm = nc.tensor.matmul(ps[:, HB, d * JT + jj:d * JT + jj + 1], acc[:, d, jj * P:(jj + 1) * P], one[:, :],
                                                          start=(d == 0 and jj == 0), stop=(d == 1 and jj == JT - 1), skip_group_check=True)
                            mm.then_inc(s_den, 1)

                pe.wait_ge(s_c, 4)
                over(pe, HEADS, each_group(run), last_differs=False)
                for k in range(KH):
                    turn_hn(HEADS - 1, 1, k)

            @block.scalar
            def _(act):
                def split_q(n):
                    act.wait_ge(s_q, 16 * KH * (n + 1))
                    nc.scalar.activation(q_hi[:, :, :], qr[:, :, :], ACT.Copy).then_inc(s_qhi, 1)

                def split_k(h, k):
                    act.wait_ge(s_kr[k % 2], 16 * (4 * h + k // 2 + 1))
                    nc.scalar.activation(k_hi[:, k, :], kr[:, k % 2, :], ACT.Copy).then_inc(s_khi, 1)

                split_q(0)
                for k in range(KH):
                    split_k(0, k)

                def weights(h, g, i, first):
                    n = gi(h, g)
                    t, d, off = subs(g)[i]
                    if i == 0:
                        act.wait_ge(s_nm, 32 * (h + 1))
                        act.wait_ge(s_hc, h + 1)
                    if not (first and i < 2):
                        act.wait_ge(s_p, NS * n + i - 1)
                    a = lambda dd: hc[:, t, dd:dd + 1]
                    q0 = g * BANK
                    if d is not None:
                        nc.scalar.activation(e[:, i % 2, 0:BANK], nm[:, d, q0:q0 + BANK], ACT.Exp, bias=a(d)).then_inc(s_e, 1)
                        return
                    j = t - JT * g
                    if j > 0:
                        nc.scalar.activation(e[:, i % 2, 0:j * P], nm[:, 1, q0:q0 + j * P], ACT.Exp, bias=a(1))
                    if j < JT - 1:
                        nc.scalar.activation(e[:, i % 2, (j + 1) * P:BANK], nm[:, 0, q0 + (j + 1) * P:q0 + BANK], ACT.Exp, bias=a(0))
                    act.wait_ge(s_arg, 2 * (JT * n + j + 1))
                    nc.scalar.activation(e[:, i % 2, j * P:(j + 1) * P], e[:, i % 2, j * P:(j + 1) * P], ACT.Exp)
                    nc.scalar.activation(e[:, i % 2, BANK:DIAG], e[:, i % 2, BANK:DIAG], ACT.Exp).then_inc(s_e, 1)

                weights(0, 0, 0, True)

                def run(h, g, first, last, first_head, last_head):
                    n = gi(h, g)
                    pieces = subs(g)
                    for i in range(NS):
                        if i + 1 < NS:
                            weights(h, g, i + 1, first)
                        t, d, off = pieces[i]
                        w = FULL if d is not None else DIAG
                        act.wait_ge(s_p, NS * n + i + 1)
                        if not first and i == 0:
                            act.wait_ge(s_pv, 2 * JT * n)
                        nc.scalar.activation(p_hi[:, off:off + w], pr[:, i % 2, 0:w], ACT.Copy).then_inc(s_phi, 1)
                        c, end = chunk_of(i)
                        if g == 0 and end:
                            for v in VAT.get(c, ()):
                                k, (t0, nt) = v // 3, VCH[v % 3]
                                act.wait_ge(s_vt, NV * h + v + 1)
                                if v == 0 and not first_head:
                                    act.wait_ge(s_pv, 2 * JT * n)
                                nc.scalar.activation(v_hi[:, t0:t0 + nt, k * P:(k + 1) * P], ps[:, VB + v % VR, 0:nt * P].rearrange("p (t e) -> p t e", e=P), ACT.Copy).then_inc(s_vhi, 1)
                                if v in (2, 5):
                                    load_kv(act, h, KH + 2 + v // 3)
                    for j in range(JT):
                        if j == 0:
                            if not last:
                                act.wait_ge(s_s, NC_ * (n + 1))
                                split_q(n + 1)
                            act.wait_ge(s_nrm, 3 * (n + 1))
                        if g == 1 and not last_head:
                            split_k(h + 1, j)
                        act.wait_ge(s_pv, 2 * (JT * n + j) + 1)
                        if not first:
                            act.wait_ge(s_ht, KH * n)
                        nc.scalar.activation(hs[:, j, :], ps[:, PB + 2 * (j % 2), :], ACT.Copy, scale=rn[:, 0, j:j + 1]).then_inc(s_pvf, 1)
                    if not last:
                        weights(h + g, 1 - g, 0, False)
                    act.wait_ge(s_ln, 5 * n + 1)
                    nc.scalar.activation(rstd[:, :], tmp4[:, :], ACT.Ln).then_inc(s_st, 1)
                    act.wait_ge(s_st, 2 * n + 1)
                    nc.scalar.activation(rstd[:, :], rstd[:, :], ACT.Exp, scale=-0.5).then_inc(s_st, 1)

                over(act, HEADS, each_group(run))

            @block.gpsimd
            def _(pool):
                nc.gpsimd.memset(one[:, :], 1.0).then_inc(s_c, 1)
                nc.gpsimd.memset(mask[:, :, :], 0.0).then_inc(s_c, 1)
                pool.wait_ge(s_c, 2)
                nc.gpsimd.affine_select(out=mask[:, 0, :], in_=mask[:, 0, :], compare_op=ALU.is_ge, fill=-1e30, base=0,
                                        pattern=[[1, P]], channel_multiplier=-1).then_inc(s_c, 1)
                nc.gpsimd.affine_select(out=mask[:, 1, :], in_=mask[:, 1, :], compare_op=ALU.is_ge, fill=-1e30, base=0,
                                        pattern=[[-1, P]], channel_multiplier=1).then_inc(s_c, 1)

                def run(h, g, first, last, first_head, last_head):
                    n = gi(h, g)
                    pool.wait_ge(s_az, n + 1)
                    for i, (t, d, off) in enumerate(subs(g)):
                        pool.wait_ge(s_p, NS * n + i + 1)
                        if i:
                            pool.wait_ge(s_acc, NS * n + i)
                        def add(dd, a, b, x):
                            return nc.gpsimd.tensor_tensor(acc[:, dd, a:b], acc[:, dd, a:b], pr[:, i % 2, x:x + b - a], ALU.add)
                        if d is not None:
                            add(d, 0, BANK, 0).then_inc(s_acc, 1)
                            continue
                        j = t - JT * g
                        if j > 0:
                            add(1, 0, j * P, 0)
                        add(0, j * P, BANK, j * P)
                        add(1, j * P, (j + 1) * P, BANK).then_inc(s_acc, 1)
                over(pool, HEADS, each_group(run), last_differs=False)

            @block.vector
            def _(dve):
                def split_q(n):
                    dve.wait_ge(s_qhi, n + 1)
                    nc.vector.tensor_tensor(q_lo[:, :, :], qr[:, :, :], q_hi[:, :, :].bitcast(F32), ALU.subtract).then_inc(s_qlo, 1)

                def split_k(h, k):
                    dve.wait_ge(s_khi, KH * h + k + 1)
                    nc.vector.tensor_tensor(k_lo[:, k, :], kr[:, k % 2, :], k_hi[:, k, :].bitcast(F32), ALU.subtract).then_inc(s_klo, 1)

                def head_cols(h):
                    nc.vector.tensor_copy(hc[:, :, :], cols[:, :, :, bass.ds(h, 1)].rearrange("p t d o -> p t (d o)")).then_inc(s_hc, 1)

                dve.wait_ge(s_c, 4)
                head_cols(0)
                nc.vector.memset(acc[:, :, :], 0.0).then_inc(s_az, 1)
                dve.wait_ge(s_hc, 1)
                split_q(0)
                for k in range(KH):
                    split_k(0, k)

                def finish(h, g, k):
                    n = KH * gi(h, g) + k
                    dve.wait_ge(s_ht, n + 1)
                    dve.wait_ge(s_fc[k % 2], 32 * (2 * gi(h, g) + k // 2 + 1))
                    yt = fc[:, k % 2, 0, :]
                    nc.vector.tensor_tensor(yt, ps[:, HB + k % 2, :], yt, ALU.mult).then_inc(s_y, 1)
                    dve.wait_ge(s_y, 2 * n + 1)
                    nc.vector.tensor_tensor(yt, yt, fc[:, k % 2, 1, :], ALU.add).then_inc(s_y, 1)

                def run(h, g, first, last, first_head, last_head):
                    n = gi(h, g)
                    pieces = subs(g)

                    def args(i):
                        t, d, off = pieces[i]
                        if d is not None:
                            return
                        j = t - JT * g
                        if i == NS - JT:
                            dve.wait_ge(s_nm, 32 * (h + 1))
                        dve.wait_ge(s_p, NS * n + i - 1)
                        for dd, c0 in ((0, j * P), (1, BANK)):
                            nc.vector.scalar_tensor_tensor(e[:, i % 2, c0:c0 + P], nm[:, dd, t * P:(t + 1) * P], hc[:, t, dd:dd + 1],
                                                           mask[:, dd, :], ALU.add, ALU.add).then_inc(s_arg, 1)

                    def low(i):
                        t, d, off = pieces[i]
                        w = FULL if d is not None else DIAG
                        dve.wait_ge(s_phi, NS * n + i + 1)
                        nc.vector.tensor_tensor(p_lo[:, off:off + w], pr[:, i % 2, 0:w], p_hi[:, off:off + w].bitcast(F32), ALU.subtract).then_inc(s_plo, 1)

                    def low_v(c):
                        if g == 0:
                            for v in VAT.get(c, ()):
                                k, (t0, nt) = v // 3, VCH[v % 3]
                                dve.wait_ge(s_vhi, NV * h + v + 1)
                                o = (slice(None), slice(t0, t0 + nt), slice(k * P, (k + 1) * P))
                                nc.vector.tensor_tensor(v_lo[o], ps[:, VB + v % VR, 0:nt * P].rearrange("p (t e) -> p t e", e=P), v_hi[o].bitcast(F32), ALU.subtract).then_inc(s_vlo, 1)

                    for i in range(NS):
                        c, end = chunk_of(i)
                        if i + 1 < NS:
                            args(i + 1)
                        dve.wait_ge(s_e, NS * n + i + 1)
                        dve.wait_ge(s_s, NC_ * n + c + 1)
                        if not (first and i < 2):
                            dve.wait_ge(s_acc, NS * n + i - 1)
                            dve.wait_ge(s_plo, NS * n + i - 1)
                        t, d, off = pieces[i]
                        p = nc.vector.tensor_tensor(pr[:, i % 2, 0:BANK], ps[:, c % SB, :], e[:, i % 2, 0:BANK], ALU.mult)
                        if d is None:
                            j = t - JT * g
                            p = nc.vector.tensor_tensor(pr[:, i % 2, BANK:DIAG], ps[:, c % SB, j * P:(j + 1) * P], e[:, i % 2, BANK:DIAG], ALU.mult)
                        p.then_inc(s_p, 1)
                        if i:
                            low(i - 1)
                            cc, ee = chunk_of(i - 1)
                            if cc in TAT and ee and not first:
                                pg = (h if g else h - 1, 1 - g)
                                finish(*pg, TAT.index(cc))
                        if end:
                            low_v(c)
                    low(NS - 1)
                    dve.wait_ge(s_den, n + 1)
                    den = ps[:, HB, 0:2 * JT].rearrange("p (d j) -> p d j", d=2)
                    em_g = em[:, JT * g:JT * (g + 1), :, bass.ds(h, 1)].rearrange("p j d o -> p d (j o)")
                    nc.vector.scalar_tensor_tensor(rn[:, :, :], den, -1.0, em_g, ALU.mult, ALU.max).then_inc(s_nrm, 1)
                    dve.wait_ge(s_nrm, 3 * n + 1)
                    nc.vector.tensor_tensor(rn[:, :, :], den, rn[:, :, :], ALU.max).then_inc(s_nrm, 1)
                    dve.wait_ge(s_nrm, 3 * n + 2)
                    nc.vector.reciprocal(rn[:, :, :], rn[:, :, :]).then_inc(s_nrm, 1)
                    if not last:
                        nc.vector.memset(acc[:, :, :], 0.0).then_inc(s_az, 1)
                        split_q(n + 1)
                    if g == 1 and not last_head:
                        head_cols(h + 1)
                    for j in range(JT):
                        if g == 1 and not last_head:
                            split_k(h + 1, j)
                        m = JT * n + j
                        dve.wait_ge(s_pvf, m + 1)
                        dve.wait_ge(s_pv, 2 * (m + 1))
                        dve.wait_ge(s_nrm, 3 * (n + 1))
                        nc.vector.scalar_tensor_tensor(hs[:, j, :], ps[:, PB + 1 + 2 * (j % 2), :], rn[:, 1, j:j + 1], hs[:, j, :], ALU.mult, ALU.add).then_inc(s_pvb, 1)
                        dve.wait_ge(s_pvb, m + 1)
                        nc.vector.bn_stats(st6[:, j, :], hs[:, j, :]).then_inc(s_hs2, 1)
                    dve.wait_ge(s_hs2, JT * (n + 1))
                    nc.vector.memset(tmp4[:, :], EPS).then_inc(s_hs3, 1)
                    for j in range(JT):
                        nc.vector.bn_aggr(mv[:, j, :], st6[:, j, :]).then_inc(s_hs3, 1)
                    dve.wait_ge(s_hs3, (JT + 1) * (n + 1))
                    nc.vector.tensor_tensor(tmp4[:, :], tmp4[:, :], mv[:, :, 1], ALU.add).then_inc(s_ln, 1)
                    dve.wait_ge(s_st, 2 * (n + 1))
                    dve.wait_ge(s_ln, 5 * n + 1)
                    nc.vector.tensor_tensor(tmp4[:, :], tmp4[:, :], rstd[:, :], ALU.mult).then_inc(s_ln, 1)
                    dve.wait_ge(s_ln, 5 * n + 2)
                    nc.vector.tensor_tensor(tmp4[:, :], tmp4[:, :], rstd[:, :], ALU.mult).then_inc(s_ln, 1)
                    dve.wait_ge(s_ln, 5 * n + 3)
                    nc.vector.tensor_scalar(tmp4[:, :], tmp4[:, :], -0.5, 1.5, ALU.mult, ALU.add).then_inc(s_ln, 1)
                    dve.wait_ge(s_ln, 5 * n + 4)
                    nc.vector.tensor_tensor(rstd[:, :], rstd[:, :], tmp4[:, :], ALU.mult).then_inc(s_ln, 1)
                    dve.wait_ge(s_ln, 5 * n + 5)
                    for j in range(JT):
                        nc.vector.tensor_scalar(hs[:, j, :], hs[:, j, :], mv[:, j, 0:1], rstd[:, j:j + 1], ALU.subtract, ALU.mult).then_inc(s_hn, 1)

                over(dve, HEADS, each_group(run))
                for k in range(KH):
                    finish(HEADS - 1, 1, k)


def out_phase(nc, sem, keep, scr, io, layer):
    ps = keep["ps"]
    last_layer = layer == 1
    n_tiles = NTX if last_layer else NT
    pairs = n_tiles // 2
    WR = 3
    y_src = scr["yT"].rearrange("(k p) t -> p k t", p=P)
    x_in = (io["x"][0], io["ctx"][0]) if not last_layer else (scr["x1"], None)
    dst = io["out"][0] if last_layer else scr["x1"]
    w_src = io["m_w_out" if last_layer else "conv_w_out"][0].rearrange("(k p) n -> k p n", p=P)
    H = D // BANK
    LAG = 3
    with ExitStack() as st:
        sb = lambda n, s, d=F32: st.enter_context(nc.sbuf_tensor(f"c{layer}_{n}", s, d))
        w_hi, w_lo = sb("w_hi", [P, KI, D], F32R), sb("w_lo", [P, KI, D], F32R)
        wr = sb("wr", [P, WR, D])
        yr, y_hi, y_lo = sb("yr", [P, KI, P]), sb("y_hi", [P, 2, KI, P], F32R), sb("y_lo", [P, 2, KI, P], F32R)
        x = sb("x", [P, 2, D])
        bc = sb("bc", [P, 2, D])
        o = sb("o", [P, 1, D])
        ss, ms, rt = sb("ss", [P, 1]), sb("ms", [P, 1]), sb("rt", [P, 1])
        s_w = [sem(f"c{layer}_w_loaded{i}") for i in range(WR)]
        s_x = [sem(f"c{layer}_x_loaded{i}") for i in range(2)]
        s_bc, s_y, s_whi, s_wlo, s_yhi, s_ylo, s_mm, s_ep, s_fin, s_sq, s_st, s_fn = (sem(f"c{layer}_{n}") for n in (
            "bc_loaded", "y_loaded", "w_hi_made", "w_lo_made", "y_hi_made", "y_lo_made", "chunk_done", "gated", "tile_made", "squared", "stored", "final_step"))
        with nc.Block() as block:
            @block.sync
            def _(sp):
                def load_y(t):
                    sp.dma_start(yr[:, :, :], y_src[:, :, bass.ds(t * P, P)]).then_inc(s_y, 16)

                def load_x(t, par, ctx):
                    src = x_in[1 if ctx else 0]
                    sp.dma_start(x[:, par, :], src[bass.ds((t - NTX if ctx else t) * P, P), :]).then_inc(s_x[par], 16)

                load_y(0)
                for k in range(KI):
                    if k >= WR:
                        sp.wait_ge(s_wlo, k - WR + 1)
                    sp.dma_start(wr[:, k % WR, :], w_src[k]).then_inc(s_w[k % WR], 16)
                    if k == 1:
                        sp.wait_ge(s_ylo, 1)
                        load_y(1)
                sp.dma_start(bc[:, 0, :], scr["gates"][layer][0:1, :].to_broadcast([P, D])).then_inc(s_bc, 16)
                second = io["final_g"].rearrange("(o d) -> o d", o=1) if last_layer else scr["gates"][layer][1:2, :]
                sp.dma_start(bc[:, 1, :], second.to_broadcast([P, D])).then_inc(s_bc, 16)
                load_x(0, 0, False)
                load_x(1, 1, False)

                def pair(i, more, ctx_next):
                    for par in range(2):
                        t = 2 * i + par
                        if more:
                            sp.wait_ge(s_ylo, t + 2)
                            load_y(t + 2)
                        sp.wait_ge(s_fin, t + 1)
                        sp.dma_start(dst[bass.ds(t * P, P), :], o[:, 0, :]).then_inc(s_st, 16)
                        if more:
                            load_x(t + 2, par, ctx_next)
                loop = pairs - 1 if last_layer else pairs - 2
                with sp.Fori(0, loop) as i:
                    pair(i, True, False)
                if not last_layer:
                    pair(pairs - 2, True, True)
                pair(pairs - 1, False, False)
                sp.wait_ge(s_st, 16 * n_tiles)

            @block.tensor
            def _(pe):
                def product(par, half, k):
                    cols = slice(half * BANK, (half + 1) * BANK)
                    mm = mm3(nc, ps[:, 2 * par + half, :], y_hi[:, par, k], y_lo[:, par, k], w_hi[:, k, cols], w_lo[:, k, cols], k == 0, k == KI - 1)
                    if k == KI - 1:
                        mm.then_inc(s_mm, 1)

                for at in range(KI + LAG):
                    for par in range(2):
                        k = at - LAG * par
                        if 0 <= k < KI:
                            if k == 0:
                                pe.wait_ge(s_ylo, par + 1)
                            if par == 0:
                                pe.wait_ge(s_wlo, k + 1)
                            for half in range(H):
                                product(par, half, k)
                with pe.Fori(1, pairs) as i:
                    for par in range(2):
                        t = 2 * i + par
                        pe.wait_ge(s_ylo, t + 1)
                        for half in range(H):
                            pe.wait_ge(s_ep, H * (t - 2) + half + 1)
                            for k in range(KI):
                                product(par, half, k)

            @block.scalar
            def _(act):
                def split(t, par):
                    act.wait_ge(s_y, 16 * (t + 1))
                    nc.scalar.activation(y_hi[:, par], yr[:, :, :], ACT.Copy).then_inc(s_yhi, 1)

                split(0, 0)
                for k in range(KI):
                    act.wait_ge(s_w[k % WR], 16 * (k // WR + 1))
                    nc.scalar.activation(w_hi[:, k, :], wr[:, k % WR, :], ACT.Copy).then_inc(s_whi, 1)
                    if k == LAG - 1:
                        split(1, 1)

                def pair(i, more):
                    for par in range(2):
                        t = 2 * i + par
                        if more:
                            act.wait_ge(s_mm, H * (t + 1))
                            split(t + 2, par)
                        if last_layer:
                            act.wait_ge(s_fn, 5 * t + 1)
                            nc.scalar.activation(o[:, 0, :], x[:, par, :], ACT.Square, accum_out=ss[:, :]).then_inc(s_sq, 1)
                            act.wait_ge(s_fn, 5 * t + 2)
                            nc.scalar.activation(rt[:, :], ms[:, :], ACT.Sqrt).then_inc(s_sq, 1)
                with act.Fori(0, pairs - 1) as i:
                    pair(i, True)
                if last_layer:
                    pair(pairs - 1, False)

            @block.vector
            def _(dve):
                def split(t, par):
                    dve.wait_ge(s_yhi, t + 1)
                    nc.vector.tensor_tensor(y_lo[:, par], yr[:, :, :], y_hi[:, par].bitcast(F32), ALU.subtract).then_inc(s_ylo, 1)

                split(0, 0)
                for k in range(KI):
                    dve.wait_ge(s_whi, k + 1)
                    nc.vector.tensor_tensor(w_lo[:, k, :], wr[:, k % WR, :], w_hi[:, k, :].bitcast(F32), ALU.subtract).then_inc(s_wlo, 1)
                    if k == LAG - 1:
                        split(1, 1)
                dve.wait_ge(s_bc, 32)

                def pair(i, first, more, ctx):
                    for par in range(2):
                        t = 2 * i + par
                        dve.wait_ge(s_x[par], 16 * (i + 1))
                        if not (first and par == 0):
                            dve.wait_ge(s_st, 16 * t)
                        for half in range(H):
                            cols = slice(half * BANK, (half + 1) * BANK)
                            dve.wait_ge(s_mm, H * t + half + 1)
                            nc.vector.tensor_tensor(o[:, 0, cols], ps[:, 2 * par + half, :], bc[:, 1 if ctx else 0, cols], ALU.mult).then_inc(s_ep, 1)
                        if more:
                            split(t + 2, par)
                        dve.wait_ge(s_ep, H * (t + 1))
                        if not last_layer:
                            nc.vector.tensor_tensor(o[:, 0, :], o[:, 0, :], x[:, par, :], ALU.add).then_inc(s_fin, 1)
                            continue
                        nc.vector.tensor_tensor(x[:, par, :], o[:, 0, :], x[:, par, :], ALU.add).then_inc(s_fn, 1)
                        dve.wait_ge(s_sq, 2 * t + 1)
                        nc.vector.tensor_scalar(ms[:, :], ss[:, :], 1.0 / D, EPS, ALU.mult, ALU.add).then_inc(s_fn, 1)
                        dve.wait_ge(s_sq, 2 * t + 2)
                        nc.vector.reciprocal(ms[:, :], rt[:, :]).then_inc(s_fn, 2)
                        dve.wait_ge(s_fn, 5 * t + 4)
                        nc.vector.scalar_tensor_tensor(o[:, 0, :], x[:, par, :], ms[:, :], bc[:, 1, :], ALU.mult, ALU.mult).then_inc(s_fin, 1)
                        nc.vector.tensor_copy(rt[:, :], ms[:, :]).then_inc(s_fn, 1)
                pair(0, True, True, False)
                with dve.Fori(1, pairs - 1) as i:
                    pair(i, False, True, False)
                pair(pairs - 1, False, False, not last_layer)


INS = ["x", "c", "ctx", "c_ctx", "norm_g", "mod_w", "mod_b", "conv_w_in", "conv_w", "conv_w_out", "m_w_in", "m_conv_w",
       "m_wq", "m_wk", "m_wv", "m_w_gate", "m_b_gate", "m_norm_g", "m_skip", "m_w_out", "final_g"]


def kernel(**inputs):
    import numpy as np
    import concourse.bacc as bacc
    from concourse.bass_utils import run_bass_kernel_spmd

    nc = bacc.Bacc("TRN2", target_bir_lowering=False, num_devices=1)
    arrays, io = {}, {}
    for name in INS:
        a = np.ascontiguousarray(inputs[name])
        arrays[f"in_{name}"] = a
        io[name] = nc.dram_tensor(f"in_{name}", a.shape, mybir.dt.from_np(a.dtype), kind="ExternalInput").ap()
    io["out"] = nc.dram_tensor("out_0", (1, TX, D), F32, kind="ExternalOutput").ap()
    build(nc, io)
    r = run_bass_kernel_spmd(nc, [arrays], core_ids=[0])
    return r.results[0]["out_0"]
```

```python
import concourse.bass as bass
from concourse import mybir
from contextlib import ExitStack

D = 1024
DI = 2048
TX = 1024
TC = 256
TT = TX + TC
HEADS = 4
DH = DI // HEADS
ROW = 64
EPS = 1e-6
P = 128
KD = D // P
KI = DI // P
KH = DH // P
NT = TT // P
NTX = TX // P
BANK = 512
GROUPS = [(0, 512), (512, 512), (1024, 256)]

F32 = mybir.dt.float32
F32R = mybir.dt.float32r
ALU = mybir.AluOpType
ACT = mybir.ActivationFunctionType

COL_CONV, COL_MCONV, COL_NORM, COL_SKIP, COL_G, COL_C = 0, 48, 96, 112, 128, 144


def over(eng, n, step, last_differs=True):
    step(0, True, False)
    end = n - 1 if last_differs else n
    with eng.Fori(1, end) as i:
        step(i, False, False)
    if last_differs:
        step(n - 1, False, True)


def mm3(nc, out, w_hi, w_lo, x_hi, x_lo, first, last):
    nc.tensor.matmul(out, w_lo, x_hi, start=first, stop=False)
    nc.tensor.matmul(out, w_hi, x_lo, start=False, stop=False)
    return nc.tensor.matmul(out, w_hi, x_hi, start=False, stop=last)


def build(nc, io):
    es = ExitStack()
    with es:
        held = []

        def sem(name):
            held.append(nc.alloc_semaphore(name=name))
            return held[-1]

        def end_phase():
            nc.clear_and_free_semaphores(held)
            held.clear()
            nc.all_engine_barrier()

        def dram(name, shape):
            return nc.dram_tensor(name, shape, F32, kind="Internal").ap()

        keep = {
            "ps": es.enter_context(nc.psum_tensor("ps", [P, 8, BANK], F32)),
            "ident": es.enter_context(nc.sbuf_tensor("ident", [P, P], F32)),
            "par": es.enter_context(nc.sbuf_tensor("par", [P, 160], F32)),
            "mod": es.enter_context(nc.sbuf_tensor("mod", [P, 2, 2, 2, KD], F32)),
        }
        scr = {
            "gates": dram("gate_rows", (2, 2, D)),
            "yT": dram("yT", (DI, TT)),
            "x1": dram("x1", (TT, D)),
            "uT": dram("uT", (DI, TT)),
            "ucT": dram("ucT", (DI, TT)),
            "qkvT": dram("qkvT", (3, DI, TT)),
            "ymul": dram("ymul", (DI, TX)),
            "yadd": dram("yadd", (DI, TX)),
            "nmrow": dram("nmrow", (2, HEADS, TX)),
        }
        modulation(nc, sem, keep, scr, io)
        end_phase()
        for layer in range(2):
            with ExitStack() as hold:
                h_hi = hold.enter_context(nc.sbuf_tensor(f"h{layer}_hi", [P, KD, TT], F32R))
                h_lo = hold.enter_context(nc.sbuf_tensor(f"h{layer}_lo", [P, KD, TT], F32R))
                norm_phase(nc, sem, keep, scr, io, layer, h_hi, h_lo)
                end_phase()
                if layer == 0:
                    conv_in_phase(nc, sem, keep, scr, io, h_hi, h_lo)
                else:
                    lstm_in_phase(nc, sem, keep, scr, io, h_hi, h_lo)
                end_phase()
            if layer == 1:
                with ExitStack() as hold:
                    bg = hold.enter_context(nc.sbuf_tensor("gate_bias", [P, 1], F32))
                    with ExitStack() as inner:
                        early = {n: inner.enter_context(nc.sbuf_tensor(n, [P, w], F32))
                                 for n, w in (("gate_sums", TT), ("ones", TT), ("a_rows", TT), ("av", TT), ("fold", P))}
                        qkv_phase(nc, sem, keep, scr, io, early, bg)
                        end_phase()
                    attention_phase(nc, sem, keep, scr, io, early, bg)
                    end_phase()
            out_phase(nc, sem, keep, scr, io, layer)
            end_phase()


def modulation(nc, sem, keep, scr, io):
    ps, ident, par, mod = keep["ps"], keep["ident"], keep["par"], keep["mod"]
    NCH = 3 * D // BANK
    RING = 3
    with ExitStack() as st:
        sb = lambda n, s, d=F32: st.enter_context(nc.sbuf_tensor(n, s, d))
        rows1, rows2 = sb("par_rows1", [P, P]), sb("par_rows2", [32, P])
        sg, sc = sb("sc_sig", [P, 16]), sb("sc", [P, 16])
        w = sb("modw", [P, RING, KD, BANK])
        brow, mrow = sb("mod_brow", [2, 2, 3 * D]), sb("mod_row", [2, 2, 3 * D])
        s_id, s_par, s_tp, s_cp, s_sg, s_sc = (sem(n) for n in ("id_made", "par_loaded", "par_turned", "par_copied", "sc_sigmoid", "sc_made"))
        s_w = [sem(f"modw_loaded{i}") for i in range(RING)]
        s_mm, s_row, s_tr, s_col, s_b, s_out = (sem(n) for n in ("mod_product", "mod_row_made", "mod_turned", "mod_col_made", "modb_loaded", "gate_stored"))

        def wsrc(l, n):
            return io["mod_w"][l].rearrange("(k p) n -> p k n", p=P)[:, :, n * BANK:(n + 1) * BANK]

        with nc.Block() as block:
            @block.sync
            def _(sp):
                for src, r0, n in ((io["conv_w"], 0, 48), (io["m_conv_w"], 48, 48)):
                    sp.dma_start(rows1[r0:r0 + n, :], src[0].rearrange("j (f p) -> (j f) p", p=P)).then_inc(s_par, 16)
                for src, r0 in ((io["m_norm_g"], 96), (io["m_skip"], 112)):
                    sp.dma_start(rows1[r0:r0 + 16, :], src[0].rearrange("(f p) -> f p", p=P)).then_inc(s_par, 16)
                sp.dma_start(rows2[0:16, :], io["norm_g"].rearrange("l (k p) -> (l k) p", p=P)).then_inc(s_par, 16)
                sp.dma_start(rows2[16:24, :], io["c"][0].rearrange("(k p) -> k p", p=P)).then_inc(s_par, 16)
                sp.dma_start(rows2[24:32, :], io["c_ctx"].rearrange("(k p) -> k p", p=P)).then_inc(s_par, 16)
                for r in range(2):
                    sp.dma_start(brow[r:r + 1, :, :], io["mod_b"].rearrange("(o l) n -> o l n", o=1)).then_inc(s_b, 16)
                for i in range(2 * NCH):
                    if i >= RING:
                        sp.wait_ge(s_mm, i - RING + 1)
                    sp.dma_start(w[:, i % RING], wsrc(i // NCH, i % NCH)).then_inc(s_w[i % RING], 16)
                for l in range(2):
                    sp.wait_ge(s_row, NCH * (l + 1))
                    sp.dma_start(scr["gates"][l], mrow[:, l, 2 * D:3 * D]).then_inc(s_out, 16)
                sp.wait_ge(s_out, 32)

            @block.gpsimd
            def _(pool):
                nc.gpsimd.memset(ident[:, :], 0.0).then_inc(s_id, 1)
                pool.wait_ge(s_id, 1)
                nc.gpsimd.affine_select(out=ident[:, :], in_=ident[:, :], compare_op=ALU.not_equal, fill=1.0, base=0,
                                        pattern=[[-1, P]], channel_multiplier=1).then_inc(s_id, 1)

            @block.tensor
            def _(pe):
                pe.wait_ge(s_id, 2)
                pe.wait_ge(s_par, 16 * 7)
                nc.tensor.transpose(ps[:, 0, 0:P], rows1[:, :], ident[:, :]).then_inc(s_tp, 1)
                nc.tensor.transpose(ps[:, 1, 0:32], rows2[:, :], ident[0:32, 0:32]).then_inc(s_tp, 1)
                pe.wait_ge(s_sc, 1)
                for i in range(2 * NCH):
                    pe.wait_ge(s_w[i % RING], 16 * (i // RING + 1))
                    if i >= 4:
                        pe.wait_ge(s_row, i - 3)
                    for k in range(KD):
                        mm = nc.tensor.matmul(ps[0:2, 2 + i % 4, :], sc[:, k:16:KD], w[:, i % RING, k, :], start=(k == 0), stop=(k == KD - 1))
                    mm.then_inc(s_mm, 1)
                for l in range(2):
                    pe.wait_ge(s_row, NCH * (l + 1))
                    for j in range(2 * KD):
                        tr = nc.tensor.transpose(ps[:, l, 2 * j:2 * j + 2], mrow[:, l, j * P:(j + 1) * P], ident[0:2, 0:2])
                    tr.then_inc(s_tr, 1)

            @block.scalar
            def _(act):
                act.wait_ge(s_tp, 2)
                nc.scalar.activation(par[:, 0:P], ps[:, 0, 0:P], ACT.Copy).then_inc(s_cp, 1)
                nc.scalar.activation(par[:, P:160], ps[:, 1, 0:32], ACT.Copy).then_inc(s_cp, 1)
                act.wait_ge(s_cp, 2)
                nc.scalar.activation(sg[:, :], par[:, COL_C:COL_C + 16], ACT.Sigmoid).then_inc(s_sg, 1)

            @block.vector
            def _(dve):
                dve.wait_ge(s_sg, 1)
                nc.vector.tensor_tensor(sc[:, :], sg[:, :], par[:, COL_C:COL_C + 16], ALU.mult).then_inc(s_sc, 1)
                dve.wait_ge(s_b, 32)
                for i in range(2 * NCH):
                    l, n = i // NCH, i % NCH
                    dve.wait_ge(s_mm, i + 1)
                    nc.vector.tensor_tensor(mrow[:, l, n * BANK:(n + 1) * BANK], ps[0:2, 2 + i % 4, :],
                                            brow[:, l, n * BANK:(n + 1) * BANK], ALU.add).then_inc(s_row, 1)
                for l in range(2):
                    dve.wait_ge(s_tr, l + 1)
                    for s in range(2):
                        g = par[:, COL_G + KD * l:COL_G + KD * (l + 1)]
                        nc.vector.tensor_copy(mod[:, l, 1, s, :], ps[:, l, s:2 * KD:2]).then_inc(s_col, 1)
                        nc.vector.scalar_tensor_tensor(mod[:, l, 0, s, :], ps[:, l, 2 * KD + s:4 * KD:2], 1.0, g, ALU.add, ALU.mult).then_inc(s_col, 1)


def norm_phase(nc, sem, keep, scr, io, layer, h_hi, h_lo):
    ps, ident, mod = keep["ps"], keep["ident"], keep["mod"]
    GT = [(0, 4), (4, 4), (8, 2)]
    if layer == 0:
        tiles = io["x"][0].rearrange("(t p) d -> t p d", p=P), io["ctx"][0].rearrange("(t p) d -> t p d", p=P)
        src = lambda t: tiles[0][t] if t < NTX else tiles[1][t - NTX]
    else:
        tiles = scr["x1"].rearrange("(t p) d -> t p d", p=P)
        src = lambda t: tiles[t]
    with ExitStack() as st:
        sb = lambda n, s, d=F32: st.enter_context(nc.sbuf_tensor(f"n{layer}_{n}", s, d))
        x, xn = sb("x", [P, 4, D]), sb("xn", [P, 2, 4, D])
        junk, ss, rt, rs = sb("junk", [P, D]), sb("ss", [P, NT]), sb("rt", [P, NT]), sb("rs", [P, NT])
        hf = sb("hf", [P, 2, BANK])
        s_x = [sem(f"n{layer}_x_loaded{i}") for i in range(4)]
        s_ss, s_ms, s_rt, s_rs, s_xn, s_tr, s_hf, s_hi, s_lo = (sem(f"n{layer}_{n}") for n in (
            "squared", "mean", "root", "rsqrt", "scaled", "turned", "modulated", "hi_made", "lo_made"))
        with nc.Block() as block:
            @block.sync
            def _(sp):
                for t in range(NT):
                    if t >= 4:
                        sp.wait_ge(s_xn, t - 3)
                    sp.dma_start(x[:, t % 4, :], src(t)).then_inc(s_x[t % 4], 16)

            def chunks():
                n = 0
                for g, (t0, nt) in enumerate(GT):
                    for k in range(KD):
                        yield n, g, t0, nt, k
                        n += 1

            @block.scalar
            def _(act):
                def roots(t):
                    act.wait_ge(s_x[t % 4], 16 * (t // 4 + 1))
                    if t:
                        act.wait_ge(s_ss, t)
                    nc.scalar.activation(junk[:, :], x[:, t % 4, :], ACT.Square, accum_out=ss[:, t:t + 1]).then_inc(s_ss, 1)
                    act.wait_ge(s_ms, t + 1)
                    nc.scalar.activation(rt[:, t:t + 1], rs[:, t:t + 1], ACT.Sqrt).then_inc(s_rt, 1)

                for t in range(4):
                    roots(t)
                for n, g, t0, nt, k in chunks():
                    if k < 4 and t0 + nt + k < min(NT, t0 + nt + 4):
                        roots(t0 + nt + k)
                    s = 0 if g < 2 else 1
                    act.wait_ge(s_tr, n + 1)
                    if n >= 2:
                        act.wait_ge(s_lo, n - 1)
                    nc.scalar.activation(hf[:, n % 2, 0:nt * P], ps[:, n % 4, 0:nt * P], ACT.Identity,
                                         bias=mod[:, layer, 1, s, k:k + 1], scale=mod[:, layer, 0, s, k:k + 1]).then_inc(s_hf, 1)
                    act.wait_ge(s_hf, n + 1)
                    nc.scalar.activation(h_hi[:, k, t0 * P:(t0 + nt) * P], hf[:, n % 2, 0:nt * P], ACT.Copy).then_inc(s_hi, 1)

            @block.vector
            def _(dve):
                def scale(t):
                    dve.wait_ge(s_ss, t + 1)
                    nc.vector.tensor_scalar(rs[:, t:t + 1], ss[:, t:t + 1], 1.0 / D, EPS, ALU.mult, ALU.add).then_inc(s_ms, 1)
                    dve.wait_ge(s_rt, t + 1)
                    nc.vector.reciprocal(ss[:, t:t + 1], rt[:, t:t + 1]).then_inc(s_rs, 1)
                    dve.wait_ge(s_rs, t + 1)
                    if t >= 8:
                        dve.wait_ge(s_tr, KD)
                    nc.vector.tensor_scalar(xn[:, (t // 4) % 2, t % 4, :], x[:, t % 4, :], ss[:, t:t + 1], None, ALU.mult).then_inc(s_xn, 1)

                for t in range(4):
                    scale(t)
                for n, g, t0, nt, k in chunks():
                    if k < 4 and t0 + nt + k < min(NT, t0 + nt + 4):
                        scale(t0 + nt + k)
                    dve.wait_ge(s_hi, n + 1)
                    cols = slice(t0 * P, (t0 + nt) * P)
                    nc.vector.tensor_tensor(h_lo[:, k, cols], hf[:, n % 2, 0:nt * P], h_hi[:, k, cols].bitcast(F32), ALU.subtract).then_inc(s_lo, 1)

            @block.tensor
            def _(pe):
                for n, g, t0, nt, k in chunks():
                    if k == 0:
                        pe.wait_ge(s_xn, t0 + nt)
                    if n >= 4:
                        pe.wait_ge(s_hf, n - 3)
                    for i in range(nt):
                        tr = nc.tensor.transpose(ps[:, n % 4, i * P:(i + 1) * P], xn[:, g % 2, i, k * P:(k + 1) * P], ident[:, :])
                    tr.then_inc(s_tr, 1)


def conv_taps(nc, dve, out, x, par, col0, f, s_done, base):
    tap = lambda j: par[:, bass.ds(col0 + j * KI + f, 1)]
    nc.vector.tensor_scalar(out[:, :], x[:, :], tap(1), None, ALU.mult).then_inc(s_done, 1)
    xr, orow = (a[:, 0:TX].rearrange("p (r c) -> p r c", c=ROW) for a in (x, out))
    dve.wait_ge(s_done, base + 1)
    nc.vector.scalar_tensor_tensor(orow[:, :, 1:], xr[:, :, :-1], tap(0), orow[:, :, 1:], ALU.mult, ALU.add).then_inc(s_done, 1)
    nc.vector.scalar_tensor_tensor(out[:, TX + 1:], x[:, TX:TT - 1], tap(0), out[:, TX + 1:], ALU.mult, ALU.add).then_inc(s_done, 1)
    dve.wait_ge(s_done, base + 3)
    nc.vector.scalar_tensor_tensor(orow[:, :, :-1], xr[:, :, 1:], tap(2), orow[:, :, :-1], ALU.mult, ALU.add).then_inc(s_done, 1)
    nc.vector.scalar_tensor_tensor(out[:, TX:TT - 1], x[:, TX + 1:], tap(2), out[:, TX:TT - 1], ALU.mult, ALU.add).then_inc(s_done, 1)


def conv_in_phase(nc, sem, keep, scr, io, h_hi, h_lo):
    ps, par = keep["ps"], keep["par"]
    UNITS = (1, 2, 3, 0)
    U, G = len(UNITS), len(GROUPS)
    CH = U * G
    R = 6
    w_src = io["conv_w_in"][0].rearrange("(k p) n -> p k n", p=P)
    y_dst = scr["yT"].rearrange("(f p) t -> f p t", p=P)
    with ExitStack() as st:
        sb = lambda n, s, d=F32: st.enter_context(nc.sbuf_tensor(f"a0_{n}", s, d))
        raw, w_hi, w_lo = sb("raw", [P, U, KD, P]), sb("w_hi", [P, U, KD, P], F32R), sb("w_lo", [P, U, KD, P], F32R)
        ev = sb("ev", [P, U, TT])
        sg, cu, cv, y = sb("sg", [P, TT]), sb("cu", [P, TT]), sb("cv", [P, TT]), sb("y", [P, TT])
        s_w = [sem(f"a0_w_loaded{q}") for q in range(U)]
        s_hi, s_lo, s_mm, s_ev, s_sg, s_ew, s_y, s_st = (sem(f"a0_{n}") for n in (
            "w_hi_made", "w_lo_made", "chunk_done", "chunk_read", "sigmoid", "mixed", "y_made", "y_stored"))
        EW = 8
        with nc.Block() as block:
            @block.sync
            def _(sp):
                def load(f, q):
                    sp.dma_start(raw[:, q], w_src[:, :, bass.ds(UNITS[q] * DI + f * P, P)]).then_inc(s_w[q], 16)

                def store(f):
                    sp.wait_ge(s_y, f + 1)
                    sp.dma_start(y_dst[bass.ds(f, 1)].rearrange("a p t -> p (a t)"), y[:, :]).then_inc(s_st, 16)

                for q in range(U):
                    load(0, q)

                def step(f, first, last):
                    nxt = f + 1 if first or last else sp.snap(f + 1)
                    if not last:
                        for q in range(U):
                            if q < U - 2:
                                sp.wait_ge(s_lo, U * f + q + 1)
                            elif q == U - 2:
                                sp.wait_ge(s_lo, U * f + U)
                            load(nxt, q)
                    if not first:
                        store(f - 1)
                over(sp, KI, step)
                store(KI - 1)
                sp.wait_ge(s_st, 16 * KI)

            @block.tensor
            def _(pe):
                def step(f, first, last):
                    for q in range(U):
                        pe.wait_ge(s_lo, U * f + q + 1)
                        for g, (t0, n) in enumerate(GROUPS):
                            c = q * G + g
                            if not (first and c < R):
                                pe.wait_ge(s_ev, CH * f + c - R + 1)
                            out = ps[:, c % R, 0:n]
                            for k in range(KD):
                                mm = mm3(nc, out, w_hi[:, q, k], w_lo[:, q, k], h_hi[:, k, t0:t0 + n], h_lo[:, k, t0:t0 + n], k == 0, k == KD - 1)
                            mm.then_inc(s_mm, 1)
                over(pe, KI, step, last_differs=False)

            @block.scalar
            def _(act):
                def split(f, q):
                    act.wait_ge(s_w[q], 16 * (f + 1))
                    nc.scalar.activation(w_hi[:, q], raw[:, q], ACT.Copy).then_inc(s_hi, 1)

                for q in range(U):
                    split(0, q)

                def step(f, first, last):
                    for q in range(U):
                        if not first:
                            act.wait_ge(s_ew, EW * (f - 1) + (6, 6, 7, 8)[q])
                        for g, (t0, n) in enumerate(GROUPS):
                            c = q * G + g
                            act.wait_ge(s_mm, CH * f + c + 1)
                            if q == 2:
                                nc.scalar.activation(sg[:, t0:t0 + n], ps[:, c % R, 0:n], ACT.Sigmoid).then_inc(s_sg, 1)
                            nc.scalar.activation(ev[:, q, t0:t0 + n], ps[:, c % R, 0:n], ACT.Copy).then_inc(s_ev, 1)
                        if not last:
                            split(f + 1, q)
                over(act, KI, step)

            @block.vector
            def _(dve):
                def split(f, q, mm=None):
                    dve.wait_ge(s_hi, U * f + q + 1)
                    nc.vector.tensor_tensor(w_lo[:, q], raw[:, q], w_hi[:, q].bitcast(F32), ALU.subtract).then_inc(s_lo, 1)

                for q in range(U):
                    split(0, q)

                def step(f, first, last):
                    if not last:
                        split(f + 1, 0)
                    dve.wait_ge(s_ev, CH * f + 2 * G)
                    nc.vector.tensor_tensor(cu[:, :], ev[:, 0, :], ev[:, 1, :], ALU.mult).then_inc(s_ew, 1)
                    dve.wait_ge(s_ew, EW * f + 1)
                    conv_taps(nc, dve, cv, cu, par, COL_CONV, f, s_ew, EW * f + 1)
                    if not last:
                        split(f + 1, 1)
                    dve.wait_ge(s_ev, CH * f + 3 * G)
                    dve.wait_ge(s_sg, G * (f + 1))
                    dve.wait_ge(s_ew, EW * f + 6)
                    nc.vector.tensor_tensor(ev[:, 2, :], ev[:, 2, :], sg[:, :], ALU.mult).then_inc(s_ew, 1)
                    dve.wait_ge(s_ew, EW * f + 7)
                    nc.vector.tensor_tensor(cv[:, :], cv[:, :], ev[:, 2, :], ALU.mult).then_inc(s_ew, 1)
                    if not last:
                        split(f + 1, 2)
                    dve.wait_ge(s_ev, CH * (f + 1))
                    dve.wait_ge(s_ew, EW * f + 8)
                    if not first:
                        dve.wait_ge(s_st, 16 * f)
                    nc.vector.tensor_tensor(y[:, :], cv[:, :], ev[:, 3, :], ALU.mult).then_inc(s_y, 1)
                    if not last:
                        split(f + 1, 3)
                over(dve, KI, step)


def lstm_in_phase(nc, sem, keep, scr, io, h_hi, h_lo):
    ps, par = keep["ps"], keep["par"]
    U = 3
    GR = (GROUPS, GROUPS[:2], GROUPS[:2])
    CH = sum(len(g) for g in GR)
    FIRST = (0, 3, 5)
    R = CH
    w_src = io["m_w_in"][0].rearrange("(k p) n -> p k n", p=P)
    by_tile = lambda a: a.rearrange("(f p) t -> f p t", p=P)
    dst = [by_tile(scr[n]) for n in ("uT", "ucT", "ymul", "yadd")]
    with ExitStack() as st:
        sb = lambda n, s, d=F32: st.enter_context(nc.sbuf_tensor(f"a1_{n}", s, d))
        raw, w_hi, w_lo = sb("raw", [P, U, KD, P]), sb("w_hi", [P, U, KD, P], F32R), sb("w_lo", [P, U, KD, P], F32R)
        u, cv, sc, uc = sb("u", [P, TT]), sb("cv", [P, TT]), sb("sc", [P, TT]), sb("uc", [P, TT])
        z, sz, so, mul, add = (sb(n, [P, TX]) for n in ("z", "sz", "so", "mul", "add"))
        out_tiles = (u, uc, mul, add)
        s_w = [sem(f"a1_w_loaded{q}") for q in range(U)]
        s_hi, s_lo, s_mm, s_ev, s_cv, s_scv, s_ew, s_st = (sem(f"a1_{n}") for n in (
            "w_hi_made", "w_lo_made", "chunk_done", "chunk_read", "conv_round", "conv_sigmoid", "mixed", "stored"))
        s_uo = sem("a1_u_stored")
        EW = 5
        with nc.Block() as block:
            @block.sync
            def _(sp):
                def load(f, q):
                    sp.dma_start(raw[:, q], w_src[:, :, bass.ds(q * DI + f * P, P)]).then_inc(s_w[q], 16)

                def store(f):
                    sp.wait_ge(s_ev, CH * f + 3)
                    sp.dma_start(dst[0][bass.ds(f, 1)].rearrange("a p t -> p (a t)"), u[:, :]).then_inc(s_uo, 16)
                    sp.wait_ge(s_ew, EW * (f + 1))
                    for i in range(1, 4):
                        sp.dma_start(dst[i][bass.ds(f, 1)].rearrange("a p t -> p (a t)"), out_tiles[i][:, :]).then_inc(s_st, 16)

                for q in range(U):
                    load(0, q)

                def step(f, first, last):
                    nxt = f + 1 if first or last else sp.snap(f + 1)
                    if not last:
                        for q in range(U):
                            sp.wait_ge(s_lo, U * f + q + 1)
                            load(nxt, q)
                    if not first:
                        store(f - 1)
                over(sp, KI, step)
                store(KI - 1)
                sp.wait_ge(s_uo, 16 * KI)
                sp.wait_ge(s_st, 48 * KI)

            @block.tensor
            def _(pe):
                def step(f, first, last):
                    for q in range(U):
                        pe.wait_ge(s_lo, U * f + q + 1)
                        for g, (t0, n) in enumerate(GR[q]):
                            c = FIRST[q] + g
                            if not first:
                                pe.wait_ge(s_ev, CH * f + c - R + 1)
                            out = ps[:, c, 0:n]
                            for k in range(KD):
                                mm = mm3(nc, out, w_hi[:, q, k], w_lo[:, q, k], h_hi[:, k, t0:t0 + n], h_lo[:, k, t0:t0 + n], k == 0, k == KD - 1)
                            mm.then_inc(s_mm, 1)
                over(pe, KI, step, last_differs=False)

            @block.scalar
            def _(act):
                def split(f, q):
                    act.wait_ge(s_w[q], 16 * (f + 1))
                    nc.scalar.activation(w_hi[:, q], raw[:, q], ACT.Copy).then_inc(s_hi, 1)

                for q in range(U):
                    split(0, q)

                def step(f, first, last):
                    if not first:
                        act.wait_ge(s_uo, 16 * f)
                        act.wait_ge(s_cv, 5 * f)
                    for g, (t0, n) in enumerate(GR[0]):
                        act.wait_ge(s_mm, CH * f + g + 1)
                        nc.scalar.activation(u[:, t0:t0 + n], ps[:, g, 0:n], ACT.Copy).then_inc(s_ev, 1)
                    if not last:
                        split(f + 1, 0)
                    act.wait_ge(s_cv, 5 * (f + 1))
                    if not first:
                        act.wait_ge(s_ew, EW * f)
                    nc.scalar.activation(sc[:, :], cv[:, :], ACT.Sigmoid).then_inc(s_scv, 1)
                    for g, (t0, n) in enumerate(GR[1]):
                        c = FIRST[1] + g
                        act.wait_ge(s_mm, CH * f + c + 1)
                        nc.scalar.activation(sz[:, t0:t0 + n], ps[:, c, 0:n], ACT.Sigmoid).then_inc(s_scv, 1)
                        nc.scalar.activation(z[:, t0:t0 + n], ps[:, c, 0:n], ACT.Copy).then_inc(s_ev, 1)
                    if not last:
                        split(f + 1, 1)
                    for g, (t0, n) in enumerate(GR[2]):
                        c = FIRST[2] + g
                        act.wait_ge(s_mm, CH * f + c + 1)
                        nc.scalar.activation(so[:, t0:t0 + n], ps[:, c, 0:n], ACT.Sigmoid).then_inc(s_ev, 1)
                    if not last:
                        split(f + 1, 2)
                over(act, KI, step)

            @block.vector
            def _(dve):
                def split(f, q):
                    dve.wait_ge(s_hi, U * f + q + 1)
                    nc.vector.tensor_tensor(w_lo[:, q], raw[:, q], w_hi[:, q].bitcast(F32), ALU.subtract).then_inc(s_lo, 1)

                for q in range(U):
                    split(0, q)

                def step(f, first, last):
                    dve.wait_ge(s_ev, CH * f + 3)
                    if not first:
                        dve.wait_ge(s_ew, EW * f)
                    conv_taps(nc, dve, cv, u, par, COL_MCONV, f, s_cv, 5 * f)
                    if not last:
                        split(f + 1, 0)
                    dve.wait_ge(s_cv, 5 * (f + 1))
                    dve.wait_ge(s_scv, 3 * f + 1)
                    if not first:
                        dve.wait_ge(s_st, 48 * f)
                    nc.vector.tensor_tensor(uc[:, :], cv[:, :], sc[:, :], ALU.mult).then_inc(s_ew, 1)
                    dve.wait_ge(s_ev, CH * f + 5)
                    dve.wait_ge(s_scv, 3 * f + 3)
                    nc.vector.tensor_tensor(z[:, :], z[:, :], sz[:, :], ALU.mult).then_inc(s_ew, 1)
                    if not last:
                        split(f + 1, 1)
                    dve.wait_ge(s_ew, EW * f + 2)
                    nc.vector.scalar_tensor_tensor(add[:, :], uc[:, 0:TX], par[:, bass.ds(COL_SKIP + f, 1)], z[:, :], ALU.mult, ALU.mult).then_inc(s_ew, 1)
                    dve.wait_ge(s_ev, CH * (f + 1))
                    nc.vector.scalar_tensor_tensor(mul[:, :], so[:, :], par[:, bass.ds(COL_NORM + f, 1)], z[:, :], ALU.mult, ALU.mult).then_inc(s_ew, 2)
                    if not last:
                        split(f + 1, 2)
                over(dve, KI, step)


def qkv_phase(nc, sem, keep, scr, io, early, bg):
    ps = keep["ps"]
    UN = 6
    RS = 3
    EB = 2
    G = len(GROUPS)
    CH = UN * EB * G
    R = 4
    TILES = UN * EB
    RT = 3
    XS = 4
    CR = 3
    LAG = 2
    SCALE = float(DH) ** -0.5
    w_src = [io[n][0].rearrange("h (k p) e -> h p k e", p=P) for n in ("m_wq", "m_wk", "m_wv")]
    x_src = [scr[n].rearrange("(f p) t -> f p t", p=P) for n in ("ucT", "uT")]
    dst = scr["qkvT"].rearrange("m (f p) t -> m f p t", p=P)
    KINDS = (0, 2, 1, 3)
    with ExitStack() as st:
        sb = lambda n, s, d=F32: st.enter_context(nc.sbuf_tensor(f"q_{n}", s, d))
        raw, w_hi, w_lo = sb("raw", [P, RS, KH, EB * P]), sb("w_hi", [P, RS, KH, EB * P], F32R), sb("w_lo", [P, RS, KH, EB * P], F32R)
        xr = sb("xr", [P, XS, TT])
        x_hi, x_lo = sb("x_hi", [P, 2, KH, TT], F32R), sb("x_lo", [P, 2, KH, TT], F32R)
        wg = sb("wg", [P, 3, HEADS * KH, 4 * HEADS])
        wgp, wgr = sb("wgp", [P, TILES, P]), sb("wgr", [P, TILES, P], F32R)
        tile = sb("tile", [P, RT, TT])
        t_hi, t_lo = sb("t_hi", [P, CR, BANK], F32R), sb("t_lo", [P, CR, BANK], F32R)
        s_w = [sem(f"q_w_loaded{i}") for i in range(RS)]
        s_xr = [sem(f"q_x_loaded{i}") for i in range(XS)]
        s_st = [sem(f"q_tile_stored{i}") for i in range(RT)]
        s_hi, s_lo, s_xhi, s_xlo, s_mm, s_ev, s_thi, s_tlo, s_g, s_gr, s_wg, s_wgz, s_wgp, s_wgh, s_wgl, s_bz, s_c = (sem(f"q_{n}") for n in (
            "w_hi_made", "w_lo_made", "x_hi_made", "x_lo_made", "chunk_done", "chunk_read", "chunk_hi_made", "chunk_lo_made",
            "gates_done", "gates_read", "gate_w_loaded", "gate_w_cleared", "gate_w_placed", "gate_w_hi_made", "gate_w_lo_made",
            "bias_cleared", "constants"))

        def xwhich(h, j):
            return x_src[j // KH][bass.ds(h * KH + j % KH, 1)].rearrange("a p t -> p (a t)")

        with nc.Block() as block:
            @block.sync
            def _(sp):
                def load_w(h, n):
                    m, e0 = n // 2, (n % 2) * EB * P
                    sp.dma_start(raw[:, n % RS], w_src[m][bass.ds(h, 1), :, :, e0:e0 + EB * P].rearrange("a p k e -> p (a k) e")).then_inc(s_w[n % RS], 16)

                def load_x(h, j):
                    sp.dma_start(xr[:, j % XS], xwhich(h, j)).then_inc(s_xr[j % XS], 16)

                for j in range(KH):
                    load_x(0, j)
                load_w(0, 0)
                sp.dma_start(wg[:, :, :, :], io["m_w_gate"][0].rearrange("(m f p) c -> p m f c", m=3, p=P)).then_inc(s_wg, 16)
                sp.wait_ge(s_bz, 1)
                for q, kind in enumerate(KINDS):
                    sp.dma_start(bg[32 * kind:32 * kind + HEADS, :], io["m_b_gate"][0, q * HEADS:(q + 1) * HEADS].rearrange("(h o) -> h o", o=1)).then_inc(s_wg, 16)
                load_w(0, 1)
                load_w(0, 2)
                for j in range(KH, 2 * KH):
                    sp.wait_ge(s_xlo, j - KH + 1)
                    load_x(0, j)

                def step(h, first, last):
                    for n in range(UN):
                        if n + RS < UN or not last:
                            if n != 2:
                                sp.wait_ge(s_lo, UN * h + (n + 1 if n != 1 else 3))
                            if n + RS >= UN:
                                load_w(h + 1, n + RS - UN)
                            elif n == 1:
                                load_w(h, 5)
                                load_w(h, 4)
                            elif n != 2:
                                load_w(h, n + RS)
                        if n == 1 and not last:
                            for j in range(KH):
                                sp.wait_ge(s_xlo, 8 * h + KH + j + 1)
                                load_x(h + 1, j)
                        for e in range(EB):
                            t = n * EB + e
                            sp.wait_ge(s_ev, CH * h + (t + 1) * G)
                            sp.dma_start(dst[n // 2][bass.ds(h * KH + t % KH, 1)].rearrange("a p t -> p (a t)"), tile[:, t % RT, :]).then_inc(s_st[t % RT], 16)
                    if not last:
                        for j in range(KH, 2 * KH):
                            sp.wait_ge(s_xlo, 8 * (h + 1) + j - KH + 1)
                            load_x(h + 1, j)
                over(sp, HEADS, step)
                for i in range(RT):
                    sp.wait_ge(s_st[i], 16 * HEADS * TILES // RT)

            @block.gpsimd
            def _(pool):
                fold = early["fold"][:, :]
                nc.gpsimd.memset(bg[:, :], 0.0).then_inc(s_bz, 1)
                nc.gpsimd.memset(fold, 0.0).then_inc(s_c, 1)
                nc.gpsimd.memset(early["ones"][:, :], 1.0).then_inc(s_c, 1)
                nc.gpsimd.memset(early["a_rows"][:, :], 0.0).then_inc(s_c, 1)
                for i, below in enumerate((0, 16)):
                    pool.wait_ge(s_c, 3 + i)
                    nc.gpsimd.affine_select(out=fold, in_=fold, compare_op=ALU.not_equal, fill=1.0, base=-below,
                                            pattern=[[-1, P]], channel_multiplier=1).then_inc(s_c, 1)

            @block.tensor
            def _(pe):
                def gate_products(h, c, first, last):
                    t, g = c // G, c % G
                    nn = GROUPS[g][1]
                    pe.wait_ge(s_tlo, CH * h + c + 1)
                    if t % KH == 0 and g == 0:
                        pe.wait_ge(s_wgl, 3 * h + t // KH + 1)
                    nc.tensor.matmul(ps[:, R + g, 0:nn], wgr[:, t, :], t_lo[:, c % CR, 0:nn], start=first and t == 0, stop=False)
                    nc.tensor.matmul(ps[:, R + g, 0:nn], wgr[:, t, :], t_hi[:, c % CR, 0:nn], start=False, stop=last and t == TILES - 1).then_inc(s_g, 1)

                def step(h, first, last):
                    for n in range(UN):
                        pe.wait_ge(s_lo, UN * h + n + 1)
                        src = 0 if n < 4 else 1
                        if n == 0:
                            pe.wait_ge(s_xlo, 8 * h + KH)
                        if n == 4:
                            pe.wait_ge(s_xlo, 8 * h + 2 * KH)
                        for e in range(EB):
                            for g, (t0, nn) in enumerate(GROUPS):
                                c = (n * EB + e) * G + g
                                if not (first and c < R):
                                    pe.wait_ge(s_ev, CH * h + c - R + 1)
                                for k in range(KH):
                                    mm = mm3(nc, ps[:, c % R, 0:nn], w_hi[:, n % RS, k, e * P:(e + 1) * P], w_lo[:, n % RS, k, e * P:(e + 1) * P],
                                             x_hi[:, src, k, t0:t0 + nn], x_lo[:, src, k, t0:t0 + nn], k == 0, k == KH - 1)
                                mm.then_inc(s_mm, 1)
                                if c >= LAG:
                                    gate_products(h, c - LAG, first, last)
                                elif not first:
                                    gate_products(h - 1, CH - LAG + c, False, False)
                over(pe, HEADS, step)
                for c in range(CH - LAG, CH):
                    gate_products(HEADS - 1, c, False, True)

            @block.scalar
            def _(act):
                def split_w(h, n):
                    act.wait_ge(s_w[n % RS], 32 * h + 16 * (n // RS + 1))
                    nc.scalar.activation(w_hi[:, n % RS], raw[:, n % RS], ACT.Copy).then_inc(s_hi, 1)

                def split_x(h, j):
                    act.wait_ge(s_xr[j % XS], 32 * h + 16 * (j // XS + 1))
                    nc.scalar.activation(x_hi[:, j // KH, j % KH, :], xr[:, j % XS, :], ACT.Copy).then_inc(s_xhi, 1)

                def round_gate_w(h, m, first):
                    act.wait_ge(s_wgp, 4 * (3 * h + m + 1))
                    if not first:
                        act.wait_ge(s_g, CH * (h - 1) + KH * (m + 1) * G)
                    nc.scalar.activation(wgr[:, KH * m:KH * (m + 1), :], wgp[:, KH * m:KH * (m + 1), :], ACT.Copy).then_inc(s_wgh, 1)

                for j in range(KH):
                    split_x(0, j)
                for n in range(RS):
                    split_w(0, n)
                for m in range(3):
                    round_gate_w(0, m, True)
                for j in range(KH, 2 * KH):
                    split_x(0, j)

                def step(h, first, last):
                    for n in range(UN):
                        for c in range(n * EB * G, (n + 1) * EB * G):
                            t, g = c // G, c % G
                            t0, nn = GROUPS[g]
                            act.wait_ge(s_mm, CH * h + c + 1)
                            if g == 0 and not (first and t < RT):
                                act.wait_ge(s_st[t % RT], 16 * ((TILES // RT) * h + t // RT))
                                act.wait_ge(s_tlo, CH * h + (t - RT + 1) * G)
                            nc.scalar.activation(tile[:, t % RT, t0:t0 + nn], ps[:, c % R, 0:nn], ACT.Copy,
                                                 scale=SCALE if n // 2 == 1 else 1.0).then_inc(s_ev, 1)
                            act.wait_ge(s_ev, CH * h + c + 1)
                            if not (first and c < CR):
                                act.wait_ge(s_g, CH * h + c - CR + 1)
                            nc.scalar.activation(t_hi[:, c % CR, 0:nn], tile[:, t % RT, t0:t0 + nn], ACT.Copy).then_inc(s_thi, 1)
                        if n + RS < UN:
                            split_w(h, n + RS)
                        elif not last:
                            split_w(h + 1, n + RS - UN)
                        if n == 0 and not first:
                            round_gate_w(h, 2, False)
                        if n in (2, 4) and not last:
                            round_gate_w(h + 1, n // 2 - 1, False)
                        if n == 1 and not first:
                            for j in range(KH, 2 * KH):
                                split_x(h, j)
                        if n == 4 and not last:
                            for j in range(KH):
                                split_x(h + 1, j)
                over(act, HEADS, step)
                act.wait_ge(s_g, CH * HEADS)
                for g in (0, 2):
                    t0, nn = GROUPS[g]
                    nc.scalar.activation(early["gate_sums"][:, t0:t0 + nn], ps[:, R + g, 0:nn], ACT.Copy).then_inc(s_gr, 1)

            @block.vector
            def _(dve):
                def split_w(h, n):
                    dve.wait_ge(s_hi, UN * h + n + 1)
                    nc.vector.tensor_tensor(w_lo[:, n % RS], raw[:, n % RS], w_hi[:, n % RS].bitcast(F32), ALU.subtract).then_inc(s_lo, 1)

                def split_x(h, j):
                    dve.wait_ge(s_xhi, 8 * h + j + 1)
                    a = (slice(None), j // KH, j % KH)
                    nc.vector.tensor_tensor(x_lo[a], xr[:, j % XS, :], x_hi[a].bitcast(F32), ALU.subtract).then_inc(s_xlo, 1)

                def gate_w_view(w, m, twice, group):
                    at = 32 * group + 16 * twice
                    return w[:, KH * m:KH * (m + 1), :].rearrange("p k (b c) -> p k b c", b=2)[:, :, :, at:at + HEADS]

                def place(h, m, first):
                    if not first:
                        dve.wait_ge(s_wgh, 3 * (h - 1) + m + 1)
                    for twice in range(2):
                        for group in range(2):
                            nc.vector.tensor_copy(gate_w_view(wgp, m, twice, group),
                                                  wg[:, m, bass.ds(h * KH, KH), 8 * group:8 * group + 8].rearrange("p k (b c) -> p k b c", b=2)).then_inc(s_wgp, 1)

                def gate_w_low(h, m):
                    dve.wait_ge(s_wgh, 3 * h + m + 1)
                    for group in range(2):
                        v = gate_w_view(wgr, m, 1, group)
                        low = nc.vector.tensor_tensor(v, gate_w_view(wgp, m, 1, group), v.bitcast(F32), ALU.subtract)
                    low.then_inc(s_wgl, 1)

                nc.vector.memset(wgp[:, :, :], 0.0).then_inc(s_wgz, 1)
                for j in range(KH):
                    split_x(0, j)
                split_w(0, 0)
                split_w(0, 1)
                split_w(0, 2)
                dve.wait_ge(s_wgz, 1)
                dve.wait_ge(s_wg, 80)
                for m in range(3):
                    place(0, m, True)
                for m in range(3):
                    gate_w_low(0, m)
                for j in range(KH, 2 * KH):
                    split_x(0, j)

                def step(h, first, last):
                    for n in range(UN):
                        if n == 0 and not first:
                            place(h, 2, False)
                        if n in (2, 4) and not last:
                            place(h + 1, n // 2 - 1, False)
                        for c in range(n * EB * G, (n + 1) * EB * G):
                            t, (t0, nn) = c // G, GROUPS[c % G]
                            dve.wait_ge(s_thi, CH * h + c + 1)
                            nc.vector.tensor_tensor(t_lo[:, c % CR, 0:nn], tile[:, t % RT, t0:t0 + nn], t_hi[:, c % CR, 0:nn].bitcast(F32), ALU.subtract).then_inc(s_tlo, 1)
                        if n + RS < UN:
                            split_w(h, n + RS)
                        elif not last:
                            split_w(h + 1, n + RS - UN)
                        if n == 0 and not first:
                            gate_w_low(h, 2)
                        if n in (2, 4) and not last:
                            gate_w_low(h + 1, n // 2 - 1)
                        if n == 1 and not first:
                            for j in range(KH, 2 * KH):
                                split_x(h, j)
                        if n == 4 and not last:
                            for j in range(KH):
                                split_x(h + 1, j)
                over(dve, HEADS, step)
                dve.wait_ge(s_g, CH * HEADS)
                t0, nn = GROUPS[1]
                nc.vector.tensor_copy(early["gate_sums"][:, t0:t0 + nn], ps[:, R + 1, 0:nn]).then_inc(s_gr, 1)


def attention_phase(nc, sem, keep, scr, io, early, bg):
    ps, ident = keep["ps"], keep["ident"]
    NG = 2
    JT = BANK // P
    FULL, DIAG = BANK, BANK + P
    PT = 4 * FULL + 4 * FULL + 4 * DIAG
    NV = KH * 3
    VCH = [(0, 4), (4, 4), (8, 2)]
    src = scr["qkvT"].rearrange("m (h k p) t -> m h k p t", p=P, k=KH)
    fac = [scr[n].rearrange("(f p) t -> f p t", p=P) for n in ("ymul", "yadd")]
    y_dst = scr["yT"].rearrange("(f p) t -> f p t", p=P)

    def subs(g):
        out = []
        for t in (NTX, NTX + 1):
            for d in range(2):
                out.append((t, d, len(out) * FULL))
        off = 4 * FULL
        for t in range(NTX):
            if not JT * g <= t < JT * (g + 1):
                out.append((t, 0 if t < JT * g else 1, off))
                off += FULL
        for t in range(JT * g, JT * (g + 1)):
            out.append((t, None, off))
            off += DIAG
        return out

    NS = len(subs(0))
    NC_ = NT
    with ExitStack() as st:
        sb = lambda n, s, d=F32: st.enter_context(nc.sbuf_tensor(f"b_{n}", s, d))
        p_hi = sb("p_hi", [P, PT], F32R)
        with ExitStack() as inner:
            gates, lf, t1, bsum, big = (inner.enter_context(nc.sbuf_tensor(f"g_{n}", [P, TT], F32)) for n in ("gates", "lf", "t1", "bsum", "big"))
        p_lo = sb("p_lo", [P, PT], F32R)
        q_hi, q_lo = sb("q_hi", [P, KH, BANK], F32R), sb("q_lo", [P, KH, BANK], F32R)
        k_hi, k_lo = sb("k_hi", [P, KH, TT], F32R), sb("k_lo", [P, KH, TT], F32R)
        v_hi, v_lo = sb("v_hi", [P, NT, DH], F32R), sb("v_lo", [P, NT, DH], F32R)
        cols, em = sb("a_cols", [P, NT, 2, HEADS]), sb("em_cols", [P, NTX, 2, HEADS])
        ones, a_out, av = early["ones"], early["a_rows"], early["av"]
        mc = sb("mc", [64, 1])
        X, C = slice(0, TX), slice(TX, TT)
        BOTH = slice(0, 64)
        TURNS = ((3, 0, 4), (4, 4, 4), (7, 8, 2))
        qr, kr = sb("qr", [P, KH, BANK]), sb("kr", [P, 2, TT])
        nm = sb("nm", [P, 2, TX])
        e, pr = sb("e", [P, 2, DIAG]), sb("pr", [P, 2, DIAG])
        mask = sb("mask", [P, 2, P])
        one = sb("one", [P, 1])
        hc = sb("hc", [P, NT, 2])
        acc = sb("acc", [P, 2, BANK])
        rn, st6, mv, rstd, tmp4 = sb("rn", [P, 2, JT]), sb("st6", [P, JT, 6]), sb("mv", [P, JT, 2]), sb("rstd", [P, JT]), sb("tmp4", [P, JT])
        hs = sb("hs", [P, JT, DH])
        fc = sb("fc", [P, 2, 2, BANK])
        names = ("q_loaded", "nm_loaded", "q_hi_made", "q_lo_made", "k_hi_made", "k_lo_made", "v_hi_made", "v_lo_made",
                 "v_turned", "s_done", "arg_made", "e_made", "p_made", "p_hi_made", "p_lo_made", "p_summed", "acc_cleared",
                 "den_done", "norm_step", "pv_done", "pvf_read", "pvb_read", "stat_step", "ln_step", "hn_made", "hn_turned", "y_step", "const")
        (s_q, s_nm, s_qhi, s_qlo, s_khi, s_klo, s_vhi, s_vlo, s_vt, s_s, s_arg, s_e, s_p, s_phi, s_plo, s_acc, s_az,
         s_den, s_nrm, s_pv, s_pvf, s_pvb, s_st, s_ln, s_hn, s_ht, s_y, s_c) = (sem("b_" + n) for n in names)
        s_kr, s_fc, s_yst = ([sem(f"b_{n}{i}") for i in range(2)] for n in ("kr_loaded", "fac_loaded", "y_stored"))
        s_gf, s_gt, s_gv, s_ga, s_gx, s_gtr, s_gcp, s_gout = (sem(f"g_{n}") for n in (
            "folded", "gates_made", "vector_step", "log_step", "rows_made", "turned", "copied", "stored"))
        s_hc, s_hs2, s_hs3 = sem("b_head_cols"), sem("b_head_stats"), sem("b_head_mean")

        def chunk_of(i):
            return (i // 2, i % 2 == 1) if i < 4 else (i - 2, True)

        def pieces_to(c):
            return 2 * c + 2 if c < 2 else c + 3

        VAT = {1: [0, 1], 2: [2], 3: [3, 4], 4: [5], 5: [6, 7], 6: [8, 9], 7: [10, 11]}
        SB, HB, VB, PB = 3, 3, 5, 4
        VR = 3
        TAT = (2, 4, 5, 7)

        def gi(h, g):
            return NG * h + g

        def load_kv(eng, h, j):
            eng.dma_start(kr[:, j % 2], src[1 + j // KH][bass.ds(h, 1), j % KH].rearrange("a p t -> p (a t)")).then_inc(s_kr[j % 2], 16)

        with nc.Block() as block:
            @block.sync
            def _(sp):
                def load_q(h, g):
                    for k in range(KH):
                        sp.dma_start(qr[:, k], src[0][bass.ds(h, 1), k, :, g * BANK:(g + 1) * BANK].rearrange("a p t -> p (a t)")).then_inc(s_q, 16)

                def load_nm(h):
                    for d in range(2):
                        sp.dma_start(nm[:, d, :], scr["nmrow"][d][bass.ds(h, 1), :].to_broadcast([P, TX])).then_inc(s_nm, 16)

                def factors(h, g):
                    for k in range(KH + 1):
                        if k < KH:
                            if k > 1 or not isinstance(h, int) or h or g:
                                sp.wait_ge(s_yst[k % 2], 16 * (2 * gi(h, g) + k // 2))
                            for i in range(2):
                                sp.dma_start(fc[:, k % 2, i, :], fac[i][bass.ds(h * KH + k, 1), :, g * BANK:(g + 1) * BANK].rearrange("a p t -> p (a t)")).then_inc(s_fc[k % 2], 16)
                        if k:
                            sp.wait_ge(s_y, 2 * (KH * gi(h, g) + k))
                            sp.dma_start(y_dst[bass.ds(h * KH + k - 1, 1), :, g * BANK:(g + 1) * BANK].rearrange("a p t -> p (a t)"), fc[:, (k - 1) % 2, 0, :]).then_inc(s_yst[(k - 1) % 2], 16)

                load_q(0, 0)
                load_kv(sp, 0, 0)
                load_kv(sp, 0, 1)
                for j in (2, 3):
                    sp.wait_ge(s_klo, j - 1)
                    load_kv(sp, 0, j)
                sp.wait_ge(s_gv, 14)
                for d in range(2):
                    sp.dma_start(scr["nmrow"][d], lf[32 * d:32 * d + HEADS, X]).then_inc(s_gout, 16)
                sp.wait_ge(s_gout, 32)
                load_nm(0)

                def step(h, first, last):
                    for j in (KH, KH + 1):
                        sp.wait_ge(s_klo, KH * h + j - 1)
                        load_kv(sp, h, j)
                    sp.wait_ge(s_qlo, NG * h + 1)
                    load_q(h, 1)
                    if not first:
                        factors(h - 1, 1)
                    if not last:
                        sp.wait_ge(s_qlo, NG * h + 2)
                        load_q(h + 1, 0)
                    factors(h, 0)
                    if not last:
                        sp.wait_ge(s_e, NG * (h + 1) * NS)
                        load_nm(h + 1)
                        sp.wait_ge(s_vt, NV * (h + 1))
                        for j in range(KH):
                            if j > 1:
                                sp.wait_ge(s_klo, KH * (h + 1) + j - 1)
                            load_kv(sp, h + 1, j)
                over(sp, HEADS, step)
                factors(HEADS - 1, 1)
                for i in range(2):
                    sp.wait_ge(s_yst[i], 16 * (KH // 2) * NG * HEADS)

            def each_group(run):
                def step(h, first, last):
                    for g in range(NG):
                        run(h, g, first and g == 0, last and g == NG - 1, first, last)
                return step

            @block.tensor
            def _(pe):
                def turn_hn(h, g, k):
                    pe.wait_ge(s_hn, JT * (gi(h, g) + 1))
                    n = KH * gi(h, g) + k
                    if k > 1 or not isinstance(h, int) or h or g:
                        pe.wait_ge(s_y, 2 * n - 3)
                    for j in range(JT):
                        tr = nc.tensor.transpose(ps[:, HB + k % 2, j * P:(j + 1) * P], hs[:, j, k * P:(k + 1) * P], ident[:, :])
                    tr.then_inc(s_ht, 1)

                def run(h, g, first, last, first_head, last_head):
                    n = gi(h, g)
                    pieces = subs(g)
                    order = [pieces[0][0], pieces[2][0]] + [x[0] for x in pieces[4:]]
                    pe.wait_ge(s_qlo, n + 1)
                    if g == 0:
                        pe.wait_ge(s_klo, KH * (h + 1))
                    for c, t in enumerate(order):
                        if c >= SB:
                            pe.wait_ge(s_p, NS * n + pieces_to(c - SB))
                        elif not first:
                            pe.wait_ge(s_p, NS * n)
                        for k in range(KH):
                            mm = mm3(nc, ps[:, c % SB, :], k_hi[:, k, t * P:(t + 1) * P], k_lo[:, k, t * P:(t + 1) * P], q_hi[:, k, :], q_lo[:, k, :], k == 0, k == KH - 1)
                        mm.then_inc(s_s, 1)
                        if c in TAT and not first:
                            turn_hn(h if g else h - 1, 1 - g, TAT.index(c))
                        if g == 0:
                            for v in VAT.get(c, ()):
                                k, (t0, nt) = v // 3, VCH[v % 3]
                                if v % 3 == 0:
                                    kr_uses = 4 * h + (KH + k) // 2 + 1
                                    pe.wait_ge(s_kr[k % 2], 16 * kr_uses)
                                if v >= VR:
                                    pe.wait_ge(s_vlo, NV * h + v - VR + 1)
                                elif v == 2 and first_head:
                                    pe.wait_ge(s_gcp, len(TURNS))
                                elif v == 0 and not first_head:
                                    pe.wait_ge(s_pvf, JT * n)
                                    pe.wait_ge(s_pvb, JT * n)
                                for i in range(nt):
                                    tr = nc.tensor.transpose(ps[:, VB + v % VR, i * P:(i + 1) * P], kr[:, k % 2, (t0 + i) * P:(t0 + i + 1) * P], ident[:, :])
                                tr.then_inc(s_vt, 1)
                    where = {(t, d): off for t, d, off in pieces}
                    for j in range(JT):
                        J = JT * g + j
                        for d in range(2):
                            keys = [(t, where[(t, d)] + j * P) for t in (NTX, NTX + 1)]
                            for t, dd, off in pieces[4:]:
                                if dd is None:
                                    if t == J:
                                        keys.append((t, off + (j * P if d == 0 else BANK)))
                                    elif (t < J) == (d == 0):
                                        keys.append((t, off + j * P))
                                elif dd == d:
                                    keys.append((t, off + j * P))
                            b = PB + 2 * (j % 2) + d
                            if not (first and j < 2):
                                pe.wait_ge(s_pvf if d == 0 else s_pvb, JT * n + j - 1)
                            if j == 0 and d == 0 and not first:
                                pe.wait_ge(s_y, 2 * KH * n - 1)
                            for i, (t, off) in enumerate(keys):
                                if j == 0:
                                    piece = [x[0] for x in pieces].index(t) + (d if t >= NTX else 0)
                                    pe.wait_ge(s_plo, NS * n + piece + 1)
                                    if d == 0 and i == 0 and g == 0:
                                        pe.wait_ge(s_vlo, NV * (h + 1))
                                mm = mm3(nc, ps[:, b, :], p_hi[:, off:off + P], p_lo[:, off:off + P], v_hi[:, t, :], v_lo[:, t, :], i == 0, i == len(keys) - 1)
                            mm.then_inc(s_pv, 1)
                        if j == 0:
                            pe.wait_ge(s_acc, NS * (n + 1))
                            for d in range(2):
                                for jj in range(JT):
                                    mm = nc.tensor.matmul(ps[:, HB, d * JT + jj:d * JT + jj + 1], acc[:, d, jj * P:(jj + 1) * P], one[:, :],
                                                          start=(d == 0 and jj == 0), stop=(d == 1 and jj == JT - 1), skip_group_check=True)
                            mm.then_inc(s_den, 1)

                for g, (t0, nn) in enumerate(GROUPS):
                    nc.tensor.matmul(ps[:, 5 + g, 0:nn], early["fold"][:, :], early["gate_sums"][:, t0:t0 + nn], start=True, stop=True).then_inc(s_gf, 1)
                pe.wait_ge(s_gx, 5)
                pe.wait_ge(s_gt, 12)
                for bank, first_tile, nt in TURNS:
                    for i in range(nt):
                        t = first_tile + i
                        tr = nc.tensor.transpose(ps[:, bank, i * P:(i + 1) * P], a_out[:, t * P:(t + 1) * P], ident[:, :])
                    tr.then_inc(s_gtr, 1)
                pe.wait_ge(s_c, 4)
                over(pe, HEADS, each_group(run), last_differs=False)
                for k in range(KH):
                    turn_hn(HEADS - 1, 1, k)

            @block.scalar
            def _(act):
                def split_q(n):
                    act.wait_ge(s_q, 16 * KH * (n + 1))
                    nc.scalar.activation(q_hi[:, :, :], qr[:, :, :], ACT.Copy).then_inc(s_qhi, 1)

                def split_k(h, k):
                    act.wait_ge(s_kr[k % 2], 16 * (4 * h + k // 2 + 1))
                    nc.scalar.activation(k_hi[:, k, :], kr[:, k % 2, :], ACT.Copy).then_inc(s_khi, 1)

                for g, (t0, nn) in enumerate(GROUPS):
                    act.wait_ge(s_gf, g + 1)
                    for kind in (0, 2):
                        r = slice(32 * kind, 32 * (kind + 1))
                        nc.scalar.activation(gates[r, t0:t0 + nn], ps[r, 5 + g, 0:nn], ACT.Identity, bias=bg[r, :]).then_inc(s_gt, 1)
                act.wait_ge(s_gv, 1)
                nc.scalar.activation(t1[BOTH, :], t1[BOTH, :], ACT.Exp, scale=-1.0).then_inc(s_ga, 1)
                act.wait_ge(s_ga, 1)
                nc.scalar.activation(t1[BOTH, :], t1[BOTH, :], ACT.Ln, bias=1.0).then_inc(s_ga, 1)
                split_q(0)
                for k in range(2):
                    split_k(0, k)
                act.wait_ge(s_gv, 7)
                nc.scalar.activation(a_out[0:32, :], av[0:32, :], ACT.Copy).then_inc(s_gx, 1)
                for s in (X, C):
                    nc.scalar.activation(a_out[32:64, s][:, ::-1], av[32:64, s], ACT.Copy).then_inc(s_gx, 1)
                act.wait_ge(s_gv, 11)
                nc.scalar.activation(a_out[64:96, X], t1[0:32, X], ACT.Exp, scale=-1.0).then_inc(s_gx, 1)
                nc.scalar.activation(a_out[96:128, X][:, ::-1], t1[32:64, X], ACT.Exp, scale=-1.0).then_inc(s_gx, 1)
                for k in (2, 3):
                    split_k(0, k)
                for i, (bank, first_tile, nt) in enumerate(TURNS):
                    act.wait_ge(s_gtr, i + 1)
                    turned = ps[:, bank, 0:nt * P].rearrange("p (t c) -> p t c", c=P)
                    for d in range(2):
                        if first_tile < NTX:
                            nc.scalar.activation(em[:, first_tile:first_tile + nt, d, :], turned[:, :, 64 + 32 * d:64 + 32 * d + HEADS], ACT.Copy)
                        cp = nc.scalar.activation(cols[:, first_tile:first_tile + nt, d, :], turned[:, :, 32 * d:32 * d + HEADS], ACT.Copy)
                    cp.then_inc(s_gcp, 1)

                def weights(h, g, i, first):
                    n = gi(h, g)
                    t, d, off = subs(g)[i]
                    if i == 0:
                        act.wait_ge(s_nm, 32 * (h + 1))
                        act.wait_ge(s_hc, h + 1)
                    if not (first and i < 2):
                        act.wait_ge(s_p, NS * n + i - 1)
                    a = lambda dd: hc[:, t, dd:dd + 1]
                    q0 = g * BANK
                    if d is not None:
                        nc.scalar.activation(e[:, i % 2, 0:BANK], nm[:, d, q0:q0 + BANK], ACT.Exp, bias=a(d)).then_inc(s_e, 1)
                        return
                    j = t - JT * g
                    if j > 0:
                        nc.scalar.activation(e[:, i % 2, 0:j * P], nm[:, 1, q0:q0 + j * P], ACT.Exp, bias=a(1))
                    if j < JT - 1:
                        nc.scalar.activation(e[:, i % 2, (j + 1) * P:BANK], nm[:, 0, q0 + (j + 1) * P:q0 + BANK], ACT.Exp, bias=a(0))
                    act.wait_ge(s_arg, 2 * (JT * n + j + 1))
                    nc.scalar.activation(e[:, i % 2, j * P:(j + 1) * P], e[:, i % 2, j * P:(j + 1) * P], ACT.Exp)
                    nc.scalar.activation(e[:, i % 2, BANK:DIAG], e[:, i % 2, BANK:DIAG], ACT.Exp).then_inc(s_e, 1)

                weights(0, 0, 0, True)

                def run(h, g, first, last, first_head, last_head):
                    n = gi(h, g)
                    pieces = subs(g)
                    for i in range(NS):
                        if i + 1 < NS:
                            weights(h, g, i + 1, first)
                        t, d, off = pieces[i]
                        w = FULL if d is not None else DIAG
                        act.wait_ge(s_p, NS * n + i + 1)
                        if not first and i == 0:
                            act.wait_ge(s_pv, 2 * JT * n)
                        nc.scalar.activation(p_hi[:, off:off + w], pr[:, i % 2, 0:w], ACT.Copy).then_inc(s_phi, 1)
                        c, end = chunk_of(i)
                        if g == 0 and end:
                            for v in VAT.get(c, ()):
                                k, (t0, nt) = v // 3, VCH[v % 3]
                                act.wait_ge(s_vt, NV * h + v + 1)
                                if v == 0 and not first_head:
                                    act.wait_ge(s_pv, 2 * JT * n)
                                nc.scalar.activation(v_hi[:, t0:t0 + nt, k * P:(k + 1) * P], ps[:, VB + v % VR, 0:nt * P].rearrange("p (t e) -> p t e", e=P), ACT.Copy).then_inc(s_vhi, 1)
                                if v in (2, 5):
                                    load_kv(act, h, KH + 2 + v // 3)
                    for j in range(JT):
                        if j == 0:
                            if not last:
                                act.wait_ge(s_s, NC_ * (n + 1))
                                split_q(n + 1)
                            act.wait_ge(s_nrm, 3 * (n + 1))
                        if g == 1 and not last_head:
                            split_k(h + 1, j)
                        act.wait_ge(s_pv, 2 * (JT * n + j) + 1)
                        if not first:
                            act.wait_ge(s_ht, KH * n)
                        nc.scalar.activation(hs[:, j, :], ps[:, PB + 2 * (j % 2), :], ACT.Copy, scale=rn[:, 0, j:j + 1]).then_inc(s_pvf, 1)
                    if not last:
                        weights(h + g, 1 - g, 0, False)
                    act.wait_ge(s_ln, 5 * n + 1)
                    nc.scalar.activation(rstd[:, :], tmp4[:, :], ACT.Ln).then_inc(s_st, 1)
                    act.wait_ge(s_st, 2 * n + 1)
                    nc.scalar.activation(rstd[:, :], rstd[:, :], ACT.Exp, scale=-0.5).then_inc(s_st, 1)

                over(act, HEADS, each_group(run))

            @block.gpsimd
            def _(pool):
                nc.gpsimd.memset(one[:, :], 1.0).then_inc(s_c, 1)
                nc.gpsimd.memset(mask[:, :, :], 0.0).then_inc(s_c, 1)
                pool.wait_ge(s_c, 2)
                nc.gpsimd.affine_select(out=mask[:, 0, :], in_=mask[:, 0, :], compare_op=ALU.is_ge, fill=-1e30, base=0,
                                        pattern=[[1, P]], channel_multiplier=-1).then_inc(s_c, 1)
                nc.gpsimd.affine_select(out=mask[:, 1, :], in_=mask[:, 1, :], compare_op=ALU.is_ge, fill=-1e30, base=0,
                                        pattern=[[-1, P]], channel_multiplier=1).then_inc(s_c, 1)

                def run(h, g, first, last, first_head, last_head):
                    n = gi(h, g)
                    pool.wait_ge(s_az, n + 1)
                    for i, (t, d, off) in enumerate(subs(g)):
                        pool.wait_ge(s_p, NS * n + i + 1)
                        if i:
                            pool.wait_ge(s_acc, NS * n + i)
                        def add(dd, a, b, x):
                            return nc.gpsimd.tensor_tensor(acc[:, dd, a:b], acc[:, dd, a:b], pr[:, i % 2, x:x + b - a], ALU.add)
                        if d is not None:
                            add(d, 0, BANK, 0).then_inc(s_acc, 1)
                            continue
                        j = t - JT * g
                        if j > 0:
                            add(1, 0, j * P, 0)
                        add(0, j * P, BANK, j * P)
                        add(1, j * P, (j + 1) * P, BANK).then_inc(s_acc, 1)
                over(pool, HEADS, each_group(run), last_differs=False)

            @block.vector
            def _(dve):
                def split_q(n):
                    dve.wait_ge(s_qhi, n + 1)
                    nc.vector.tensor_tensor(q_lo[:, :, :], qr[:, :, :], q_hi[:, :, :].bitcast(F32), ALU.subtract).then_inc(s_qlo, 1)

                def split_k(h, k):
                    dve.wait_ge(s_khi, KH * h + k + 1)
                    nc.vector.tensor_tensor(k_lo[:, k, :], kr[:, k % 2, :], k_hi[:, k, :].bitcast(F32), ALU.subtract).then_inc(s_klo, 1)

                def head_cols(h):
                    nc.vector.tensor_copy(hc[:, :, :], cols[:, :, :, bass.ds(h, 1)].rearrange("p t d o -> p t (d o)")).then_inc(s_hc, 1)

                for g, (t0, nn) in enumerate(GROUPS):
                    dve.wait_ge(s_gf, g + 1)
                    to = slice(TX - t0 - nn, TX - t0) if g < 2 else C
                    for kind in (1, 3):
                        r = slice(32 * kind, 32 * (kind + 1))
                        nc.vector.tensor_scalar(gates[r, to][:, ::-1], ps[r, 5 + g, 0:nn], bg[r, :], None, ALU.add).then_inc(s_gt, 1)
                dve.wait_ge(s_gt, 12)
                f = gates[64:128, :]
                nc.vector.scalar_tensor_tensor(t1[BOTH, :], f, -1.0, f, ALU.mult, ALU.max).then_inc(s_gv, 1)
                nc.vector.tensor_scalar(bsum[BOTH, :], f, 0.0, None, ALU.min).then_inc(s_gv, 1)
                nc.vector.memset(acc[:, :, :], 0.0).then_inc(s_az, 1)
                dve.wait_ge(s_gv, 2)
                dve.wait_ge(s_ga, 2)
                nc.vector.tensor_tensor(lf[BOTH, :], bsum[BOTH, :], t1[BOTH, :], ALU.subtract).then_inc(s_gv, 1)
                dve.wait_ge(s_gv, 3)
                for s in (X, C):
                    nc.vector.tensor_tensor_scan(bsum[BOTH, s], ones[BOTH, s], lf[BOTH, s], 0.0, ALU.mult, ALU.add).then_inc(s_gv, 1)
                dve.wait_ge(s_gv, 5)
                nc.vector.tensor_tensor(av[BOTH, :], gates[BOTH, :], bsum[BOTH, :], ALU.subtract).then_inc(s_gv, 1)
                dve.wait_ge(s_gv, 6)
                total = bsum[BOTH, TT - 1:TT]
                nc.vector.tensor_scalar(av[BOTH, C], av[BOTH, C], total, None, ALU.add).then_inc(s_gv, 1)
                split_q(0)
                for k in range(2):
                    split_k(0, k)
                dve.wait_ge(s_gv, 7)
                nc.vector.reduce_max(mc[:, :], av[BOTH, C], mybir.AxisListType.X).then_inc(s_gv, 1)
                dve.wait_ge(s_gv, 8)
                nc.vector.tensor_tensor(mc[:, :], mc[:, :], total, ALU.max).then_inc(s_gv, 1)
                dve.wait_ge(s_gv, 9)
                nc.vector.tensor_tensor_scan(big[BOTH, X], ones[BOTH, X], av[BOTH, X], mc[:, :], ALU.mult, ALU.max).then_inc(s_gv, 1)
                dve.wait_ge(s_gv, 10)
                nc.vector.tensor_tensor(t1[BOTH, X], big[BOTH, X], bsum[BOTH, X], ALU.add).then_inc(s_gv, 1)
                nc.vector.tensor_scalar(lf[0:32, X], big[0:32, X], -1.0, None, ALU.mult).then_inc(s_gv, 1)
                nc.vector.tensor_scalar(lf[32:64, X][:, ::-1], big[32:64, X], -1.0, None, ALU.mult).then_inc(s_gv, 2)
                for k in (2, 3):
                    split_k(0, k)
                dve.wait_ge(s_c, 4)
                dve.wait_ge(s_gcp, len(TURNS))
                head_cols(0)

                def finish(h, g, k):
                    n = KH * gi(h, g) + k
                    dve.wait_ge(s_ht, n + 1)
                    dve.wait_ge(s_fc[k % 2], 32 * (2 * gi(h, g) + k // 2 + 1))
                    yt = fc[:, k % 2, 0, :]
                    nc.vector.tensor_tensor(yt, ps[:, HB + k % 2, :], yt, ALU.mult).then_inc(s_y, 1)
                    dve.wait_ge(s_y, 2 * n + 1)
                    nc.vector.tensor_tensor(yt, yt, fc[:, k % 2, 1, :], ALU.add).then_inc(s_y, 1)

                def run(h, g, first, last, first_head, last_head):
                    n = gi(h, g)
                    pieces = subs(g)

                    def args(i):
                        t, d, off = pieces[i]
                        if d is not None:
                            return
                        j = t - JT * g
                        if i == NS - JT:
                            dve.wait_ge(s_nm, 32 * (h + 1))
                        dve.wait_ge(s_p, NS * n + i - 1)
                        for dd, c0 in ((0, j * P), (1, BANK)):
                            nc.vector.scalar_tensor_tensor(e[:, i % 2, c0:c0 + P], nm[:, dd, t * P:(t + 1) * P], hc[:, t, dd:dd + 1],
                                                           mask[:, dd, :], ALU.add, ALU.add).then_inc(s_arg, 1)

                    def low(i):
                        t, d, off = pieces[i]
                        w = FULL if d is not None else DIAG
                        dve.wait_ge(s_phi, NS * n + i + 1)
                        nc.vector.tensor_tensor(p_lo[:, off:off + w], pr[:, i % 2, 0:w], p_hi[:, off:off + w].bitcast(F32), ALU.subtract).then_inc(s_plo, 1)

                    def low_v(c):
                        if g == 0:
                            for v in VAT.get(c, ()):
                                k, (t0, nt) = v // 3, VCH[v % 3]
                                dve.wait_ge(s_vhi, NV * h + v + 1)
                                o = (slice(None), slice(t0, t0 + nt), slice(k * P, (k + 1) * P))
                                nc.vector.tensor_tensor(v_lo[o], ps[:, VB + v % VR, 0:nt * P].rearrange("p (t e) -> p t e", e=P), v_hi[o].bitcast(F32), ALU.subtract).then_inc(s_vlo, 1)

                    for i in range(NS):
                        c, end = chunk_of(i)
                        if i + 1 < NS:
                            args(i + 1)
                        dve.wait_ge(s_e, NS * n + i + 1)
                        dve.wait_ge(s_s, NC_ * n + c + 1)
                        if not (first and i < 2):
                            dve.wait_ge(s_acc, NS * n + i - 1)
                            dve.wait_ge(s_plo, NS * n + i - 1)
                        t, d, off = pieces[i]
                        p = nc.vector.tensor_tensor(pr[:, i % 2, 0:BANK], ps[:, c % SB, :], e[:, i % 2, 0:BANK], ALU.mult)
                        if d is None:
                            j = t - JT * g
                            p = nc.vector.tensor_tensor(pr[:, i % 2, BANK:DIAG], ps[:, c % SB, j * P:(j + 1) * P], e[:, i % 2, BANK:DIAG], ALU.mult)
                        p.then_inc(s_p, 1)
                        if i:
                            low(i - 1)
                            cc, ee = chunk_of(i - 1)
                            if cc in TAT and ee and not first:
                                pg = (h if g else h - 1, 1 - g)
                                finish(*pg, TAT.index(cc))
                        if end:
                            low_v(c)
                    low(NS - 1)
                    dve.wait_ge(s_den, n + 1)
                    den = ps[:, HB, 0:2 * JT].rearrange("p (d j) -> p d j", d=2)
                    em_g = em[:, JT * g:JT * (g + 1), :, bass.ds(h, 1)].rearrange("p j d o -> p d (j o)")
                    nc.vector.scalar_tensor_tensor(rn[:, :, :], den, -1.0, em_g, ALU.mult, ALU.max).then_inc(s_nrm, 1)
                    dve.wait_ge(s_nrm, 3 * n + 1)
                    nc.vector.tensor_tensor(rn[:, :, :], den, rn[:, :, :], ALU.max).then_inc(s_nrm, 1)
                    dve.wait_ge(s_nrm, 3 * n + 2)
                    nc.vector.reciprocal(rn[:, :, :], rn[:, :, :]).then_inc(s_nrm, 1)
                    if not last:
                        nc.vector.memset(acc[:, :, :], 0.0).then_inc(s_az, 1)
                        split_q(n + 1)
                    if g == 1 and not last_head:
                        head_cols(h + 1)
                    for j in range(JT):
                        if g == 1 and not last_head:
                            split_k(h + 1, j)
                        m = JT * n + j
                        dve.wait_ge(s_pvf, m + 1)
                        dve.wait_ge(s_pv, 2 * (m + 1))
                        dve.wait_ge(s_nrm, 3 * (n + 1))
                        nc.vector.scalar_tensor_tensor(hs[:, j, :], ps[:, PB + 1 + 2 * (j % 2), :], rn[:, 1, j:j + 1], hs[:, j, :], ALU.mult, ALU.add).then_inc(s_pvb, 1)
                        dve.wait_ge(s_pvb, m + 1)
                        nc.vector.bn_stats(st6[:, j, :], hs[:, j, :]).then_inc(s_hs2, 1)
                    dve.wait_ge(s_hs2, JT * (n + 1))
                    nc.vector.memset(tmp4[:, :], EPS).then_inc(s_hs3, 1)
                    for j in range(JT):
                        nc.vector.bn_aggr(mv[:, j, :], st6[:, j, :]).then_inc(s_hs3, 1)
                    dve.wait_ge(s_hs3, (JT + 1) * (n + 1))
                    nc.vector.tensor_tensor(tmp4[:, :], tmp4[:, :], mv[:, :, 1], ALU.add).then_inc(s_ln, 1)
                    dve.wait_ge(s_st, 2 * (n + 1))
                    dve.wait_ge(s_ln, 5 * n + 1)
                    nc.vector.tensor_tensor(tmp4[:, :], tmp4[:, :], rstd[:, :], ALU.mult).then_inc(s_ln, 1)
                    dve.wait_ge(s_ln, 5 * n + 2)
                    nc.vector.tensor_tensor(tmp4[:, :], tmp4[:, :], rstd[:, :], ALU.mult).then_inc(s_ln, 1)
                    dve.wait_ge(s_ln, 5 * n + 3)
                    nc.vector.tensor_scalar(tmp4[:, :], tmp4[:, :], -0.5, 1.5, ALU.mult, ALU.add).then_inc(s_ln, 1)
                    dve.wait_ge(s_ln, 5 * n + 4)
                    nc.vector.tensor_tensor(rstd[:, :], rstd[:, :], tmp4[:, :], ALU.mult).then_inc(s_ln, 1)
                    dve.wait_ge(s_ln, 5 * n + 5)
                    for j in range(JT):
                        nc.vector.tensor_scalar(hs[:, j, :], hs[:, j, :], mv[:, j, 0:1], rstd[:, j:j + 1], ALU.subtract, ALU.mult).then_inc(s_hn, 1)

                over(dve, HEADS, each_group(run))
                for k in range(KH):
                    finish(HEADS - 1, 1, k)


def out_phase(nc, sem, keep, scr, io, layer):
    ps = keep["ps"]
    last_layer = layer == 1
    n_tiles = NTX if last_layer else NT
    pairs = n_tiles // 2
    WR = 3
    y_src = scr["yT"].rearrange("(k p) t -> p k t", p=P)
    x_in = (io["x"][0], io["ctx"][0]) if not last_layer else (scr["x1"], None)
    dst = io["out"][0] if last_layer else scr["x1"]
    w_src = io["m_w_out" if last_layer else "conv_w_out"][0].rearrange("(k p) n -> k p n", p=P)
    H = D // BANK
    LAG = 3
    with ExitStack() as st:
        sb = lambda n, s, d=F32: st.enter_context(nc.sbuf_tensor(f"c{layer}_{n}", s, d))
        w_hi, w_lo = sb("w_hi", [P, KI, D], F32R), sb("w_lo", [P, KI, D], F32R)
        wr = sb("wr", [P, WR, D])
        yr, y_hi, y_lo = sb("yr", [P, KI, P]), sb("y_hi", [P, 2, KI, P], F32R), sb("y_lo", [P, 2, KI, P], F32R)
        x = sb("x", [P, 2, D])
        bc = sb("bc", [P, 2, D])
        o = sb("o", [P, 1, D])
        ss, ms, rt = sb("ss", [P, 1]), sb("ms", [P, 1]), sb("rt", [P, 1])
        s_w = [sem(f"c{layer}_w_loaded{i}") for i in range(WR)]
        s_x = [sem(f"c{layer}_x_loaded{i}") for i in range(2)]
        s_bc, s_y, s_whi, s_wlo, s_yhi, s_ylo, s_mm, s_ep, s_fin, s_sq, s_st, s_fn = (sem(f"c{layer}_{n}") for n in (
            "bc_loaded", "y_loaded", "w_hi_made", "w_lo_made", "y_hi_made", "y_lo_made", "chunk_done", "gated", "tile_made", "squared", "stored", "final_step"))
        with nc.Block() as block:
            @block.sync
            def _(sp):
                def load_y(t):
                    sp.dma_start(yr[:, :, :], y_src[:, :, bass.ds(t * P, P)]).then_inc(s_y, 16)

                def load_x(t, par, ctx):
                    src = x_in[1 if ctx else 0]
                    sp.dma_start(x[:, par, :], src[bass.ds((t - NTX if ctx else t) * P, P), :]).then_inc(s_x[par], 16)

                load_y(0)
                for k in range(KI):
                    if k >= WR:
                        sp.wait_ge(s_wlo, k - WR + 1)
                    sp.dma_start(wr[:, k % WR, :], w_src[k]).then_inc(s_w[k % WR], 16)
                    if k == 1:
                        sp.wait_ge(s_ylo, 1)
                        load_y(1)
                sp.dma_start(bc[:, 0, :], scr["gates"][layer][0:1, :].to_broadcast([P, D])).then_inc(s_bc, 16)
                second = io["final_g"].rearrange("(o d) -> o d", o=1) if last_layer else scr["gates"][layer][1:2, :]
                sp.dma_start(bc[:, 1, :], second.to_broadcast([P, D])).then_inc(s_bc, 16)
                load_x(0, 0, False)
                load_x(1, 1, False)

                def pair(i, more, ctx_next):
                    for par in range(2):
                        t = 2 * i + par
                        if more:
                            sp.wait_ge(s_ylo, t + 2)
                            load_y(t + 2)
                        sp.wait_ge(s_fin, t + 1)
                        sp.dma_start(dst[bass.ds(t * P, P), :], o[:, 0, :]).then_inc(s_st, 16)
                        if more:
                            load_x(t + 2, par, ctx_next)
                loop = pairs - 1 if last_layer else pairs - 2
                with sp.Fori(0, loop) as i:
                    pair(i, True, False)
                if not last_layer:
                    pair(pairs - 2, True, True)
                pair(pairs - 1, False, False)
                sp.wait_ge(s_st, 16 * n_tiles)

            @block.tensor
            def _(pe):
                def product(par, half, k):
                    cols = slice(half * BANK, (half + 1) * BANK)
                    mm = mm3(nc, ps[:, 2 * par + half, :], y_hi[:, par, k], y_lo[:, par, k], w_hi[:, k, cols], w_lo[:, k, cols], k == 0, k == KI - 1)
                    if k == KI - 1:
                        mm.then_inc(s_mm, 1)

                for at in range(KI + LAG):
                    for par in range(2):
                        k = at - LAG * par
                        if 0 <= k < KI:
                            if k == 0:
                                pe.wait_ge(s_ylo, par + 1)
                            if par == 0:
                                pe.wait_ge(s_wlo, k + 1)
                            for half in range(H):
                                product(par, half, k)
                with pe.Fori(1, pairs) as i:
                    for par in range(2):
                        t = 2 * i + par
                        pe.wait_ge(s_ylo, t + 1)
                        for half in range(H):
                            pe.wait_ge(s_ep, H * (t - 2) + half + 1)
                            for k in range(KI):
                                product(par, half, k)

            @block.scalar
            def _(act):
                def split(t, par):
                    act.wait_ge(s_y, 16 * (t + 1))
                    nc.scalar.activation(y_hi[:, par], yr[:, :, :], ACT.Copy).then_inc(s_yhi, 1)

                split(0, 0)
                for k in range(KI):
                    act.wait_ge(s_w[k % WR], 16 * (k // WR + 1))
                    nc.scalar.activation(w_hi[:, k, :], wr[:, k % WR, :], ACT.Copy).then_inc(s_whi, 1)
                    if k == LAG - 1:
                        split(1, 1)

                def pair(i, more):
                    for par in range(2):
                        t = 2 * i + par
                        if more:
                            act.wait_ge(s_mm, H * (t + 1))
                            split(t + 2, par)
                        if last_layer:
                            act.wait_ge(s_fn, 5 * t + 1)
                            nc.scalar.activation(o[:, 0, :], x[:, par, :], ACT.Square, accum_out=ss[:, :]).then_inc(s_sq, 1)
                            act.wait_ge(s_fn, 5 * t + 2)
                            nc.scalar.activation(rt[:, :], ms[:, :], ACT.Sqrt).then_inc(s_sq, 1)
                with act.Fori(0, pairs - 1) as i:
                    pair(i, True)
                if last_layer:
                    pair(pairs - 1, False)

            @block.vector
            def _(dve):
                def split(t, par):
                    dve.wait_ge(s_yhi, t + 1)
                    nc.vector.tensor_tensor(y_lo[:, par], yr[:, :, :], y_hi[:, par].bitcast(F32), ALU.subtract).then_inc(s_ylo, 1)

                split(0, 0)
                for k in range(KI):
                    dve.wait_ge(s_whi, k + 1)
                    nc.vector.tensor_tensor(w_lo[:, k, :], wr[:, k % WR, :], w_hi[:, k, :].bitcast(F32), ALU.subtract).then_inc(s_wlo, 1)
                    if k == LAG - 1:
                        split(1, 1)
                dve.wait_ge(s_bc, 32)

                def pair(i, first, more, ctx):
                    for par in range(2):
                        t = 2 * i + par
                        dve.wait_ge(s_x[par], 16 * (i + 1))
                        if not (first and par == 0):
                            dve.wait_ge(s_st, 16 * t)
                        for half in range(H):
                            cols = slice(half * BANK, (half + 1) * BANK)
                            dve.wait_ge(s_mm, H * t + half + 1)
                            nc.vector.tensor_tensor(o[:, 0, cols], ps[:, 2 * par + half, :], bc[:, 1 if ctx else 0, cols], ALU.mult).then_inc(s_ep, 1)
                        if more:
                            split(t + 2, par)
                        dve.wait_ge(s_ep, H * (t + 1))
                        if not last_layer:
                            nc.vector.tensor_tensor(o[:, 0, :], o[:, 0, :], x[:, par, :], ALU.add).then_inc(s_fin, 1)
                            continue
                        nc.vector.tensor_tensor(x[:, par, :], o[:, 0, :], x[:, par, :], ALU.add).then_inc(s_fn, 1)
                        dve.wait_ge(s_sq, 2 * t + 1)
                        nc.vector.tensor_scalar(ms[:, :], ss[:, :], 1.0 / D, EPS, ALU.mult, ALU.add).then_inc(s_fn, 1)
                        dve.wait_ge(s_sq, 2 * t + 2)
                        nc.vector.reciprocal(ms[:, :], rt[:, :]).then_inc(s_fn, 2)
                        dve.wait_ge(s_fn, 5 * t + 4)
                        nc.vector.scalar_tensor_tensor(o[:, 0, :], x[:, par, :], ms[:, :], bc[:, 1, :], ALU.mult, ALU.mult).then_inc(s_fin, 1)
                        nc.vector.tensor_copy(rt[:, :], ms[:, :]).then_inc(s_fn, 1)
                pair(0, True, True, False)
                with dve.Fori(1, pairs - 1) as i:
                    pair(i, False, True, False)
                pair(pairs - 1, False, False, not last_layer)


INS = ["x", "c", "ctx", "c_ctx", "norm_g", "mod_w", "mod_b", "conv_w_in", "conv_w", "conv_w_out", "m_w_in", "m_conv_w",
       "m_wq", "m_wk", "m_wv", "m_w_gate", "m_b_gate", "m_norm_g", "m_skip", "m_w_out", "final_g"]


def kernel(**inputs):
    import numpy as np
    import concourse.bacc as bacc
    from concourse.bass_utils import run_bass_kernel_spmd

    nc = bacc.Bacc("TRN2", target_bir_lowering=False, num_devices=1)
    arrays, io = {}, {}
    for name in INS:
        a = np.ascontiguousarray(inputs[name])
        arrays[f"in_{name}"] = a
        io[name] = nc.dram_tensor(f"in_{name}", a.shape, mybir.dt.from_np(a.dtype), kind="ExternalInput").ap()
    io["out"] = nc.dram_tensor("out_0", (1, TX, D), F32, kind="ExternalOutput").ap()
    build(nc, io)
    r = run_bass_kernel_spmd(nc, [arrays], core_ids=[0])
    return r.results[0]["out_0"]
```

```python
import concourse.bass as bass
from concourse import mybir
from contextlib import ExitStack

D = 1024
DI = 2048
TX = 1024
TC = 256
TT = TX + TC
HEADS = 4
DH = DI // HEADS
ROW = 64
EPS = 1e-6
P = 128
KD = D // P
KI = DI // P
KH = DH // P
NT = TT // P
NTX = TX // P
BANK = 512
GROUPS = [(0, 512), (512, 512), (1024, 256)]

F32 = mybir.dt.float32
F32R = mybir.dt.float32r
ALU = mybir.AluOpType
ACT = mybir.ActivationFunctionType

COL_CONV, COL_MCONV, COL_NORM, COL_SKIP, COL_G, COL_C = 0, 48, 96, 112, 128, 144


def over(eng, n, step, last_differs=True):
    step(0, True, False)
    end = n - 1 if last_differs else n
    with eng.Fori(1, end) as i:
        step(i, False, False)
    if last_differs:
        step(n - 1, False, True)


def mm3(nc, out, w_hi, w_lo, x_hi, x_lo, first, last):
    nc.tensor.matmul(out, w_lo, x_hi, start=first, stop=False)
    nc.tensor.matmul(out, w_hi, x_lo, start=False, stop=False)
    return nc.tensor.matmul(out, w_hi, x_hi, start=False, stop=last)


class InputWeights:

    def __init__(self, nc, sem, hold, io, layer):
        self.units = (1, 2, 3, 0) if layer == 0 else (0, 1, 2)
        sb = lambda n, d: hold.enter_context(nc.sbuf_tensor(f"a{layer}_{n}", [P, len(self.units), KD, P], d))
        self.raw, self.hi, self.lo = sb("raw", F32), sb("w_hi", F32R), sb("w_lo", F32R)
        self.s_w = [sem(f"a{layer}_w_loaded{q}") for q in range(len(self.units))]
        self.s_hi, self.s_lo = sem(f"a{layer}_w_hi_made"), sem(f"a{layer}_w_lo_made")
        self.semaphores = (*self.s_w, self.s_hi, self.s_lo)
        self.src = io["conv_w_in" if layer == 0 else "m_w_in"][0].rearrange("(k p) n -> p k n", p=P)
        self.nc = nc

    def load(self, eng, f, q):
        eng.dma_start(self.raw[:, q], self.src[:, :, bass.ds(self.units[q] * DI + f * P, P)]).then_inc(self.s_w[q], 16)

    def split_hi(self, act, f, q):
        act.wait_ge(self.s_w[q], 16 * (f + 1))
        self.nc.scalar.activation(self.hi[:, q], self.raw[:, q], ACT.Copy).then_inc(self.s_hi, 1)

    def split_lo(self, dve, f, q):
        dve.wait_ge(self.s_hi, len(self.units) * f + q + 1)
        self.nc.vector.tensor_tensor(self.lo[:, q], self.raw[:, q], self.hi[:, q].bitcast(F32), ALU.subtract).then_inc(self.s_lo, 1)


def build(nc, io):
    es = ExitStack()
    with es:
        held = []

        def sem(name):
            held.append(nc.alloc_semaphore(name=name))
            return held[-1]

        def end_phase(going_on=()):
            nc.clear_and_free_semaphores([s for s in held if all(s is not g for g in going_on)])
            held[:] = going_on
            nc.all_engine_barrier()

        def dram(name, shape):
            return nc.dram_tensor(name, shape, F32, kind="Internal").ap()

        keep = {
            "ps": es.enter_context(nc.psum_tensor("ps", [P, 8, BANK], F32)),
            "ident": es.enter_context(nc.sbuf_tensor("ident", [P, P], F32)),
            "par": es.enter_context(nc.sbuf_tensor("par", [P, 160], F32)),
            "mod": es.enter_context(nc.sbuf_tensor("mod", [P, 2, 2, 2, KD], F32)),
        }
        scr = {
            "gates": dram("gate_rows", (2, 2, D)),
            "yT": dram("yT", (DI, TT)),
            "x1": dram("x1", (TT, D)),
            "xn1": dram("xn1_rows", (TT, D)),
            "uT": dram("uT", (DI, TT)),
            "ucT": dram("ucT", (DI, TT)),
            "qkvT": dram("qkvT", (3, DI, TT)),
            "ymul": dram("ymul", (DI, TX)),
            "yadd": dram("yadd", (DI, TX)),
            "nmrow": dram("nmrow", (2, HEADS, TX)),
        }
        for layer in range(2):
            with ExitStack() as hold:
                xn = hold.enter_context(nc.sbuf_tensor(f"xn{layer}", [P, NT, D], F32))
                if layer == 0:
                    modulation(nc, sem, keep, scr, io, xn)
                    end_phase()
                h_hi = hold.enter_context(nc.sbuf_tensor(f"h{layer}_hi", [P, KD, TT], F32R))
                h_lo = hold.enter_context(nc.sbuf_tensor(f"h{layer}_lo", [P, KD, TT], F32R))
                w = InputWeights(nc, sem, hold, io, layer)
                norm_phase(nc, sem, keep, scr, layer, xn, h_hi, h_lo, w)
                end_phase(w.semaphores)
                if layer == 0:
                    conv_in_phase(nc, sem, keep, scr, io, h_hi, h_lo, w)
                else:
                    lstm_in_phase(nc, sem, keep, scr, io, h_hi, h_lo, w)
                end_phase()
            if layer == 1:
                with ExitStack() as hold:
                    bg = hold.enter_context(nc.sbuf_tensor("gate_bias", [P, 1], F32))
                    with ExitStack() as inner:
                        early = {n: inner.enter_context(nc.sbuf_tensor(n, [P, w], F32))
                                 for n, w in (("gate_sums", TT), ("ones", TT), ("a_rows", TT), ("av", TT), ("fold", P))}
                        qkv_phase(nc, sem, keep, scr, io, early, bg)
                        end_phase()
                    attention_phase(nc, sem, keep, scr, io, early, bg)
                    end_phase()
            out_phase(nc, sem, keep, scr, io, layer)
            end_phase()


def modulation(nc, sem, keep, scr, io, xn):
    ps, ident, par, mod = keep["ps"], keep["ident"], keep["par"], keep["mod"]
    NCH = 3 * D // BANK
    RING = 3
    XR = 4
    BEHIND = 2
    with ExitStack() as st:
        sb = lambda n, s, d=F32: st.enter_context(nc.sbuf_tensor(n, s, d))
        rows1, rows2 = sb("par_rows1", [P, P]), sb("par_rows2", [32, P])
        sg, sc = sb("sc_sig", [P, 16]), sb("sc", [P, 16])
        w = sb("modw", [P, RING, KD, BANK])
        brow, mrow = sb("mod_brow", [2, 2, 3 * D]), sb("mod_row", [2, 2, 3 * D])
        xs = sb("xs", [P, XR, D])
        ss, ms, rt = sb("ss", [P, NT]), sb("ms", [P, NT]), sb("rt", [P, NT])
        s_x = [sem(f"x_loaded{i}") for i in range(XR)]
        s_ss, s_ms, s_rt, s_rs, s_xn = (sem(f"x_{n}") for n in ("squared", "mean", "root", "rsqrt", "scaled"))
        x_tiles = [io["x"][0, t * P:(t + 1) * P, :] for t in range(NTX)] + [io["ctx"][0, t * P:(t + 1) * P, :] for t in range(TC // P)]
        s_id, s_par, s_tp, s_cp, s_sg, s_sc = (sem(n) for n in ("id_made", "par_loaded", "par_turned", "par_copied", "sc_sigmoid", "sc_made"))
        s_w = [sem(f"modw_loaded{i}") for i in range(RING)]
        s_mm, s_row, s_tr, s_col, s_b, s_out = (sem(n) for n in ("mod_product", "mod_row_made", "mod_turned", "mod_col_made", "modb_loaded", "gate_stored"))

        def wsrc(l, n):
            return io["mod_w"][l].rearrange("(k p) n -> p k n", p=P)[:, :, n * BANK:(n + 1) * BANK]

        with nc.Block() as block:
            @block.sync
            def _(sp):
                for src, r0, n in ((io["conv_w"], 0, 48), (io["m_conv_w"], 48, 48)):
                    sp.dma_start(rows1[r0:r0 + n, :], src[0].rearrange("j (f p) -> (j f) p", p=P)).then_inc(s_par, 16)
                for src, r0 in ((io["m_norm_g"], 96), (io["m_skip"], 112)):
                    sp.dma_start(rows1[r0:r0 + 16, :], src[0].rearrange("(f p) -> f p", p=P)).then_inc(s_par, 16)
                sp.dma_start(rows2[0:16, :], io["norm_g"].rearrange("l (k p) -> (l k) p", p=P)).then_inc(s_par, 16)
                sp.dma_start(rows2[16:24, :], io["c"][0].rearrange("(k p) -> k p", p=P)).then_inc(s_par, 16)
                sp.dma_start(rows2[24:32, :], io["c_ctx"].rearrange("(k p) -> k p", p=P)).then_inc(s_par, 16)
                for r in range(2):
                    sp.dma_start(brow[r:r + 1, :, :], io["mod_b"].rearrange("(o l) n -> o l n", o=1)).then_inc(s_b, 16)
                for i in range(2 * NCH):
                    if i >= RING:
                        sp.wait_ge(s_mm, i - RING + 1)
                    sp.dma_start(w[:, i % RING], wsrc(i // NCH, i % NCH)).then_inc(s_w[i % RING], 16)
                    t = i - BEHIND
                    if 0 <= t < NT:
                        if t >= XR:
                            sp.wait_ge(s_xn, t - XR + 1)
                        sp.dma_start(xs[:, t % XR, :], x_tiles[t]).then_inc(s_x[t % XR], 16)
                for l in range(2):
                    sp.wait_ge(s_row, NCH * (l + 1))
                    sp.dma_start(scr["gates"][l], mrow[:, l, 2 * D:3 * D]).then_inc(s_out, 16)
                sp.wait_ge(s_out, 32)

            @block.gpsimd
            def _(pool):
                nc.gpsimd.memset(ident[:, :], 0.0).then_inc(s_id, 1)
                pool.wait_ge(s_id, 1)
                nc.gpsimd.affine_select(out=ident[:, :], in_=ident[:, :], compare_op=ALU.not_equal, fill=1.0, base=0,
                                        pattern=[[-1, P]], channel_multiplier=1).then_inc(s_id, 1)

            @block.tensor
            def _(pe):
                pe.wait_ge(s_id, 2)
                pe.wait_ge(s_par, 16 * 7)
                nc.tensor.transpose(ps[:, 0, 0:P], rows1[:, :], ident[:, :]).then_inc(s_tp, 1)
                nc.tensor.transpose(ps[:, 1, 0:32], rows2[:, :], ident[0:32, 0:32]).then_inc(s_tp, 1)
                pe.wait_ge(s_sc, 1)
                for i in range(2 * NCH):
                    pe.wait_ge(s_w[i % RING], 16 * (i // RING + 1))
                    if i >= 4:
                        pe.wait_ge(s_row, i - 3)
                    for k in range(KD):
                        mm = nc.tensor.matmul(ps[0:2, 2 + i % 4, :], sc[:, k:16:KD], w[:, i % RING, k, :], start=(k == 0), stop=(k == KD - 1))
                    mm.then_inc(s_mm, 1)
                for l in range(2):
                    pe.wait_ge(s_row, NCH * (l + 1))
                    for j in range(2 * KD):
                        tr = nc.tensor.transpose(ps[:, l, 2 * j:2 * j + 2], mrow[:, l, j * P:(j + 1) * P], ident[0:2, 0:2])
                    tr.then_inc(s_tr, 1)

            @block.scalar
            def _(act):
                act.wait_ge(s_tp, 2)
                nc.scalar.activation(par[:, 0:P], ps[:, 0, 0:P], ACT.Copy).then_inc(s_cp, 1)
                nc.scalar.activation(par[:, P:160], ps[:, 1, 0:32], ACT.Copy).then_inc(s_cp, 1)
                act.wait_ge(s_cp, 2)
                nc.scalar.activation(sg[:, :], par[:, COL_C:COL_C + 16], ACT.Sigmoid).then_inc(s_sg, 1)
                for t in range(NT):
                    act.wait_ge(s_x[t % XR], 16 * (t // XR + 1))
                    nc.scalar.activation(xn[:, t, :], xs[:, t % XR, :], ACT.Square, accum_out=ss[:, t:t + 1]).then_inc(s_ss, 1)
                    act.wait_ge(s_ms, t + 1)
                    nc.scalar.activation(rt[:, t:t + 1], ms[:, t:t + 1], ACT.Sqrt).then_inc(s_rt, 1)

            @block.vector
            def _(dve):
                dve.wait_ge(s_sg, 1)
                nc.vector.tensor_tensor(sc[:, :], sg[:, :], par[:, COL_C:COL_C + 16], ALU.mult).then_inc(s_sc, 1)
                def divide(t):
                    dve.wait_ge(s_ss, t + 1)
                    nc.vector.tensor_scalar(ms[:, t:t + 1], ss[:, t:t + 1], 1.0 / D, EPS, ALU.mult, ALU.add).then_inc(s_ms, 1)
                    dve.wait_ge(s_rt, t + 1)
                    nc.vector.reciprocal(ss[:, t:t + 1], rt[:, t:t + 1]).then_inc(s_rs, 1)
                    dve.wait_ge(s_rs, t + 1)
                    nc.vector.tensor_scalar(xn[:, t, :], xs[:, t % XR, :], ss[:, t:t + 1], None, ALU.mult).then_inc(s_xn, 1)

                dve.wait_ge(s_b, 32)
                for i in range(2 * NCH):
                    l, n = i // NCH, i % NCH
                    dve.wait_ge(s_mm, i + 1)
                    nc.vector.tensor_tensor(mrow[:, l, n * BANK:(n + 1) * BANK], ps[0:2, 2 + i % 4, :],
                                            brow[:, l, n * BANK:(n + 1) * BANK], ALU.add).then_inc(s_row, 1)
                    if i > BEHIND:
                        divide(i - BEHIND - 1)
                divide(NT - 1)
                for l in range(2):
                    dve.wait_ge(s_tr, l + 1)
                    for s in range(2):
                        g = par[:, COL_G + KD * l:COL_G + KD * (l + 1)]
                        nc.vector.tensor_copy(mod[:, l, 1, s, :], ps[:, l, s:2 * KD:2]).then_inc(s_col, 1)
                        nc.vector.scalar_tensor_tensor(mod[:, l, 0, s, :], ps[:, l, 2 * KD + s:4 * KD:2], 1.0, g, ALU.add, ALU.mult).then_inc(s_col, 1)


def norm_phase(nc, sem, keep, scr, layer, xn, h_hi, h_lo, w):
    ps, ident, mod = keep["ps"], keep["ident"], keep["mod"]
    GT = [(0, 4), (4, 4), (8, 2)]
    HR = 4
    with ExitStack() as st:
        hf = st.enter_context(nc.sbuf_tensor(f"n{layer}_hf", [P, HR, BANK], F32))
        s_x = [sem(f"n{layer}_x_loaded{g}") for g in range(len(GT))]
        s_tr, s_hf, s_hi, s_hid, s_lo = (sem(f"n{layer}_{n}") for n in ("turned", "modulated", "odd_hi_made", "even_hi_made", "lo_made"))

        def chunks():
            n = 0
            for g, (t0, nt) in enumerate(GT):
                for k in range(KD):
                    yield n, g, t0, nt, k
                    n += 1

        with nc.Block() as block:
            @block.sync
            def _(sp):
                if layer == 1:
                    tiles = scr["xn1"].rearrange("(t p) d -> t p d", p=P)
                    for g, (t0, nt) in enumerate(GT):
                        for t in range(t0, t0 + nt):
                            sp.dma_start(xn[:, t, :], tiles[t]).then_inc(s_x[g], 16)
                for q in range(len(w.units)):
                    w.load(sp, 0, q)

            @block.tensor
            def _(pe):
                for n, g, t0, nt, k in chunks():
                    if layer == 1 and k == 0:
                        pe.wait_ge(s_x[g], 16 * nt)
                    if n >= HR:
                        pe.wait_ge(s_hf, n - HR + 1)
                    for i in range(nt):
                        tr = nc.tensor.transpose(ps[:, n % HR, i * P:(i + 1) * P], xn[:, t0 + i, k * P:(k + 1) * P], ident[:, :])
                    tr.then_inc(s_tr, 1)

            @block.scalar
            def _(act):
                for n, g, t0, nt, k in chunks():
                    s = 0 if g < 2 else 1
                    act.wait_ge(s_tr, n + 1)
                    if n >= HR:
                        act.wait_ge(s_lo, n - HR + 1)
                    nc.scalar.activation(hf[:, n % HR, 0:nt * P], ps[:, n % HR, 0:nt * P], ACT.Identity,
                                         bias=mod[:, layer, 1, s, k:k + 1], scale=mod[:, layer, 0, s, k:k + 1]).then_inc(s_hf, 1)
                    if n % 2:
                        act.wait_ge(s_hf, n + 1)
                        nc.scalar.activation(h_hi[:, k, t0 * P:(t0 + nt) * P], hf[:, n % HR, 0:nt * P], ACT.Copy).then_inc(s_hi, 1)
                    if n >= 2 * KD - len(w.units) and g == 1:
                        w.split_hi(act, 0, n - 2 * KD + len(w.units))

            @block.vector
            def _(dve):
                for n, g, t0, nt, k in chunks():
                    cols = slice(t0 * P, (t0 + nt) * P)
                    if n % 2 == 0:
                        dve.wait_ge(s_hf, n + 1)
                        nc.vector.tensor_copy(h_hi[:, k, cols], hf[:, n % HR, 0:nt * P]).then_inc(s_hid, 1)
                        dve.wait_ge(s_hid, n // 2 + 1)
                    else:
                        dve.wait_ge(s_hi, n // 2 + 1)
                    nc.vector.tensor_tensor(h_lo[:, k, cols], hf[:, n % HR, 0:nt * P], h_hi[:, k, cols].bitcast(F32), ALU.subtract).then_inc(s_lo, 1)
                    if n >= 2 * KD - len(w.units) and g == 1:
                        w.split_lo(dve, 0, n - 2 * KD + len(w.units))


def conv_taps(nc, dve, out, x, par, col0, f, s_done, base):
    tap = lambda j: par[:, bass.ds(col0 + j * KI + f, 1)]
    nc.vector.tensor_scalar(out[:, :], x[:, :], tap(1), None, ALU.mult).then_inc(s_done, 1)
    xr, orow = (a[:, 0:TX].rearrange("p (r c) -> p r c", c=ROW) for a in (x, out))
    dve.wait_ge(s_done, base + 1)
    nc.vector.scalar_tensor_tensor(orow[:, :, 1:], xr[:, :, :-1], tap(0), orow[:, :, 1:], ALU.mult, ALU.add).then_inc(s_done, 1)
    nc.vector.scalar_tensor_tensor(out[:, TX + 1:], x[:, TX:TT - 1], tap(0), out[:, TX + 1:], ALU.mult, ALU.add).then_inc(s_done, 1)
    dve.wait_ge(s_done, base + 3)
    nc.vector.scalar_tensor_tensor(orow[:, :, :-1], xr[:, :, 1:], tap(2), orow[:, :, :-1], ALU.mult, ALU.add).then_inc(s_done, 1)
    nc.vector.scalar_tensor_tensor(out[:, TX:TT - 1], x[:, TX + 1:], tap(2), out[:, TX:TT - 1], ALU.mult, ALU.add).then_inc(s_done, 1)


def conv_in_phase(nc, sem, keep, scr, io, h_hi, h_lo, w):
    ps, par = keep["ps"], keep["par"]
    U, G = len(w.units), len(GROUPS)
    w_hi, w_lo, s_lo = w.hi, w.lo, w.s_lo
    CH = U * G
    R = 6
    y_dst = scr["yT"].rearrange("(f p) t -> f p t", p=P)
    with ExitStack() as st:
        sb = lambda n, s, d=F32: st.enter_context(nc.sbuf_tensor(f"a0_{n}", s, d))
        ev = sb("ev", [P, U, TT])
        sg, cu, cv = sb("sg", [P, TT]), sb("cu", [P, TT]), sb("cv", [P, TT])
        y = cu
        s_mm, s_ev, s_sg, s_ew, s_y, s_st = (sem(f"a0_{n}") for n in (
            "chunk_done", "chunk_read", "sigmoid", "mixed", "y_made", "y_stored"))
        EW = 8
        with nc.Block() as block:
            @block.sync
            def _(sp):
                def store(f):
                    sp.wait_ge(s_y, f + 1)
                    sp.dma_start(y_dst[bass.ds(f, 1)].rearrange("a p t -> p (a t)"), y[:, :]).then_inc(s_st, 16)

                def step(f, first, last):
                    nxt = f + 1 if first or last else sp.snap(f + 1)
                    if not last:
                        for q in range(U):
                            if q < U - 2:
                                sp.wait_ge(s_lo, U * f + q + 1)
                            elif q == U - 2:
                                sp.wait_ge(s_lo, U * f + U)
                            w.load(sp, nxt, q)
                    if not first:
                        store(f - 1)
                over(sp, KI, step)
                store(KI - 1)
                sp.wait_ge(s_st, 16 * KI)

            @block.tensor
            def _(pe):
                def step(f, first, last):
                    for q in range(U):
                        pe.wait_ge(s_lo, U * f + q + 1)
                        for g, (t0, n) in enumerate(GROUPS):
                            c = q * G + g
                            if not (first and c < R):
                                pe.wait_ge(s_ev, CH * f + c - R + 1)
                            out = ps[:, c % R, 0:n]
                            for k in range(KD):
                                mm = mm3(nc, out, w_hi[:, q, k], w_lo[:, q, k], h_hi[:, k, t0:t0 + n], h_lo[:, k, t0:t0 + n], k == 0, k == KD - 1)
                            mm.then_inc(s_mm, 1)
                over(pe, KI, step, last_differs=False)

            @block.scalar
            def _(act):
                def step(f, first, last):
                    for q in range(U):
                        if not first:
                            act.wait_ge(s_ew, EW * (f - 1) + (6, 6, 7, 8)[q])
                        for g, (t0, n) in enumerate(GROUPS):
                            c = q * G + g
                            act.wait_ge(s_mm, CH * f + c + 1)
                            if q == 2:
                                nc.scalar.activation(sg[:, t0:t0 + n], ps[:, c % R, 0:n], ACT.Sigmoid).then_inc(s_sg, 1)
                            nc.scalar.activation(ev[:, q, t0:t0 + n], ps[:, c % R, 0:n], ACT.Copy).then_inc(s_ev, 1)
                        if not last:
                            w.split_hi(act, f + 1, q)
                over(act, KI, step)

            @block.vector
            def _(dve):
                def step(f, first, last):
                    if not last:
                        w.split_lo(dve, f + 1, 0)
                    dve.wait_ge(s_ev, CH * f + 2 * G)
                    if not first:
                        dve.wait_ge(s_st, 16 * f)
                    nc.vector.tensor_tensor(cu[:, :], ev[:, 0, :], ev[:, 1, :], ALU.mult).then_inc(s_ew, 1)
                    dve.wait_ge(s_ew, EW * f + 1)
                    conv_taps(nc, dve, cv, cu, par, COL_CONV, f, s_ew, EW * f + 1)
                    if not last:
                        w.split_lo(dve, f + 1, 1)
                    dve.wait_ge(s_ev, CH * f + 3 * G)
                    dve.wait_ge(s_sg, G * (f + 1))
                    dve.wait_ge(s_ew, EW * f + 6)
                    nc.vector.tensor_tensor(ev[:, 2, :], ev[:, 2, :], sg[:, :], ALU.mult).then_inc(s_ew, 1)
                    dve.wait_ge(s_ew, EW * f + 7)
                    nc.vector.tensor_tensor(cv[:, :], cv[:, :], ev[:, 2, :], ALU.mult).then_inc(s_ew, 1)
                    if not last:
                        w.split_lo(dve, f + 1, 2)
                    dve.wait_ge(s_ev, CH * (f + 1))
                    dve.wait_ge(s_ew, EW * f + 8)
                    nc.vector.tensor_tensor(y[:, :], cv[:, :], ev[:, 3, :], ALU.mult).then_inc(s_y, 1)
                    if not last:
                        w.split_lo(dve, f + 1, 3)
                over(dve, KI, step)


def lstm_in_phase(nc, sem, keep, scr, io, h_hi, h_lo, w):
    ps, par = keep["ps"], keep["par"]
    U = len(w.units)
    w_hi, w_lo, s_lo = w.hi, w.lo, w.s_lo
    GR = (GROUPS, GROUPS[:2], GROUPS[:2])
    CH = sum(len(g) for g in GR)
    FIRST = (0, 3, 5)
    R = CH
    by_tile = lambda a: a.rearrange("(f p) t -> f p t", p=P)
    dst = [by_tile(scr[n]) for n in ("uT", "ucT", "ymul", "yadd")]
    with ExitStack() as st:
        sb = lambda n, s, d=F32: st.enter_context(nc.sbuf_tensor(f"a1_{n}", s, d))
        u, cv, sc, uc = sb("u", [P, TT]), sb("cv", [P, TT]), sb("sc", [P, TT]), sb("uc", [P, TT])
        z, sz, so, mul, add = (sb(n, [P, TX]) for n in ("z", "sz", "so", "mul", "add"))
        out_tiles = (u, uc, mul, add)
        s_mm, s_ev, s_cv, s_scv, s_ew, s_st = (sem(f"a1_{n}") for n in (
            "chunk_done", "chunk_read", "conv_round", "conv_sigmoid", "mixed", "stored"))
        s_uo = sem("a1_u_stored")
        EW = 5
        with nc.Block() as block:
            @block.sync
            def _(sp):
                def store(f):
                    sp.wait_ge(s_ev, CH * f + 3)
                    sp.dma_start(dst[0][bass.ds(f, 1)].rearrange("a p t -> p (a t)"), u[:, :]).then_inc(s_uo, 16)
                    sp.wait_ge(s_ew, EW * (f + 1))
                    for i in range(1, 4):
                        sp.dma_start(dst[i][bass.ds(f, 1)].rearrange("a p t -> p (a t)"), out_tiles[i][:, :]).then_inc(s_st, 16)

                def step(f, first, last):
                    nxt = f + 1 if first or last else sp.snap(f + 1)
                    if not last:
                        for q in range(U):
                            sp.wait_ge(s_lo, U * f + q + 1)
                            w.load(sp, nxt, q)
                    if not first:
                        store(f - 1)
                over(sp, KI, step)
                store(KI - 1)
                sp.wait_ge(s_uo, 16 * KI)
                sp.wait_ge(s_st, 48 * KI)

            @block.tensor
            def _(pe):
                def step(f, first, last):
                    for q in range(U):
                        pe.wait_ge(s_lo, U * f + q + 1)
                        for g, (t0, n) in enumerate(GR[q]):
                            c = FIRST[q] + g
                            if not first:
                                pe.wait_ge(s_ev, CH * f + c - R + 1)
                            out = ps[:, c, 0:n]
                            for k in range(KD):
                                mm = mm3(nc, out, w_hi[:, q, k], w_lo[:, q, k], h_hi[:, k, t0:t0 + n], h_lo[:, k, t0:t0 + n], k == 0, k == KD - 1)
                            mm.then_inc(s_mm, 1)
                over(pe, KI, step, last_differs=False)

            @block.scalar
            def _(act):
                def step(f, first, last):
                    if not first:
                        act.wait_ge(s_uo, 16 * f)
                        act.wait_ge(s_cv, 5 * f)
                    for g, (t0, n) in enumerate(GR[0]):
                        act.wait_ge(s_mm, CH * f + g + 1)
                        nc.scalar.activation(u[:, t0:t0 + n], ps[:, g, 0:n], ACT.Copy).then_inc(s_ev, 1)
                    if not last:
                        w.split_hi(act, f + 1, 0)
                    act.wait_ge(s_cv, 5 * (f + 1))
                    if not first:
                        act.wait_ge(s_ew, EW * f)
                    nc.scalar.activation(sc[:, :], cv[:, :], ACT.Sigmoid).then_inc(s_scv, 1)
                    for g, (t0, n) in enumerate(GR[1]):
                        c = FIRST[1] + g
                        act.wait_ge(s_mm, CH * f + c + 1)
                        nc.scalar.activation(sz[:, t0:t0 + n], ps[:, c, 0:n], ACT.Sigmoid).then_inc(s_scv, 1)
                        nc.scalar.activation(z[:, t0:t0 + n], ps[:, c, 0:n], ACT.Copy).then_inc(s_ev, 1)
                    if not last:
                        w.split_hi(act, f + 1, 1)
                    for g, (t0, n) in enumerate(GR[2]):
                        c = FIRST[2] + g
                        act.wait_ge(s_mm, CH * f + c + 1)
                        nc.scalar.activation(so[:, t0:t0 + n], ps[:, c, 0:n], ACT.Sigmoid).then_inc(s_ev, 1)
                    if not last:
                        w.split_hi(act, f + 1, 2)
                over(act, KI, step)

            @block.vector
            def _(dve):
                def step(f, first, last):
                    dve.wait_ge(s_ev, CH * f + 3)
                    if not first:
                        dve.wait_ge(s_ew, EW * f)
                    conv_taps(nc, dve, cv, u, par, COL_MCONV, f, s_cv, 5 * f)
                    if not last:
                        w.split_lo(dve, f + 1, 0)
                    dve.wait_ge(s_cv, 5 * (f + 1))
                    dve.wait_ge(s_scv, 3 * f + 1)
                    if not first:
                        dve.wait_ge(s_st, 48 * f)
                    nc.vector.tensor_tensor(uc[:, :], cv[:, :], sc[:, :], ALU.mult).then_inc(s_ew, 1)
                    dve.wait_ge(s_ev, CH * f + 5)
                    dve.wait_ge(s_scv, 3 * f + 3)
                    nc.vector.tensor_tensor(z[:, :], z[:, :], sz[:, :], ALU.mult).then_inc(s_ew, 1)
                    if not last:
                        w.split_lo(dve, f + 1, 1)
                    dve.wait_ge(s_ew, EW * f + 2)
                    nc.vector.scalar_tensor_tensor(add[:, :], uc[:, 0:TX], par[:, bass.ds(COL_SKIP + f, 1)], z[:, :], ALU.mult, ALU.mult).then_inc(s_ew, 1)
                    dve.wait_ge(s_ev, CH * (f + 1))
                    nc.vector.scalar_tensor_tensor(mul[:, :], so[:, :], par[:, bass.ds(COL_NORM + f, 1)], z[:, :], ALU.mult, ALU.mult).then_inc(s_ew, 2)
                    if not last:
                        w.split_lo(dve, f + 1, 2)
                over(dve, KI, step)


def qkv_phase(nc, sem, keep, scr, io, early, bg):
    ps = keep["ps"]
    UN = 6
    RS = 3
    EB = 2
    G = len(GROUPS)
    CH = UN * EB * G
    R = 4
    TILES = UN * EB
    RT = 3
    XS = 4
    U_SPLITS, UC_SPLITS = {0: (4,), 1: (5,), 2: (6, 7)}, {3: (0, 1), 4: (2, 3)}
    X_LOADS = {1: (0,), 2: (1,), 3: (2, 3), 4: (4, 5), 5: (6, 7)}
    CR = 4
    LAG = 3
    SCALE = float(DH) ** -0.5
    w_src = [io[n][0].rearrange("h (k p) e -> h p k e", p=P) for n in ("m_wq", "m_wk", "m_wv")]
    x_src = [scr[n].rearrange("(f p) t -> f p t", p=P) for n in ("ucT", "uT")]
    dst = scr["qkvT"].rearrange("m (f p) t -> m f p t", p=P)
    KINDS = (0, 2, 1, 3)
    with ExitStack() as st:
        sb = lambda n, s, d=F32: st.enter_context(nc.sbuf_tensor(f"q_{n}", s, d))
        raw, w_hi, w_lo = sb("raw", [P, RS, KH, EB * P]), sb("w_hi", [P, RS, KH, EB * P], F32R), sb("w_lo", [P, RS, KH, EB * P], F32R)
        xr = sb("xr", [P, XS, TT])
        x_hi, x_lo = sb("x_hi", [P, 2, KH, TT], F32R), sb("x_lo", [P, 2, KH, TT], F32R)
        wg = sb("wg", [P, 3, HEADS * KH, 4 * HEADS])
        wgp, wgr = sb("wgp", [P, TILES, P]), sb("wgr", [P, TILES, P], F32R)
        tile = sb("tile", [P, RT, TT])
        t_hi, t_lo = sb("t_hi", [P, CR, BANK], F32R), sb("t_lo", [P, CR, BANK], F32R)
        s_w = [sem(f"q_w_loaded{i}") for i in range(RS)]
        s_xr = [sem(f"q_x_loaded{i}") for i in range(XS)]
        s_st = [sem(f"q_tile_stored{i}") for i in range(RT)]
        s_hi, s_lo, s_xhi, s_xlo, s_mm, s_ev, s_thi, s_tlo, s_g, s_gr, s_wg, s_wgz, s_wgp, s_wgh, s_wgl, s_bz, s_c = (sem(f"q_{n}") for n in (
            "w_hi_made", "w_lo_made", "x_hi_made", "x_lo_made", "chunk_done", "chunk_read", "chunk_hi_made", "chunk_lo_made",
            "gates_done", "gates_read", "gate_w_loaded", "gate_w_cleared", "gate_w_placed", "gate_w_hi_made", "gate_w_lo_made",
            "bias_cleared", "constants"))

        def xwhich(h, j):
            return x_src[j // KH][bass.ds(h * KH + j % KH, 1)].rearrange("a p t -> p (a t)")

        with nc.Block() as block:
            @block.sync
            def _(sp):
                def load_w(h, n):
                    m, e0 = n // 2, (n % 2) * EB * P
                    sp.dma_start(raw[:, n % RS], w_src[m][bass.ds(h, 1), :, :, e0:e0 + EB * P].rearrange("a p k e -> p (a k) e")).then_inc(s_w[n % RS], 16)

                def load_x(h, j):
                    sp.dma_start(xr[:, j % XS], xwhich(h, j)).then_inc(s_xr[j % XS], 16)

                for j in range(KH):
                    load_x(0, j)
                load_w(0, 0)
                sp.dma_start(wg[:, :, :, :], io["m_w_gate"][0].rearrange("(m f p) c -> p m f c", m=3, p=P)).then_inc(s_wg, 16)
                sp.wait_ge(s_bz, 1)
                for q, kind in enumerate(KINDS):
                    sp.dma_start(bg[32 * kind:32 * kind + HEADS, :], io["m_b_gate"][0, q * HEADS:(q + 1) * HEADS].rearrange("(h o) -> h o", o=1)).then_inc(s_wg, 16)
                load_w(0, 1)
                load_w(0, 2)
                for j in range(KH, 2 * KH):
                    sp.wait_ge(s_xlo, j - KH + 1)
                    load_x(0, j)

                def step(h, first, last):
                    for n in range(UN):
                        if n + RS < UN or not last:
                            if n != 2:
                                sp.wait_ge(s_lo, UN * h + (n + 1 if n != 1 else 3))
                            if n + RS >= UN:
                                load_w(h + 1, n + RS - UN)
                            elif n == 1:
                                load_w(h, 5)
                                load_w(h, 4)
                            elif n != 2:
                                load_w(h, n + RS)
                        if not last:
                            for j in X_LOADS.get(n, ()):
                                sp.wait_ge(s_xlo, 8 * h + KH + j + 1)
                                load_x(h + 1, j)
                        for e in range(EB):
                            t = n * EB + e
                            sp.wait_ge(s_ev, CH * h + (t + 1) * G)
                            sp.dma_start(dst[n // 2][bass.ds(h * KH + t % KH, 1)].rearrange("a p t -> p (a t)"), tile[:, t % RT, :]).then_inc(s_st[t % RT], 16)
                over(sp, HEADS, step)
                for i in range(RT):
                    sp.wait_ge(s_st[i], 16 * HEADS * TILES // RT)

            @block.gpsimd
            def _(pool):
                fold = early["fold"][:, :]
                nc.gpsimd.memset(bg[:, :], 0.0).then_inc(s_bz, 1)
                nc.gpsimd.memset(fold, 0.0).then_inc(s_c, 1)
                nc.gpsimd.memset(early["ones"][:, :], 1.0).then_inc(s_c, 1)
                nc.gpsimd.memset(early["a_rows"][:, :], 0.0).then_inc(s_c, 1)
                for i, below in enumerate((0, 16)):
                    pool.wait_ge(s_c, 3 + i)
                    nc.gpsimd.affine_select(out=fold, in_=fold, compare_op=ALU.not_equal, fill=1.0, base=-below,
                                            pattern=[[-1, P]], channel_multiplier=1).then_inc(s_c, 1)

            @block.tensor
            def _(pe):
                def gate_products(h, c, first, last):
                    t, g = c // G, c % G
                    nn = GROUPS[g][1]
                    pe.wait_ge(s_tlo, CH * h + c + 1)
                    if t % KH == 0 and g == 0:
                        pe.wait_ge(s_wgl, 3 * h + t // KH + 1)
                    nc.tensor.matmul(ps[:, R + g, 0:nn], wgr[:, t, :], t_lo[:, c % CR, 0:nn], start=first and t == 0, stop=False)
                    nc.tensor.matmul(ps[:, R + g, 0:nn], wgr[:, t, :], t_hi[:, c % CR, 0:nn], start=False, stop=last and t == TILES - 1).then_inc(s_g, 1)

                def step(h, first, last):
                    for n in range(UN):
                        pe.wait_ge(s_lo, UN * h + n + 1)
                        src = 0 if n < 4 else 1
                        if n == 0:
                            pe.wait_ge(s_xlo, 8 * h + KH)
                        if n == 4:
                            pe.wait_ge(s_xlo, 8 * h + 2 * KH)
                        for e in range(EB):
                            for g, (t0, nn) in enumerate(GROUPS):
                                c = (n * EB + e) * G + g
                                if not (first and c < R):
                                    pe.wait_ge(s_ev, CH * h + c - R + 1)
                                for k in range(KH):
                                    mm = mm3(nc, ps[:, c % R, 0:nn], w_hi[:, n % RS, k, e * P:(e + 1) * P], w_lo[:, n % RS, k, e * P:(e + 1) * P],
                                             x_hi[:, src, k, t0:t0 + nn], x_lo[:, src, k, t0:t0 + nn], k == 0, k == KH - 1)
                                mm.then_inc(s_mm, 1)
                                if c >= LAG:
                                    gate_products(h, c - LAG, first, last)
                                elif not first:
                                    gate_products(h - 1, CH - LAG + c, False, False)
                over(pe, HEADS, step)
                for c in range(CH - LAG, CH):
                    gate_products(HEADS - 1, c, False, True)

            @block.scalar
            def _(act):
                def split_w(h, n):
                    act.wait_ge(s_w[n % RS], 32 * h + 16 * (n // RS + 1))
                    nc.scalar.activation(w_hi[:, n % RS], raw[:, n % RS], ACT.Copy).then_inc(s_hi, 1)

                def split_x(h, j):
                    act.wait_ge(s_xr[j % XS], 32 * h + 16 * (j // XS + 1))
                    nc.scalar.activation(x_hi[:, j // KH, j % KH, :], xr[:, j % XS, :], ACT.Copy).then_inc(s_xhi, 1)

                def round_gate_w(h, m, first):
                    act.wait_ge(s_wgp, 4 * (3 * h + m + 1))
                    if not first:
                        act.wait_ge(s_g, CH * (h - 1) + KH * (m + 1) * G)
                    nc.scalar.activation(wgr[:, KH * m:KH * (m + 1), :], wgp[:, KH * m:KH * (m + 1), :], ACT.Copy).then_inc(s_wgh, 1)

                for j in range(KH):
                    split_x(0, j)
                for n in range(RS):
                    split_w(0, n)
                for m in range(3):
                    round_gate_w(0, m, True)
                for j in range(KH, 2 * KH):
                    split_x(0, j)

                def step(h, first, last):
                    for n in range(UN):
                        for c in range(n * EB * G, (n + 1) * EB * G):
                            t, g = c // G, c % G
                            t0, nn = GROUPS[g]
                            act.wait_ge(s_mm, CH * h + c + 1)
                            if g == 0 and not (first and t < RT):
                                act.wait_ge(s_st[t % RT], 16 * ((TILES // RT) * h + t // RT))
                                act.wait_ge(s_tlo, CH * h + (t - RT + 1) * G)
                            nc.scalar.activation(tile[:, t % RT, t0:t0 + nn], ps[:, c % R, 0:nn], ACT.Copy,
                                                 scale=SCALE if n // 2 == 1 else 1.0).then_inc(s_ev, 1)
                            act.wait_ge(s_ev, CH * h + c + 1)
                            if not (first and c < CR):
                                act.wait_ge(s_g, CH * h + c - CR + 1)
                            nc.scalar.activation(t_hi[:, c % CR, 0:nn], tile[:, t % RT, t0:t0 + nn], ACT.Copy).then_inc(s_thi, 1)
                        if n + RS < UN:
                            split_w(h, n + RS)
                        elif not last:
                            split_w(h + 1, n + RS - UN)
                        if n == 0 and not first:
                            round_gate_w(h, 2, False)
                        if n in (2, 4) and not last:
                            round_gate_w(h + 1, n // 2 - 1, False)
                        if not first:
                            for j in U_SPLITS.get(n, ()):
                                split_x(h, j)
                        if not last:
                            for j in UC_SPLITS.get(n, ()):
                                split_x(h + 1, j)
                over(act, HEADS, step)
                act.wait_ge(s_g, CH * HEADS)
                for g in (0, 2):
                    t0, nn = GROUPS[g]
                    nc.scalar.activation(early["gate_sums"][:, t0:t0 + nn], ps[:, R + g, 0:nn], ACT.Copy).then_inc(s_gr, 1)

            @block.vector
            def _(dve):
                def split_w(h, n):
                    dve.wait_ge(s_hi, UN * h + n + 1)
                    nc.vector.tensor_tensor(w_lo[:, n % RS], raw[:, n % RS], w_hi[:, n % RS].bitcast(F32), ALU.subtract).then_inc(s_lo, 1)

                def split_x(h, j):
                    dve.wait_ge(s_xhi, 8 * h + j + 1)
                    a = (slice(None), j // KH, j % KH)
                    nc.vector.tensor_tensor(x_lo[a], xr[:, j % XS, :], x_hi[a].bitcast(F32), ALU.subtract).then_inc(s_xlo, 1)

                def gate_w_view(w, m, twice, group):
                    at = 32 * group + 16 * twice
                    return w[:, KH * m:KH * (m + 1), :].rearrange("p k (b c) -> p k b c", b=2)[:, :, :, at:at + HEADS]

                def place(h, m, first):
                    if not first:
                        dve.wait_ge(s_wgh, 3 * (h - 1) + m + 1)
                    for twice in range(2):
                        for group in range(2):
                            nc.vector.tensor_copy(gate_w_view(wgp, m, twice, group),
                                                  wg[:, m, bass.ds(h * KH, KH), 8 * group:8 * group + 8].rearrange("p k (b c) -> p k b c", b=2)).then_inc(s_wgp, 1)

                def gate_w_low(h, m):
                    dve.wait_ge(s_wgh, 3 * h + m + 1)
                    for group in range(2):
                        v = gate_w_view(wgr, m, 1, group)
                        low = nc.vector.tensor_tensor(v, gate_w_view(wgp, m, 1, group), v.bitcast(F32), ALU.subtract)
                    low.then_inc(s_wgl, 1)

                nc.vector.memset(wgp[:, :, :], 0.0).then_inc(s_wgz, 1)
                for j in range(KH):
                    split_x(0, j)
                split_w(0, 0)
                split_w(0, 1)
                split_w(0, 2)
                dve.wait_ge(s_wgz, 1)
                dve.wait_ge(s_wg, 80)
                for m in range(3):
                    place(0, m, True)
                for m in range(3):
                    gate_w_low(0, m)
                for j in range(KH, 2 * KH):
                    split_x(0, j)

                def step(h, first, last):
                    for n in range(UN):
                        if n == 0 and not first:
                            place(h, 2, False)
                        if n in (2, 4) and not last:
                            place(h + 1, n // 2 - 1, False)
                        for c in range(n * EB * G, (n + 1) * EB * G):
                            t, (t0, nn) = c // G, GROUPS[c % G]
                            dve.wait_ge(s_thi, CH * h + c + 1)
                            nc.vector.tensor_tensor(t_lo[:, c % CR, 0:nn], tile[:, t % RT, t0:t0 + nn], t_hi[:, c % CR, 0:nn].bitcast(F32), ALU.subtract).then_inc(s_tlo, 1)
                        if n + RS < UN:
                            split_w(h, n + RS)
                        elif not last:
                            split_w(h + 1, n + RS - UN)
                        if n == 0 and not first:
                            gate_w_low(h, 2)
                        if n in (2, 4) and not last:
                            gate_w_low(h + 1, n // 2 - 1)
                        if not first:
                            for j in U_SPLITS.get(n, ()):
                                split_x(h, j)
                        if not last:
                            for j in UC_SPLITS.get(n, ()):
                                split_x(h + 1, j)
                over(dve, HEADS, step)
                dve.wait_ge(s_g, CH * HEADS)
                t0, nn = GROUPS[1]
                nc.vector.tensor_copy(early["gate_sums"][:, t0:t0 + nn], ps[:, R + 1, 0:nn]).then_inc(s_gr, 1)


def attention_phase(nc, sem, keep, scr, io, early, bg):
    ps, ident = keep["ps"], keep["ident"]
    NG = 2
    JT = BANK // P
    FULL, DIAG = BANK, BANK + P
    PT = 4 * FULL + 4 * FULL + 4 * DIAG
    NV = KH * 3
    VCH = [(0, 4), (4, 4), (8, 2)]
    src = scr["qkvT"].rearrange("m (h k p) t -> m h k p t", p=P, k=KH)
    fac = [scr[n].rearrange("(f p) t -> f p t", p=P) for n in ("ymul", "yadd")]
    y_dst = scr["yT"].rearrange("(f p) t -> f p t", p=P)

    def subs(g):
        out = []
        for t in (NTX, NTX + 1):
            for d in range(2):
                out.append((t, d, len(out) * FULL))
        off = 4 * FULL
        for t in range(NTX):
            if not JT * g <= t < JT * (g + 1):
                out.append((t, 0 if t < JT * g else 1, off))
                off += FULL
        for t in range(JT * g, JT * (g + 1)):
            out.append((t, None, off))
            off += DIAG
        return out

    NS = len(subs(0))
    NC_ = NT
    with ExitStack() as st:
        sb = lambda n, s, d=F32: st.enter_context(nc.sbuf_tensor(f"b_{n}", s, d))
        p_hi = sb("p_hi", [P, PT], F32R)
        with ExitStack() as inner:
            gates, lf, t1, bsum, big = (inner.enter_context(nc.sbuf_tensor(f"g_{n}", [P, TT], F32)) for n in ("gates", "lf", "t1", "bsum", "big"))
        p_lo = sb("p_lo", [P, PT], F32R)
        q_hi, q_lo = sb("q_hi", [P, KH, BANK], F32R), sb("q_lo", [P, KH, BANK], F32R)
        k_hi, k_lo = sb("k_hi", [P, KH, TT], F32R), sb("k_lo", [P, KH, TT], F32R)
        v_hi, v_lo = sb("v_hi", [P, NT, DH], F32R), sb("v_lo", [P, NT, DH], F32R)
        cols, em = sb("a_cols", [P, NT, 2, HEADS]), sb("em_cols", [P, NTX, 2, HEADS])
        ones, a_out, av = early["ones"], early["a_rows"], early["av"]
        mc = sb("mc", [64, 1])
        X, C = slice(0, TX), slice(TX, TT)
        BOTH = slice(0, 64)
        TURNS = ((3, 0, 4), (4, 4, 4), (7, 8, 2))
        qr, kr = sb("qr", [P, KH, BANK]), sb("kr", [P, 2, TT])
        nm = sb("nm", [P, 2, TX])
        e, pr = sb("e", [P, 2, DIAG]), sb("pr", [P, 2, DIAG])
        mask = sb("mask", [P, 2, P])
        one = sb("one", [P, 1])
        hc = sb("hc", [P, NT, 2])
        acc = sb("acc", [P, 2, BANK])
        rn, st6, mv, rstd, tmp4 = sb("rn", [P, 2, JT]), sb("st6", [P, JT, 6]), sb("mv", [P, JT, 2]), sb("rstd", [P, JT]), sb("tmp4", [P, JT])
        hs = sb("hs", [P, JT, DH])
        fc = sb("fc", [P, 2, 2, BANK])
        names = ("q_loaded", "nm_loaded", "q_hi_made", "q_lo_made", "k_hi_made", "k_lo_made", "v_hi_made", "v_lo_made",
                 "v_turned", "s_done", "arg_made", "e_made", "p_made", "p_hi_made", "p_lo_made", "p_summed", "acc_cleared",
                 "den_done", "norm_step", "pv_done", "pvf_read", "pvb_read", "stat_step", "ln_step", "hn_made", "hn_turned", "y_step", "const")
        (s_q, s_nm, s_qhi, s_qlo, s_khi, s_klo, s_vhi, s_vlo, s_vt, s_s, s_arg, s_e, s_p, s_phi, s_plo, s_acc, s_az,
         s_den, s_nrm, s_pv, s_pvf, s_pvb, s_st, s_ln, s_hn, s_ht, s_y, s_c) = (sem("b_" + n) for n in names)
        s_kr, s_fc, s_yst = ([sem(f"b_{n}{i}") for i in range(2)] for n in ("kr_loaded", "fac_loaded", "y_stored"))
        s_gf, s_gt, s_gv, s_ga, s_gx, s_gtr, s_gcp, s_gout = (sem(f"g_{n}") for n in (
            "folded", "gates_made", "vector_step", "log_step", "rows_made", "turned", "copied", "stored"))
        s_hc, s_hs2, s_hs3 = sem("b_head_cols"), sem("b_head_stats"), sem("b_head_mean")

        def chunk_of(i):
            return (i // 2, i % 2 == 1) if i < 4 else (i - 2, True)

        def pieces_to(c):
            return 2 * c + 2 if c < 2 else c + 3

        VAT = {1: [0, 1], 2: [2], 3: [3, 4], 4: [5], 5: [6, 7], 6: [8, 9], 7: [10, 11]}
        SB, HB, VB, PB = 3, 3, 5, 4
        VR = 3
        TAT = (2, 4, 5, 7)

        def gi(h, g):
            return NG * h + g

        def load_kv(eng, h, j):
            eng.dma_start(kr[:, j % 2], src[1 + j // KH][bass.ds(h, 1), j % KH].rearrange("a p t -> p (a t)")).then_inc(s_kr[j % 2], 16)

        with nc.Block() as block:
            @block.sync
            def _(sp):
                def load_q(h, g):
                    for k in range(KH):
                        sp.dma_start(qr[:, k], src[0][bass.ds(h, 1), k, :, g * BANK:(g + 1) * BANK].rearrange("a p t -> p (a t)")).then_inc(s_q, 16)

                def load_nm(h):
                    for d in range(2):
                        sp.dma_start(nm[:, d, :], scr["nmrow"][d][bass.ds(h, 1), :].to_broadcast([P, TX])).then_inc(s_nm, 16)

                def factors(h, g):
                    for k in range(KH + 1):
                        if k < KH:
                            if k > 1 or not isinstance(h, int) or h or g:
                                sp.wait_ge(s_yst[k % 2], 16 * (2 * gi(h, g) + k // 2))
                            for i in range(2):
                                sp.dma_start(fc[:, k % 2, i, :], fac[i][bass.ds(h * KH + k, 1), :, g * BANK:(g + 1) * BANK].rearrange("a p t -> p (a t)")).then_inc(s_fc[k % 2], 16)
                        if k:
                            sp.wait_ge(s_y, 2 * (KH * gi(h, g) + k))
                            sp.dma_start(y_dst[bass.ds(h * KH + k - 1, 1), :, g * BANK:(g + 1) * BANK].rearrange("a p t -> p (a t)"), fc[:, (k - 1) % 2, 0, :]).then_inc(s_yst[(k - 1) % 2], 16)

                load_q(0, 0)
                load_kv(sp, 0, 0)
                load_kv(sp, 0, 1)
                for j in (2, 3):
                    sp.wait_ge(s_klo, j - 1)
                    load_kv(sp, 0, j)
                sp.wait_ge(s_gv, 14)
                for d in range(2):
                    sp.dma_start(scr["nmrow"][d], lf[32 * d:32 * d + HEADS, X]).then_inc(s_gout, 16)
                sp.wait_ge(s_gout, 32)
                load_nm(0)

                def step(h, first, last):
                    for j in (KH, KH + 1):
                        sp.wait_ge(s_klo, KH * h + j - 1)
                        load_kv(sp, h, j)
                    sp.wait_ge(s_qlo, NG * h + 1)
                    load_q(h, 1)
                    if not first:
                        factors(h - 1, 1)
                    if not last:
                        sp.wait_ge(s_qlo, NG * h + 2)
                        load_q(h + 1, 0)
                    factors(h, 0)
                    if not last:
                        sp.wait_ge(s_e, NG * (h + 1) * NS)
                        load_nm(h + 1)
                        sp.wait_ge(s_vt, NV * (h + 1))
                        for j in range(KH):
                            if j > 1:
                                sp.wait_ge(s_klo, KH * (h + 1) + j - 1)
                            load_kv(sp, h + 1, j)
                over(sp, HEADS, step)
                factors(HEADS - 1, 1)
                for i in range(2):
                    sp.wait_ge(s_yst[i], 16 * (KH // 2) * NG * HEADS)

            def each_group(run):
                def step(h, first, last):
                    for g in range(NG):
                        run(h, g, first and g == 0, last and g == NG - 1, first, last)
                return step

            @block.tensor
            def _(pe):
                def turn_hn(h, g, k):
                    pe.wait_ge(s_hn, JT * (gi(h, g) + 1))
                    n = KH * gi(h, g) + k
                    if k > 1 or not isinstance(h, int) or h or g:
                        pe.wait_ge(s_y, 2 * n - 3)
                    for j in range(JT):
                        tr = nc.tensor.transpose(ps[:, HB + k % 2, j * P:(j + 1) * P], hs[:, j, k * P:(k + 1) * P], ident[:, :])
                    tr.then_inc(s_ht, 1)

                def run(h, g, first, last, first_head, last_head):
                    n = gi(h, g)
                    pieces = subs(g)
                    order = [pieces[0][0], pieces[2][0]] + [x[0] for x in pieces[4:]]
                    pe.wait_ge(s_qlo, n + 1)
                    if g == 0:
                        pe.wait_ge(s_klo, KH * (h + 1))
                    for c, t in enumerate(order):
                        if c >= SB:
                            pe.wait_ge(s_p, NS * n + pieces_to(c - SB))
                        elif not first:
                            pe.wait_ge(s_p, NS * n)
                        for k in range(KH):
                            mm = mm3(nc, ps[:, c % SB, :], k_hi[:, k, t * P:(t + 1) * P], k_lo[:, k, t * P:(t + 1) * P], q_hi[:, k, :], q_lo[:, k, :], k == 0, k == KH - 1)
                        mm.then_inc(s_s, 1)
                        if c in TAT and not first:
                            turn_hn(h if g else h - 1, 1 - g, TAT.index(c))
                        if g == 0:
                            for v in VAT.get(c, ()):
                                k, (t0, nt) = v // 3, VCH[v % 3]
                                if v % 3 == 0:
                                    kr_uses = 4 * h + (KH + k) // 2 + 1
                                    pe.wait_ge(s_kr[k % 2], 16 * kr_uses)
                                if v >= VR:
                                    pe.wait_ge(s_vlo, NV * h + v - VR + 1)
                                elif v == 2 and first_head:
                                    pe.wait_ge(s_gcp, len(TURNS))
                                elif v == 0 and not first_head:
                                    pe.wait_ge(s_pvf, JT * n)
                                    pe.wait_ge(s_pvb, JT * n)
                                for i in range(nt):
                                    tr = nc.tensor.transpose(ps[:, VB + v % VR, i * P:(i + 1) * P], kr[:, k % 2, (t0 + i) * P:(t0 + i + 1) * P], ident[:, :])
                                tr.then_inc(s_vt, 1)
                    where = {(t, d): off for t, d, off in pieces}
                    for j in range(JT):
                        J = JT * g + j
                        for d in range(2):
                            keys = [(t, where[(t, d)] + j * P) for t in (NTX, NTX + 1)]
                            for t, dd, off in pieces[4:]:
                                if dd is None:
                                    if t == J:
                                        keys.append((t, off + (j * P if d == 0 else BANK)))
                                    elif (t < J) == (d == 0):
                                        keys.append((t, off + j * P))
                                elif dd == d:
                                    keys.append((t, off + j * P))
                            b = PB + 2 * (j % 2) + d
                            if not (first and j < 2):
                                pe.wait_ge(s_pvf if d == 0 else s_pvb, JT * n + j - 1)
                            if j == 0 and d == 0 and not first:
                                pe.wait_ge(s_y, 2 * KH * n - 1)
                            for i, (t, off) in enumerate(keys):
                                if j == 0:
                                    piece = [x[0] for x in pieces].index(t) + (d if t >= NTX else 0)
                                    pe.wait_ge(s_plo, NS * n + piece + 1)
                                    if d == 0 and i == 0 and g == 0:
                                        pe.wait_ge(s_vlo, NV * (h + 1))
                                mm = mm3(nc, ps[:, b, :], p_hi[:, off:off + P], p_lo[:, off:off + P], v_hi[:, t, :], v_lo[:, t, :], i == 0, i == len(keys) - 1)
                            mm.then_inc(s_pv, 1)
                        if j == 0:
                            pe.wait_ge(s_acc, NS * (n + 1))
                            for d in range(2):
                                for jj in range(JT):
                                    mm = nc.tensor.matmul(ps[:, HB, d * JT + jj:d * JT + jj + 1], acc[:, d, jj * P:(jj + 1) * P], one[:, :],
                                                          start=(d == 0 and jj == 0), stop=(d == 1 and jj == JT - 1), skip_group_check=True)
                            mm.then_inc(s_den, 1)

                for g, (t0, nn) in enumerate(GROUPS):
                    nc.tensor.matmul(ps[:, 5 + g, 0:nn], early["fold"][:, :], early["gate_sums"][:, t0:t0 + nn], start=True, stop=True).then_inc(s_gf, 1)
                pe.wait_ge(s_gx, 5)
                pe.wait_ge(s_gt, 12)
                for bank, first_tile, nt in TURNS:
                    for i in range(nt):
                        t = first_tile + i
                        tr = nc.tensor.transpose(ps[:, bank, i * P:(i + 1) * P], a_out[:, t * P:(t + 1) * P], ident[:, :])
                    tr.then_inc(s_gtr, 1)
                pe.wait_ge(s_c, 4)
                over(pe, HEADS, each_group(run), last_differs=False)
                for k in range(KH):
                    turn_hn(HEADS - 1, 1, k)

            @block.scalar
            def _(act):
                def split_q(n):
                    act.wait_ge(s_q, 16 * KH * (n + 1))
                    nc.scalar.activation(q_hi[:, :, :], qr[:, :, :], ACT.Copy).then_inc(s_qhi, 1)

                def split_k(h, k):
                    act.wait_ge(s_kr[k % 2], 16 * (4 * h + k // 2 + 1))
                    nc.scalar.activation(k_hi[:, k, :], kr[:, k % 2, :], ACT.Copy).then_inc(s_khi, 1)

                for g, (t0, nn) in enumerate(GROUPS):
                    act.wait_ge(s_gf, g + 1)
                    for kind in (0, 2):
                        r = slice(32 * kind, 32 * (kind + 1))
                        nc.scalar.activation(gates[r, t0:t0 + nn], ps[r, 5 + g, 0:nn], ACT.Identity, bias=bg[r, :]).then_inc(s_gt, 1)
                act.wait_ge(s_gv, 1)
                nc.scalar.activation(t1[BOTH, :], t1[BOTH, :], ACT.Exp, scale=-1.0).then_inc(s_ga, 1)
                act.wait_ge(s_ga, 1)
                nc.scalar.activation(t1[BOTH, :], t1[BOTH, :], ACT.Ln, bias=1.0).then_inc(s_ga, 1)
                split_q(0)
                for k in range(2):
                    split_k(0, k)
                act.wait_ge(s_gv, 7)
                nc.scalar.activation(a_out[0:32, :], av[0:32, :], ACT.Copy).then_inc(s_gx, 1)
                for s in (X, C):
                    nc.scalar.activation(a_out[32:64, s][:, ::-1], av[32:64, s], ACT.Copy).then_inc(s_gx, 1)
                act.wait_ge(s_gv, 11)
                nc.scalar.activation(a_out[64:96, X], t1[0:32, X], ACT.Exp, scale=-1.0).then_inc(s_gx, 1)
                nc.scalar.activation(a_out[96:128, X][:, ::-1], t1[32:64, X], ACT.Exp, scale=-1.0).then_inc(s_gx, 1)
                for k in (2, 3):
                    split_k(0, k)
                for i, (bank, first_tile, nt) in enumerate(TURNS):
                    act.wait_ge(s_gtr, i + 1)
                    turned = ps[:, bank, 0:nt * P].rearrange("p (t c) -> p t c", c=P)
                    for d in range(2):
                        if first_tile < NTX:
                            nc.scalar.activation(em[:, first_tile:first_tile + nt, d, :], turned[:, :, 64 + 32 * d:64 + 32 * d + HEADS], ACT.Copy)
                        cp = nc.scalar.activation(cols[:, first_tile:first_tile + nt, d, :], turned[:, :, 32 * d:32 * d + HEADS], ACT.Copy)
                    cp.then_inc(s_gcp, 1)

                def weights(h, g, i, first):
                    n = gi(h, g)
                    t, d, off = subs(g)[i]
                    if i == 0:
                        act.wait_ge(s_nm, 32 * (h + 1))
                        act.wait_ge(s_hc, h + 1)
                    if not (first and i < 2):
                        act.wait_ge(s_p, NS * n + i - 1)
                    a = lambda dd: hc[:, t, dd:dd + 1]
                    q0 = g * BANK
                    if d is not None:
                        nc.scalar.activation(e[:, i % 2, 0:BANK], nm[:, d, q0:q0 + BANK], ACT.Exp, bias=a(d)).then_inc(s_e, 1)
                        return
                    j = t - JT * g
                    if j > 0:
                        nc.scalar.activation(e[:, i % 2, 0:j * P], nm[:, 1, q0:q0 + j * P], ACT.Exp, bias=a(1))
                    if j < JT - 1:
                        nc.scalar.activation(e[:, i % 2, (j + 1) * P:BANK], nm[:, 0, q0 + (j + 1) * P:q0 + BANK], ACT.Exp, bias=a(0))
                    act.wait_ge(s_arg, 2 * (JT * n + j + 1))
                    nc.scalar.activation(e[:, i % 2, j * P:(j + 1) * P], e[:, i % 2, j * P:(j + 1) * P], ACT.Exp)
                    nc.scalar.activation(e[:, i % 2, BANK:DIAG], e[:, i % 2, BANK:DIAG], ACT.Exp).then_inc(s_e, 1)

                weights(0, 0, 0, True)

                def run(h, g, first, last, first_head, last_head):
                    n = gi(h, g)
                    pieces = subs(g)
                    for i in range(NS):
                        if i + 1 < NS:
                            weights(h, g, i + 1, first)
                        t, d, off = pieces[i]
                        w = FULL if d is not None else DIAG
                        act.wait_ge(s_p, NS * n + i + 1)
                        if not first and i == 0:
                            act.wait_ge(s_pv, 2 * JT * n)
                        nc.scalar.activation(p_hi[:, off:off + w], pr[:, i % 2, 0:w], ACT.Copy).then_inc(s_phi, 1)
                        c, end = chunk_of(i)
                        if g == 0 and end:
                            for v in VAT.get(c, ()):
                                k, (t0, nt) = v // 3, VCH[v % 3]
                                act.wait_ge(s_vt, NV * h + v + 1)
                                if v == 0 and not first_head:
                                    act.wait_ge(s_pv, 2 * JT * n)
                                nc.scalar.activation(v_hi[:, t0:t0 + nt, k * P:(k + 1) * P], ps[:, VB + v % VR, 0:nt * P].rearrange("p (t e) -> p t e", e=P), ACT.Copy).then_inc(s_vhi, 1)
                                if v in (2, 5):
                                    load_kv(act, h, KH + 2 + v // 3)
                    for j in range(JT):
                        if j == 0:
                            if not last:
                                act.wait_ge(s_s, NC_ * (n + 1))
                                split_q(n + 1)
                            act.wait_ge(s_nrm, 3 * (n + 1))
                        if g == 1 and not last_head:
                            split_k(h + 1, j)
                        act.wait_ge(s_pv, 2 * (JT * n + j) + 1)
                        if not first:
                            act.wait_ge(s_ht, KH * n)
                        nc.scalar.activation(hs[:, j, :], ps[:, PB + 2 * (j % 2), :], ACT.Copy, scale=rn[:, 0, j:j + 1]).then_inc(s_pvf, 1)
                    if not last:
                        weights(h + g, 1 - g, 0, False)
                    act.wait_ge(s_ln, 5 * n + 1)
                    nc.scalar.activation(rstd[:, :], tmp4[:, :], ACT.Ln).then_inc(s_st, 1)
                    act.wait_ge(s_st, 2 * n + 1)
                    nc.scalar.activation(rstd[:, :], rstd[:, :], ACT.Exp, scale=-0.5).then_inc(s_st, 1)

                over(act, HEADS, each_group(run))

            @block.gpsimd
            def _(pool):
                nc.gpsimd.memset(one[:, :], 1.0).then_inc(s_c, 1)
                nc.gpsimd.memset(mask[:, :, :], 0.0).then_inc(s_c, 1)
                pool.wait_ge(s_c, 2)
                nc.gpsimd.affine_select(out=mask[:, 0, :], in_=mask[:, 0, :], compare_op=ALU.is_ge, fill=-1e30, base=0,
                                        pattern=[[1, P]], channel_multiplier=-1).then_inc(s_c, 1)
                nc.gpsimd.affine_select(out=mask[:, 1, :], in_=mask[:, 1, :], compare_op=ALU.is_ge, fill=-1e30, base=0,
                                        pattern=[[-1, P]], channel_multiplier=1).then_inc(s_c, 1)

                def run(h, g, first, last, first_head, last_head):
                    n = gi(h, g)
                    pool.wait_ge(s_az, n + 1)
                    for i, (t, d, off) in enumerate(subs(g)):
                        pool.wait_ge(s_p, NS * n + i + 1)
                        if i:
                            pool.wait_ge(s_acc, NS * n + i)
                        def add(dd, a, b, x):
                            return nc.gpsimd.tensor_tensor(acc[:, dd, a:b], acc[:, dd, a:b], pr[:, i % 2, x:x + b - a], ALU.add)
                        if d is not None:
                            add(d, 0, BANK, 0).then_inc(s_acc, 1)
                            continue
                        j = t - JT * g
                        if j > 0:
                            add(1, 0, j * P, 0)
                        add(0, j * P, BANK, j * P)
                        add(1, j * P, (j + 1) * P, BANK).then_inc(s_acc, 1)
                over(pool, HEADS, each_group(run), last_differs=False)

            @block.vector
            def _(dve):
                def split_q(n):
                    dve.wait_ge(s_qhi, n + 1)
                    nc.vector.tensor_tensor(q_lo[:, :, :], qr[:, :, :], q_hi[:, :, :].bitcast(F32), ALU.subtract).then_inc(s_qlo, 1)

                def split_k(h, k):
                    dve.wait_ge(s_khi, KH * h + k + 1)
                    nc.vector.tensor_tensor(k_lo[:, k, :], kr[:, k % 2, :], k_hi[:, k, :].bitcast(F32), ALU.subtract).then_inc(s_klo, 1)

                def head_cols(h):
                    nc.vector.tensor_copy(hc[:, :, :], cols[:, :, :, bass.ds(h, 1)].rearrange("p t d o -> p t (d o)")).then_inc(s_hc, 1)

                for g, (t0, nn) in enumerate(GROUPS):
                    dve.wait_ge(s_gf, g + 1)
                    to = slice(TX - t0 - nn, TX - t0) if g < 2 else C
                    for kind in (1, 3):
                        r = slice(32 * kind, 32 * (kind + 1))
                        nc.vector.tensor_scalar(gates[r, to][:, ::-1], ps[r, 5 + g, 0:nn], bg[r, :], None, ALU.add).then_inc(s_gt, 1)
                dve.wait_ge(s_gt, 12)
                f = gates[64:128, :]
                nc.vector.scalar_tensor_tensor(t1[BOTH, :], f, -1.0, f, ALU.mult, ALU.max).then_inc(s_gv, 1)
                nc.vector.tensor_scalar(bsum[BOTH, :], f, 0.0, None, ALU.min).then_inc(s_gv, 1)
                nc.vector.memset(acc[:, :, :], 0.0).then_inc(s_az, 1)
                dve.wait_ge(s_gv, 2)
                dve.wait_ge(s_ga, 2)
                nc.vector.tensor_tensor(lf[BOTH, :], bsum[BOTH, :], t1[BOTH, :], ALU.subtract).then_inc(s_gv, 1)
                dve.wait_ge(s_gv, 3)
                for s in (X, C):
                    nc.vector.tensor_tensor_scan(bsum[BOTH, s], ones[BOTH, s], lf[BOTH, s], 0.0, ALU.mult, ALU.add).then_inc(s_gv, 1)
                dve.wait_ge(s_gv, 5)
                nc.vector.tensor_tensor(av[BOTH, :], gates[BOTH, :], bsum[BOTH, :], ALU.subtract).then_inc(s_gv, 1)
                dve.wait_ge(s_gv, 6)
                total = bsum[BOTH, TT - 1:TT]
                nc.vector.tensor_scalar(av[BOTH, C], av[BOTH, C], total, None, ALU.add).then_inc(s_gv, 1)
                split_q(0)
                for k in range(2):
                    split_k(0, k)
                dve.wait_ge(s_gv, 7)
                nc.vector.reduce_max(mc[:, :], av[BOTH, C], mybir.AxisListType.X).then_inc(s_gv, 1)
                dve.wait_ge(s_gv, 8)
                nc.vector.tensor_tensor(mc[:, :], mc[:, :], total, ALU.max).then_inc(s_gv, 1)
                dve.wait_ge(s_gv, 9)
                nc.vector.tensor_tensor_scan(big[BOTH, X], ones[BOTH, X], av[BOTH, X], mc[:, :], ALU.mult, ALU.max).then_inc(s_gv, 1)
                dve.wait_ge(s_gv, 10)
                nc.vector.tensor_tensor(t1[BOTH, X], big[BOTH, X], bsum[BOTH, X], ALU.add).then_inc(s_gv, 1)
                nc.vector.tensor_scalar(lf[0:32, X], big[0:32, X], -1.0, None, ALU.mult).then_inc(s_gv, 1)
                nc.vector.tensor_scalar(lf[32:64, X][:, ::-1], big[32:64, X], -1.0, None, ALU.mult).then_inc(s_gv, 2)
                for k in (2, 3):
                    split_k(0, k)
                dve.wait_ge(s_c, 4)
                dve.wait_ge(s_gcp, len(TURNS))
                head_cols(0)

                def finish(h, g, k):
                    n = KH * gi(h, g) + k
                    dve.wait_ge(s_ht, n + 1)
                    dve.wait_ge(s_fc[k % 2], 32 * (2 * gi(h, g) + k // 2 + 1))
                    yt = fc[:, k % 2, 0, :]
                    nc.vector.tensor_tensor(yt, ps[:, HB + k % 2, :], yt, ALU.mult).then_inc(s_y, 1)
                    dve.wait_ge(s_y, 2 * n + 1)
                    nc.vector.tensor_tensor(yt, yt, fc[:, k % 2, 1, :], ALU.add).then_inc(s_y, 1)

                def run(h, g, first, last, first_head, last_head):
                    n = gi(h, g)
                    pieces = subs(g)

                    def args(i):
                        t, d, off = pieces[i]
                        if d is not None:
                            return
                        j = t - JT * g
                        if i == NS - JT:
                            dve.wait_ge(s_nm, 32 * (h + 1))
                        dve.wait_ge(s_p, NS * n + i - 1)
                        for dd, c0 in ((0, j * P), (1, BANK)):
                            nc.vector.scalar_tensor_tensor(e[:, i % 2, c0:c0 + P], nm[:, dd, t * P:(t + 1) * P], hc[:, t, dd:dd + 1],
                                                           mask[:, dd, :], ALU.add, ALU.add).then_inc(s_arg, 1)

                    def low(i):
                        t, d, off = pieces[i]
                        w = FULL if d is not None else DIAG
                        dve.wait_ge(s_phi, NS * n + i + 1)
                        nc.vector.tensor_tensor(p_lo[:, off:off + w], pr[:, i % 2, 0:w], p_hi[:, off:off + w].bitcast(F32), ALU.subtract).then_inc(s_plo, 1)

                    def low_v(c):
                        if g == 0:
                            for v in VAT.get(c, ()):
                                k, (t0, nt) = v // 3, VCH[v % 3]
                                dve.wait_ge(s_vhi, NV * h + v + 1)
                                o = (slice(None), slice(t0, t0 + nt), slice(k * P, (k + 1) * P))
                                nc.vector.tensor_tensor(v_lo[o], ps[:, VB + v % VR, 0:nt * P].rearrange("p (t e) -> p t e", e=P), v_hi[o].bitcast(F32), ALU.subtract).then_inc(s_vlo, 1)

                    for i in range(NS):
                        c, end = chunk_of(i)
                        if i + 1 < NS:
                            args(i + 1)
                        dve.wait_ge(s_e, NS * n + i + 1)
                        dve.wait_ge(s_s, NC_ * n + c + 1)
                        if not (first and i < 2):
                            dve.wait_ge(s_acc, NS * n + i - 1)
                            dve.wait_ge(s_plo, NS * n + i - 1)
                        t, d, off = pieces[i]
                        p = nc.vector.tensor_tensor(pr[:, i % 2, 0:BANK], ps[:, c % SB, :], e[:, i % 2, 0:BANK], ALU.mult)
                        if d is None:
                            j = t - JT * g
                            p = nc.vector.tensor_tensor(pr[:, i % 2, BANK:DIAG], ps[:, c % SB, j * P:(j + 1) * P], e[:, i % 2, BANK:DIAG], ALU.mult)
                        p.then_inc(s_p, 1)
                        if i:
                            low(i - 1)
                            cc, ee = chunk_of(i - 1)
                            if cc in TAT and ee and not first:
                                pg = (h if g else h - 1, 1 - g)
                                finish(*pg, TAT.index(cc))
                        if end:
                            low_v(c)
                    low(NS - 1)
                    dve.wait_ge(s_den, n + 1)
                    den = ps[:, HB, 0:2 * JT].rearrange("p (d j) -> p d j", d=2)
                    em_g = em[:, JT * g:JT * (g + 1), :, bass.ds(h, 1)].rearrange("p j d o -> p d (j o)")
                    nc.vector.scalar_tensor_tensor(rn[:, :, :], den, -1.0, em_g, ALU.mult, ALU.max).then_inc(s_nrm, 1)
                    dve.wait_ge(s_nrm, 3 * n + 1)
                    nc.vector.tensor_tensor(rn[:, :, :], den, rn[:, :, :], ALU.max).then_inc(s_nrm, 1)
                    dve.wait_ge(s_nrm, 3 * n + 2)
                    nc.vector.reciprocal(rn[:, :, :], rn[:, :, :]).then_inc(s_nrm, 1)
                    if not last:
                        nc.vector.memset(acc[:, :, :], 0.0).then_inc(s_az, 1)
                        split_q(n + 1)
                    if g == 1 and not last_head:
                        head_cols(h + 1)
                    for j in range(JT):
                        if g == 1 and not last_head:
                            split_k(h + 1, j)
                        m = JT * n + j
                        dve.wait_ge(s_pvf, m + 1)
                        dve.wait_ge(s_pv, 2 * (m + 1))
                        dve.wait_ge(s_nrm, 3 * (n + 1))
                        nc.vector.scalar_tensor_tensor(hs[:, j, :], ps[:, PB + 1 + 2 * (j % 2), :], rn[:, 1, j:j + 1], hs[:, j, :], ALU.mult, ALU.add).then_inc(s_pvb, 1)
                        dve.wait_ge(s_pvb, m + 1)
                        nc.vector.bn_stats(st6[:, j, :], hs[:, j, :]).then_inc(s_hs2, 1)
                    dve.wait_ge(s_hs2, JT * (n + 1))
                    nc.vector.memset(tmp4[:, :], EPS).then_inc(s_hs3, 1)
                    for j in range(JT):
                        nc.vector.bn_aggr(mv[:, j, :], st6[:, j, :]).then_inc(s_hs3, 1)
                    dve.wait_ge(s_hs3, (JT + 1) * (n + 1))
                    nc.vector.tensor_tensor(tmp4[:, :], tmp4[:, :], mv[:, :, 1], ALU.add).then_inc(s_ln, 1)
                    dve.wait_ge(s_st, 2 * (n + 1))
                    dve.wait_ge(s_ln, 5 * n + 1)
                    nc.vector.tensor_tensor(tmp4[:, :], tmp4[:, :], rstd[:, :], ALU.mult).then_inc(s_ln, 1)
                    dve.wait_ge(s_ln, 5 * n + 2)
                    nc.vector.tensor_tensor(tmp4[:, :], tmp4[:, :], rstd[:, :], ALU.mult).then_inc(s_ln, 1)
                    dve.wait_ge(s_ln, 5 * n + 3)
                    nc.vector.tensor_scalar(tmp4[:, :], tmp4[:, :], -0.5, 1.5, ALU.mult, ALU.add).then_inc(s_ln, 1)
                    dve.wait_ge(s_ln, 5 * n + 4)
                    nc.vector.tensor_tensor(rstd[:, :], rstd[:, :], tmp4[:, :], ALU.mult).then_inc(s_ln, 1)
                    dve.wait_ge(s_ln, 5 * n + 5)
                    for j in range(JT):
                        nc.vector.tensor_scalar(hs[:, j, :], hs[:, j, :], mv[:, j, 0:1], rstd[:, j:j + 1], ALU.subtract, ALU.mult).then_inc(s_hn, 1)

                over(dve, HEADS, each_group(run))
                for k in range(KH):
                    finish(HEADS - 1, 1, k)


def out_phase(nc, sem, keep, scr, io, layer):
    ps = keep["ps"]
    last_layer = layer == 1
    n_tiles = NTX if last_layer else NT
    pairs = n_tiles // 2
    WR = 3
    y_src = scr["yT"].rearrange("(k p) t -> p k t", p=P)
    x_in = (io["x"][0], io["ctx"][0]) if not last_layer else (scr["x1"], None)
    dst = io["out"][0] if last_layer else scr["xn1"]
    w_src = io["m_w_out" if last_layer else "conv_w_out"][0].rearrange("(k p) n -> k p n", p=P)
    H = D // BANK
    LAG = 6
    YQ = 4
    with ExitStack() as st:
        sb = lambda n, s, d=F32: st.enter_context(nc.sbuf_tensor(f"c{layer}_{n}", s, d))
        w_hi, w_lo = sb("w_hi", [P, KI, D], F32R), sb("w_lo", [P, KI, D], F32R)
        wr = sb("wr", [P, WR, D])
        yr, y_hi, y_lo = sb("yr", [P, KI, P]), sb("y_hi", [P, 2, KI, P], F32R), sb("y_lo", [P, 2, KI, P], F32R)
        x = sb("x", [P, 2, D])
        bc = sb("bc", [P, 2, D])
        o = sb("o", [P, 1, D])
        ss, ms, rt = sb("ss", [P, 1]), sb("ms", [P, 1]), sb("rt", [P, 1])
        s_w = [sem(f"c{layer}_w_loaded{i}") for i in range(WR)]
        s_x = [sem(f"c{layer}_x_loaded{i}") for i in range(2)]
        s_sx = sem(f"c{layer}_stream_stored")
        s_y0 = [sem(f"c{layer}_first_y_loaded{i}") for i in range(YQ)]
        s_y0hi, s_y0lo = sem(f"c{layer}_first_y_hi_made"), sem(f"c{layer}_first_y_lo_made")
        s_bc, s_y, s_whi, s_wlo, s_yhi, s_ylo, s_mm, s_ep, s_fin, s_sq, s_st, s_fn = (sem(f"c{layer}_{n}") for n in (
            "bc_loaded", "y_loaded", "w_hi_made", "w_lo_made", "y_hi_made", "y_lo_made", "chunk_done", "gated", "tile_made", "squared", "stored", "final_step"))
        with nc.Block() as block:
            @block.sync
            def _(sp):
                def load_y(t):
                    sp.dma_start(yr[:, :, :], y_src[:, :, bass.ds(t * P, P)]).then_inc(s_y, 16)

                def load_x(t, par, ctx):
                    src = x_in[1 if ctx else 0]
                    sp.dma_start(x[:, par, :], src[bass.ds((t - NTX if ctx else t) * P, P), :]).then_inc(s_x[par], 16)

                for i in range(YQ):
                    at = slice(i * KI // YQ, (i + 1) * KI // YQ)
                    sp.dma_start(yr[:, at, :], y_src[:, at, 0:P]).then_inc(s_y0[i], 16)
                    if i < WR:
                        sp.dma_start(wr[:, i, :], w_src[i]).then_inc(s_w[i], 16)
                for k in range(WR, KI):
                    sp.wait_ge(s_wlo, k - WR + 1)
                    sp.dma_start(wr[:, k % WR, :], w_src[k]).then_inc(s_w[k % WR], 16)
                    if k == WR + 2:
                        sp.wait_ge(s_y0lo, YQ)
                        load_y(1)
                sp.dma_start(bc[:, 0, :], scr["gates"][layer][0:1, :].to_broadcast([P, D])).then_inc(s_bc, 16)
                second = io["final_g"].rearrange("(o d) -> o d", o=1) if last_layer else scr["gates"][layer][1:2, :]
                sp.dma_start(bc[:, 1, :], second.to_broadcast([P, D])).then_inc(s_bc, 16)
                load_x(0, 0, False)
                load_x(1, 1, False)

                def pair(i, more, ctx_next):
                    for par in range(2):
                        t = 2 * i + par
                        if more:
                            sp.wait_ge(s_ylo, t + 1)
                            load_y(t + 2)
                        if not last_layer:
                            sp.wait_ge(s_fn, 5 * t + 1)
                            sp.dma_start(scr["x1"][bass.ds(t * P, P), :], x[:, par, :]).then_inc(s_sx, 16)
                        sp.wait_ge(s_fin, t + 1)
                        sp.dma_start(dst[bass.ds(t * P, P), :], o[:, 0, :]).then_inc(s_st, 16)
                        if more:
                            if not last_layer:
                                sp.wait_ge(s_sx, 16 * (t + 1))
                            load_x(t + 2, par, ctx_next)
                loop = pairs - 1 if last_layer else pairs - 2
                with sp.Fori(0, loop) as i:
                    pair(i, True, False)
                if not last_layer:
                    pair(pairs - 2, True, True)
                pair(pairs - 1, False, False)
                sp.wait_ge(s_st, 16 * n_tiles)
                if not last_layer:
                    sp.wait_ge(s_sx, 16 * n_tiles)

            @block.tensor
            def _(pe):
                def product(par, half, k):
                    cols = slice(half * BANK, (half + 1) * BANK)
                    mm = mm3(nc, ps[:, 2 * par + half, :], y_hi[:, par, k], y_lo[:, par, k], w_hi[:, k, cols], w_lo[:, k, cols], k == 0, k == KI - 1)
                    if k == KI - 1:
                        mm.then_inc(s_mm, 1)

                for at in range(KI + LAG):
                    for par in range(2):
                        k = at - LAG * par
                        if 0 <= k < KI:
                            if par == 0 and k % (KI // YQ) == 0:
                                pe.wait_ge(s_y0lo, k // (KI // YQ) + 1)
                            if par == 1 and k == 0:
                                pe.wait_ge(s_ylo, 1)
                            if par == 0:
                                pe.wait_ge(s_wlo, k + 1)
                            for half in range(H):
                                product(par, half, k)
                with pe.Fori(1, pairs) as i:
                    for par in range(2):
                        t = 2 * i + par
                        pe.wait_ge(s_ylo, t)
                        for half in range(H):
                            pe.wait_ge(s_ep, H * (t - 2) + half + 1)
                            for k in range(KI):
                                product(par, half, k)

            @block.scalar
            def _(act):
                def round_w(k):
                    act.wait_ge(s_w[k % WR], 16 * (k // WR + 1))
                    nc.scalar.activation(w_hi[:, k, :], wr[:, k % WR, :], ACT.Copy).then_inc(s_whi, 1)

                def split(t, par):
                    act.wait_ge(s_y, 16 * t)
                    nc.scalar.activation(y_hi[:, par], yr[:, :, :], ACT.Copy).then_inc(s_yhi, 1)

                for i in range(YQ):
                    at = slice(i * KI // YQ, (i + 1) * KI // YQ)
                    act.wait_ge(s_y0[i], 16)
                    nc.scalar.activation(y_hi[:, 0, at], yr[:, at, :], ACT.Copy).then_inc(s_y0hi, 1)
                    if i < WR:
                        round_w(i)
                for k in range(WR, KI):
                    round_w(k)
                    if k == LAG - 1:
                        split(1, 1)
                def pair(i, more):
                    for par in range(2):
                        t = 2 * i + par
                        if more:
                            act.wait_ge(s_mm, H * (t + 1))
                            split(t + 2, par)
                        act.wait_ge(s_fn, 5 * t + 1)
                        nc.scalar.activation(o[:, 0, :], x[:, par, :], ACT.Square, accum_out=ss[:, :]).then_inc(s_sq, 1)
                        act.wait_ge(s_fn, 5 * t + 2)
                        nc.scalar.activation(rt[:, :], ms[:, :], ACT.Sqrt).then_inc(s_sq, 1)
                with act.Fori(0, pairs - 1) as i:
                    pair(i, True)
                pair(pairs - 1, False)

            @block.vector
            def _(dve):
                def split(t, par):
                    dve.wait_ge(s_yhi, t)
                    nc.vector.tensor_tensor(y_lo[:, par], yr[:, :, :], y_hi[:, par].bitcast(F32), ALU.subtract).then_inc(s_ylo, 1)

                def low_w(k):
                    dve.wait_ge(s_whi, k + 1)
                    nc.vector.tensor_tensor(w_lo[:, k, :], wr[:, k % WR, :], w_hi[:, k, :].bitcast(F32), ALU.subtract).then_inc(s_wlo, 1)

                for i in range(YQ):
                    at = slice(i * KI // YQ, (i + 1) * KI // YQ)
                    dve.wait_ge(s_y0hi, i + 1)
                    nc.vector.tensor_tensor(y_lo[:, 0, at], yr[:, at, :], y_hi[:, 0, at].bitcast(F32), ALU.subtract).then_inc(s_y0lo, 1)
                    if i < WR:
                        low_w(i)
                for k in range(WR, KI):
                    low_w(k)
                    if k == LAG - 1:
                        split(1, 1)
                dve.wait_ge(s_bc, 32)

                def pair(i, first, more, ctx):
                    for par in range(2):
                        t = 2 * i + par
                        dve.wait_ge(s_x[par], 16 * (i + 1))
                        if not (first and par == 0):
                            dve.wait_ge(s_st, 16 * t)
                        for half in range(H):
                            cols = slice(half * BANK, (half + 1) * BANK)
                            dve.wait_ge(s_mm, H * t + half + 1)
                            nc.vector.tensor_tensor(o[:, 0, cols], ps[:, 2 * par + half, :], bc[:, 1 if ctx else 0, cols], ALU.mult).then_inc(s_ep, 1)
                        if more:
                            split(t + 2, par)
                        dve.wait_ge(s_ep, H * (t + 1))
                        nc.vector.tensor_tensor(x[:, par, :], o[:, 0, :], x[:, par, :], ALU.add).then_inc(s_fn, 1)
                        dve.wait_ge(s_sq, 2 * t + 1)
                        nc.vector.tensor_scalar(ms[:, :], ss[:, :], 1.0 / D, EPS, ALU.mult, ALU.add).then_inc(s_fn, 1)
                        dve.wait_ge(s_sq, 2 * t + 2)
                        nc.vector.reciprocal(ms[:, :], rt[:, :]).then_inc(s_fn, 2)
                        dve.wait_ge(s_fn, 5 * t + 4)
                        if last_layer:
                            nc.vector.scalar_tensor_tensor(o[:, 0, :], x[:, par, :], ms[:, :], bc[:, 1, :], ALU.mult, ALU.mult).then_inc(s_fin, 1)
                        else:
                            nc.vector.tensor_scalar(o[:, 0, :], x[:, par, :], ms[:, :], None, ALU.mult).then_inc(s_fin, 1)
                        nc.vector.tensor_copy(rt[:, :], ms[:, :]).then_inc(s_fn, 1)
                pair(0, True, True, False)
                with dve.Fori(1, pairs - 1) as i:
                    pair(i, False, True, False)
                pair(pairs - 1, False, False, not last_layer)


INS = ["x", "c", "ctx", "c_ctx", "norm_g", "mod_w", "mod_b", "conv_w_in", "conv_w", "conv_w_out", "m_w_in", "m_conv_w",
       "m_wq", "m_wk", "m_wv", "m_w_gate", "m_b_gate", "m_norm_g", "m_skip", "m_w_out", "final_g"]


def kernel(**inputs):
    import numpy as np
    import concourse.bacc as bacc
    from concourse.bass_utils import run_bass_kernel_spmd

    nc = bacc.Bacc("TRN2", target_bir_lowering=False, num_devices=1)
    arrays, io = {}, {}
    for name in INS:
        a = np.ascontiguousarray(inputs[name])
        arrays[f"in_{name}"] = a
        io[name] = nc.dram_tensor(f"in_{name}", a.shape, mybir.dt.from_np(a.dtype), kind="ExternalInput").ap()
    io["out"] = nc.dram_tensor("out_0", (1, TX, D), F32, kind="ExternalOutput").ap()
    build(nc, io)
    r = run_bass_kernel_spmd(nc, [arrays], core_ids=[0])
    return r.results[0]["out_0"]
```
